# Optimizing a Trainium2 kernel written in Bass

```python
import math
import jax
import jax.numpy as jnp
from jax import lax
import numpy as np

D_MODEL = 1024
BATCH = 1
SEQ = 256
DEPTH = 2

SSD_HEADS = 16
SSD_HEAD_DIM = 64
SSD_INNER = SSD_HEADS * SSD_HEAD_DIM
SSD_GROUPS = 4
SSD_STATE = 128
SSD_CONV = 4
SSD_CHUNK = 128
SSD_CONV_DIM = SSD_INNER + 2 * SSD_GROUPS * SSD_STATE
SSD_COLS = SSD_INNER + SSD_CONV_DIM + SSD_HEADS

RWKV_HEADS = 16
RWKV_HEAD_DIM = 64
RWKV_DIM = RWKV_HEADS * RWKV_HEAD_DIM
DECAY_LORA = 64
AAA_LORA = 64
GATE_LORA = 128
RWKV_COLS = 3 * RWKV_DIM + DECAY_LORA + AAA_LORA + GATE_LORA
RWKV_GN_EPS = 64e-5

IN_EVEN_COLS = SSD_COLS + RWKV_COLS
MIX_EVEN = SSD_INNER + RWKV_DIM

ATT_HEADS = 16
KV_HEADS = 4
Q_PER_KV = ATT_HEADS // KV_HEADS
HEAD_DIM = 64
Q_DIM = ATT_HEADS * HEAD_DIM
KV_DIM = KV_HEADS * HEAD_DIM
IN_ODD_COLS = Q_DIM + 2 * KV_DIM
WINDOW = 128
ATT_BLOCK = 128

EXPERT_GROUPS = 4
EXPERTS_PER_GROUP = 8
N_EXPERTS = EXPERT_GROUPS * EXPERTS_PER_GROUP
TOP_K = 2
EXPERT_HIDDEN = 512
MOE_BLOCK = 256

NORM_EPS = 1e-6

kernel_name = "hybrid_ssd_rwkv7_swa_sink_hmoe"

F32 = jnp.float32

def rms_norm(x, gain, eps=NORM_EPS):
    xf = x.astype(F32)
    y = xf * lax.rsqrt(jnp.mean(xf * xf, axis=-1, keepdims=True) + eps)
    return (y * gain.astype(F32)).astype(x.dtype)

def causal_depthwise_conv(u, w, bias):
    c = u.shape[-1]
    y = lax.conv_general_dilated(
        u, w[:, None, :].astype(u.dtype), window_strides=(1,),
        padding=[(w.shape[0] - 1, 0)], dimension_numbers=("NWC", "WIO", "NWC"),
        feature_group_count=c)
    return y + bias.astype(u.dtype)

def segsum(a):
    n = a.shape[-1]
    cs = jnp.cumsum(a, axis=-1)
    diff = cs[..., :, None] - cs[..., None, :]
    mask = jnp.tril(jnp.ones((n, n), dtype=bool))
    return jnp.where(mask, diff, -jnp.inf)

def ssd_chunked(xs, adt, bm, cm):
    b, t, h, p = xs.shape
    g, n = bm.shape[2], bm.shape[3]
    k = h // g
    c = t // SSD_CHUNK
    xs = xs.reshape(b, c, SSD_CHUNK, g, k, p)
    bm = bm.reshape(b, c, SSD_CHUNK, g, n)
    cm = cm.reshape(b, c, SSD_CHUNK, g, n)
    adt = adt.reshape(b, c, SSD_CHUNK, g, k).transpose(0, 3, 4, 1, 2)
    a_cum = jnp.cumsum(adt, axis=-1)
    decay_in = jnp.exp(segsum(adt))
    cb = jnp.einsum("bclgn,bcsgn->bcgls", cm, bm)
    y_diag = jnp.einsum("bcgls,bgkcls,bcsgkp->bclgkp", cb, decay_in, xs)
    decay_states = jnp.exp(a_cum[..., -1:] - a_cum)
    states = jnp.einsum("bclgn,bgkcl,bclgkp->bcgkpn", bm, decay_states, xs)
    states = jnp.concatenate([jnp.zeros_like(states[:, :1]), states], axis=1)
    chunk_tot = jnp.pad(a_cum[..., -1], ((0, 0), (0, 0), (0, 0), (1, 0)))
    decay_chunk = jnp.exp(segsum(chunk_tot))
    states = jnp.einsum("bgkzc,bcgkpn->bzgkpn", decay_chunk, states)[:, :-1]
    y_off = jnp.einsum("bclgn,bcgkpn,bgkcl->bclgkp", cm, states, jnp.exp(a_cum))
    return (y_diag + y_off).reshape(b, t, h, p)

def ssd_mixer(z, xbc, dt, conv_w, conv_b, dt_bias, a_log, d_skip, norm_w):
    b, t, _ = xbc.shape
    xbc = jax.nn.silu(causal_depthwise_conv(xbc, conv_w, conv_b)).astype(F32)
    gn = SSD_GROUPS * SSD_STATE
    xs = xbc[..., :SSD_INNER].reshape(b, t, SSD_HEADS, SSD_HEAD_DIM)
    bm = xbc[..., SSD_INNER:SSD_INNER + gn].reshape(b, t, SSD_GROUPS, SSD_STATE)
    cm = xbc[..., SSD_INNER + gn:].reshape(b, t, SSD_GROUPS, SSD_STATE)
    dt = jax.nn.softplus(dt.astype(F32) + dt_bias.astype(F32))
    a = -jnp.exp(a_log.astype(F32))
    y = ssd_chunked(xs * dt[..., None], a * dt, bm, cm) + d_skip.astype(F32)[:, None] * xs
    y = y.reshape(b, t, SSD_INNER) * jax.nn.silu(z.astype(F32))
    yg = y.reshape(b, t, SSD_GROUPS, SSD_INNER // SSD_GROUPS)
    yg = yg * lax.rsqrt(jnp.mean(yg * yg, axis=-1, keepdims=True) + 1e-5)
    y = yg.reshape(b, t, SSD_INNER) * norm_w.astype(F32)
    return y.astype(z.dtype)

def wkv7_scan(r, w, k, v, a, bb):
    bsz, _, h, dk = r.shape

    def step(s, inp):
        r_t, w_t, k_t, v_t, a_t, b_t = inp
        sa = jnp.einsum("bhvk,bhk->bhv", s, a_t)
        s = s * w_t[:, :, None, :] + sa[..., None] * b_t[:, :, None, :] + v_t[..., None] * k_t[:, :, None, :]
        return s, jnp.einsum("bhvk,bhk->bhv", s, r_t)

    s0 = jnp.zeros((bsz, h, dk, dk), F32)
    xs = tuple(jnp.moveaxis(u, 1, 0) for u in (r, w, k, v, a, bb))
    _, ys = lax.scan(step, s0, xs)
    return jnp.moveaxis(ys, 0, 1)

def rwkv7_mixer(u, mu, w0, w2, a0, a2, g2, k_k, k_a, r_k, ln_w, ln_b):
    b, t, _ = u.shape
    prev = jnp.pad(u, ((0, 0), (1, 0), (0, 0)))[:, :-1]
    u = (u + mu.astype(u.dtype) * (prev - u)).astype(F32)
    o1, o2, o3 = RWKV_DIM, 2 * RWKV_DIM, 3 * RWKV_DIM
    o4, o5 = o3 + DECAY_LORA, o3 + DECAY_LORA + AAA_LORA
    r, k, v = u[..., :o1], u[..., o1:o2], u[..., o2:o3]
    wl, al, gl = u[..., o3:o4], u[..., o4:o5], u[..., o5:]
    w = -jax.nn.softplus(-(w0.astype(F32) + jnp.tanh(wl) @ w2.astype(F32))) - 0.5
    decay = jnp.exp(-jnp.exp(w))
    a = jax.nn.sigmoid(a0.astype(F32) + al @ a2.astype(F32))
    g = jax.nn.sigmoid(gl) @ g2.astype(F32)
    hs = (b, t, RWKV_HEADS, RWKV_HEAD_DIM)
    kk = (k * k_k.astype(F32)).reshape(hs)
    kk = kk / jnp.maximum(jnp.sqrt(jnp.sum(kk * kk, axis=-1, keepdims=True)), 1e-12)
    k = k * (1.0 + (a - 1.0) * k_a.astype(F32))
    r, k, v, a, decay = (z.reshape(hs) for z in (r, k, v, a, decay))
    y = wkv7_scan(r, decay, k, v, -kk, kk * a)
    mean = jnp.mean(y, axis=-1, keepdims=True)
    var = jnp.mean(jnp.square(y - mean), axis=-1, keepdims=True)
    y = (y - mean) * lax.rsqrt(var + RWKV_GN_EPS)
    y = y * ln_w.astype(F32).reshape(RWKV_HEADS, RWKV_HEAD_DIM) + ln_b.astype(F32).reshape(RWKV_HEADS, RWKV_HEAD_DIM)
    y = y + jnp.sum(r * k * r_k.astype(F32), axis=-1, keepdims=True) * v
    y = y.reshape(b, t, RWKV_DIM) * g
    return y.astype(mu.dtype)

def alibi_slopes(n_heads):
    return 2.0 ** (-8.0 * jnp.arange(1, n_heads + 1, dtype=F32) / n_heads)

def swa_sink_attention(proj, q_gain, k_gain, sinks):
    b, t, _ = proj.shape
    nb = t // ATT_BLOCK
    q = proj[..., :Q_DIM].reshape(b, t, KV_HEADS, Q_PER_KV, HEAD_DIM)
    k = proj[..., Q_DIM:Q_DIM + KV_DIM].reshape(b, t, KV_HEADS, HEAD_DIM)
    v = proj[..., Q_DIM + KV_DIM:].reshape(b, t, KV_HEADS, HEAD_DIM)
    q = rms_norm(q, q_gain).astype(F32).reshape(b, nb, ATT_BLOCK, KV_HEADS, Q_PER_KV, HEAD_DIM)
    k = rms_norm(k, k_gain).astype(F32).reshape(b, nb, ATT_BLOCK, KV_HEADS, HEAD_DIM)
    v = v.astype(F32).reshape(b, nb, ATT_BLOCK, KV_HEADS, HEAD_DIM)

    def with_prev(z):
        prev = jnp.pad(z, [(0, 0), (1, 0)] + [(0, 0)] * (z.ndim - 2))[:, :-1]
        return jnp.concatenate([prev, z], axis=2)

    kw, vw = with_prev(k), with_prev(v)
    s = jnp.einsum("bnqkgd,bnskd->bnkgqs", q, kw) * (HEAD_DIM ** -0.5)
    qi = jnp.arange(ATT_BLOCK)[:, None]
    sj = jnp.arange(2 * ATT_BLOCK)[None, :]
    delta = qi + ATT_BLOCK - sj
    in_band = (delta >= 0) & (delta < WINDOW)
    has_key = (jnp.arange(nb)[:, None] > 0) | (sj >= ATT_BLOCK)
    mask = in_band[None] & has_key[:, None, :]
    slopes = alibi_slopes(ATT_HEADS).reshape(KV_HEADS, Q_PER_KV)
    s = s - slopes[:, :, None, None] * delta.astype(F32)
    s = jnp.where(mask[None, :, None, None], s, -jnp.inf)
    sink = sinks.astype(F32).reshape(KV_HEADS, Q_PER_KV)[None, None, :, :, None]
    m = jnp.maximum(jnp.max(s, axis=-1), sink)
    p = jnp.exp(s - m[..., None])
    denom = jnp.sum(p, axis=-1) + jnp.exp(sink - m)
    o = jnp.einsum("bnkgqs,bnskd->bnkgqd", p, vw) / denom[..., None]
    o = o.transpose(0, 1, 4, 2, 3, 5).reshape(b, t, Q_DIM)
    return o.astype(proj.dtype)

def hier_moe(x, w_coarse, b_coarse, w_fine, b_fine, w_gate, w_up, w_down):
    b, t, d = x.shape
    n = b * t
    xt = x.reshape(n, d)
    xf = xt.astype(F32)
    coarse_p = jax.nn.softmax(xf @ w_coarse.astype(F32) + b_coarse.astype(F32), axis=-1)
    p_group, group = lax.top_k(coarse_p, 1)
    fine_logits = jnp.einsum("nd,gde->nge", xf, w_fine.astype(F32)) + b_fine.astype(F32)
    fine_sel = fine_logits[jnp.arange(n), group[:, 0]]
    p_exp, idx = lax.top_k(jax.nn.softmax(fine_sel, axis=-1), TOP_K)
    gates = p_group * p_exp / jnp.sum(p_exp, axis=-1, keepdims=True)
    expert = group * EXPERTS_PER_GROUP + idx
    a = n * TOP_K
    e_flat = expert.reshape(a)
    tok_flat = jnp.repeat(jnp.arange(n, dtype=jnp.int32), TOP_K)
    gate_flat = gates.reshape(a).astype(x.dtype)
    order = jnp.argsort(e_flat)
    e_sorted = e_flat[order]
    counts = jnp.bincount(e_flat, length=N_EXPERTS)
    padded = (counts + MOE_BLOCK - 1) // MOE_BLOCK * MOE_BLOCK
    seg_start = jnp.cumsum(counts) - counts
    pad_end = jnp.cumsum(padded)
    pad_start = pad_end - padded
    dest = pad_start[e_sorted] + jnp.arange(a) - seg_start[e_sorted]
    n_blocks = -(-a // MOE_BLOCK) + N_EXPERTS
    slots = n_blocks * MOE_BLOCK
    tok_buf = jnp.full((slots,), n, jnp.int32).at[dest].set(tok_flat[order])
    gate_buf = jnp.zeros((slots,), x.dtype).at[dest].set(gate_flat[order])
    block_expert = jnp.minimum(
        jnp.searchsorted(pad_end, jnp.arange(n_blocks) * MOE_BLOCK, side="right"), N_EXPERTS - 1)
    x_pad = jnp.concatenate([xt, jnp.zeros((1, d), xt.dtype)], axis=0)

    def run_block(args):
        tok, e = args
        xb = x_pad[tok]
        hb = jax.nn.silu(xb @ w_gate[e]) * (xb @ w_up[e])
        return hb @ w_down[e]

    y_buf = lax.map(run_block, (tok_buf.reshape(n_blocks, MOE_BLOCK), block_expert))
    y = jax.ops.segment_sum(y_buf.reshape(slots, d) * gate_buf[:, None], tok_buf, num_segments=n + 1)[:n]
    return y.reshape(b, t, d)

def setup_inputs(seed: int = 0) -> dict:
    key = jax.random.key(seed)
    ks = iter(jax.random.split(key, 64))
    ne = (DEPTH + 1) // 2
    no = DEPTH // 2

    def nrm(shape, scale):
        return jax.random.normal(next(ks), shape, F32) * scale

    def uni(shape, lo, hi):
        return jax.random.uniform(next(ks), shape, F32, lo, hi)

    d = D_MODEL
    x = nrm((BATCH, SEQ, d), 1.0)
    ln_mix = 1.0 + nrm((DEPTH, d), 0.02)
    ln_ffn = 1.0 + nrm((DEPTH, d), 0.02)
    e_w_in = nrm((ne, d, IN_EVEN_COLS), d ** -0.5)
    e_w_out = nrm((ne, MIX_EVEN, d), MIX_EVEN ** -0.5)
    ssd_conv_w = nrm((ne, SSD_CONV, SSD_CONV_DIM), SSD_CONV ** -0.5)
    ssd_conv_b = nrm((ne, SSD_CONV_DIM), 0.02)
    dt0 = jnp.exp(uni((ne, SSD_HEADS), math.log(1e-3), math.log(1e-1)))
    ssd_dt_bias = dt0 + jnp.log(-jnp.expm1(-dt0))
    ssd_a_log = jnp.log(uni((ne, SSD_HEADS), 1.0, 16.0))
    ssd_d = 1.0 + nrm((ne, SSD_HEADS), 0.1)
    ssd_norm = 1.0 + nrm((ne, SSD_INNER), 0.02)
    rwkv_mu = uni((ne, RWKV_COLS), 0.0, 1.0)
    ramp = jnp.linspace(0.0, 1.0, RWKV_DIM, dtype=F32) ** 0.85
    rwkv_w0 = -6.5 + 5.0 * ramp + nrm((ne, RWKV_DIM), 0.05)
    rwkv_w2 = nrm((ne, DECAY_LORA, RWKV_DIM), 0.1 * DECAY_LORA ** -0.5)
    rwkv_a0 = nrm((ne, RWKV_DIM), 0.1)
    rwkv_a2 = nrm((ne, AAA_LORA, RWKV_DIM), 0.1 * AAA_LORA ** -0.5)
    rwkv_g2 = nrm((ne, GATE_LORA, RWKV_DIM), GATE_LORA ** -0.5)
    rwkv_k_k = 0.85 + nrm((ne, RWKV_DIM), 0.02)
    rwkv_k_a = 1.0 + nrm((ne, RWKV_DIM), 0.02)
    rwkv_r_k = nrm((ne, RWKV_HEADS, RWKV_HEAD_DIM), 0.1)
    rwkv_ln_w = 1.0 + nrm((ne, RWKV_DIM), 0.02)
    rwkv_ln_b = nrm((ne, RWKV_DIM), 0.02)
    o_w_in = nrm((no, d, IN_ODD_COLS), d ** -0.5)
    o_w_out = nrm((no, Q_DIM, d), Q_DIM ** -0.5)
    attn_q_norm = 1.0 + nrm((no, HEAD_DIM), 0.02)
    attn_k_norm = 1.0 + nrm((no, HEAD_DIM), 0.02)
    attn_sinks = nrm((no, ATT_HEADS), 1.0)
    moe_w_coarse = nrm((DEPTH, d, EXPERT_GROUPS), d ** -0.5)
    moe_b_coarse = nrm((DEPTH, EXPERT_GROUPS), 0.01)
    moe_w_fine = nrm((DEPTH, EXPERT_GROUPS, d, EXPERTS_PER_GROUP), d ** -0.5)
    moe_b_fine = nrm((DEPTH, EXPERT_GROUPS, EXPERTS_PER_GROUP), 0.01)
    moe_w_gate = nrm((DEPTH, N_EXPERTS, d, EXPERT_HIDDEN), d ** -0.5)
    moe_w_up = nrm((DEPTH, N_EXPERTS, d, EXPERT_HIDDEN), d ** -0.5)
    moe_w_down = nrm((DEPTH, N_EXPERTS, EXPERT_HIDDEN, d), EXPERT_HIDDEN ** -0.5)
    return {
        "x": x, "ln_mix": ln_mix, "ln_ffn": ln_ffn,
        "e_w_in": e_w_in, "e_w_out": e_w_out,
        "ssd_conv_w": ssd_conv_w, "ssd_conv_b": ssd_conv_b, "ssd_dt_bias": ssd_dt_bias,
        "ssd_a_log": ssd_a_log, "ssd_d": ssd_d, "ssd_norm": ssd_norm,
        "rwkv_mu": rwkv_mu, "rwkv_w0": rwkv_w0, "rwkv_w2": rwkv_w2, "rwkv_a0": rwkv_a0,
        "rwkv_a2": rwkv_a2, "rwkv_g2": rwkv_g2, "rwkv_k_k": rwkv_k_k, "rwkv_k_a": rwkv_k_a,
        "rwkv_r_k": rwkv_r_k, "rwkv_ln_w": rwkv_ln_w, "rwkv_ln_b": rwkv_ln_b,
        "o_w_in": o_w_in, "o_w_out": o_w_out, "attn_q_norm": attn_q_norm,
        "attn_k_norm": attn_k_norm, "attn_sinks": attn_sinks,
        "moe_w_coarse": moe_w_coarse, "moe_b_coarse": moe_b_coarse,
        "moe_w_fine": moe_w_fine, "moe_b_fine": moe_b_fine,
        "moe_w_gate": moe_w_gate, "moe_w_up": moe_w_up, "moe_w_down": moe_w_down,
    }

def reference(x, ln_mix, ln_ffn, e_w_in, e_w_out, ssd_conv_w, ssd_conv_b, ssd_dt_bias,
              ssd_a_log, ssd_d, ssd_norm, rwkv_mu, rwkv_w0, rwkv_w2, rwkv_a0, rwkv_a2,
              rwkv_g2, rwkv_k_k, rwkv_k_a, rwkv_r_k, rwkv_ln_w, rwkv_ln_b, o_w_in, o_w_out,
              attn_q_norm, attn_k_norm, attn_sinks, moe_w_coarse, moe_b_coarse, moe_w_fine,
              moe_b_fine, moe_w_gate, moe_w_up, moe_w_down):
    h = x
    for layer in range(DEPTH):
        i = layer // 2
        hn = rms_norm(h, ln_mix[layer])
        if layer % 2 == 0:
            proj = hn @ e_w_in[i]
            z = proj[..., :SSD_INNER]
            xbc = proj[..., SSD_INNER:SSD_INNER + SSD_CONV_DIM]
            dt = proj[..., SSD_INNER + SSD_CONV_DIM:SSD_COLS]
            y_ssd = ssd_mixer(z, xbc, dt, ssd_conv_w[i], ssd_conv_b[i], ssd_dt_bias[i],
                              ssd_a_log[i], ssd_d[i], ssd_norm[i])
            y_rwkv = rwkv7_mixer(proj[..., SSD_COLS:], rwkv_mu[i], rwkv_w0[i], rwkv_w2[i],
                                 rwkv_a0[i], rwkv_a2[i], rwkv_g2[i], rwkv_k_k[i], rwkv_k_a[i],
                                 rwkv_r_k[i], rwkv_ln_w[i], rwkv_ln_b[i])
            mixed = jnp.concatenate([y_ssd, y_rwkv.astype(y_ssd.dtype)], axis=-1)
            h = h + (mixed @ e_w_out[i]).astype(h.dtype)
        else:
            att = swa_sink_attention(hn @ o_w_in[i], attn_q_norm[i], attn_k_norm[i], attn_sinks[i])
            h = h + (att @ o_w_out[i]).astype(h.dtype)
        hf = rms_norm(h, ln_ffn[layer])
        h = h + hier_moe(hf, moe_w_coarse[layer], moe_b_coarse[layer], moe_w_fine[layer],
                         moe_b_fine[layer], moe_w_gate[layer], moe_w_up[layer],
                         moe_w_down[layer]).astype(h.dtype)
    return h


_drawn_inputs = setup_inputs


def setup_inputs(seed=0):
    import zlib

    import numpy as np

    out = dict(_drawn_inputs(seed))
    spreads = {}
    factors = {'rwkv_w2': 7.629,
     'rwkv_k_k': 5.127,
     'rwkv_k_a': 3.122,
     'rwkv_ln_w': 2.818,
     'rwkv_ln_b': 2.772,
     'attn_q_norm': 6.291,
     'attn_k_norm': 3.862,
     'attn_sinks': 32.173,
     'moe_b_fine': 2.759}
    for name, (base, spread) in spreads.items():
        noise = np.random.default_rng([zlib.crc32(name.encode()), seed]).standard_normal(out[name].shape)
        drawn = base * np.exp(spread * noise) if base else spread * noise
        out[name] = jnp.asarray(drawn.astype(out[name].dtype))
    for name, factor in factors.items():
        out[name] = (out[name] * factor).astype(out[name].dtype)
    return out
```

```python
from contextlib import ExitStack

import concourse.bass as bass
from concourse import mybir

P = 128
F32 = mybir.dt.float32
I32 = mybir.dt.int32
U32 = mybir.dt.uint32
ALU = mybir.AluOpType
ACT = mybir.ActivationFunctionType
AX = mybir.AxisListType

D = 1024
T = 256
NT = T // P
KD = D // P
BANK = 512
NORM_EPS = 1e-6

SSD_INNER = 1024
SSD_STATE = 128
SSD_GROUPS = 4
SSD_HEADS = 16
HPG = SSD_HEADS // SSD_GROUPS
CONV_DIM = SSD_INNER + 2 * SSD_GROUPS * SSD_STATE
CONV_TAPS = 4
RWKV_DIM = 1024
RWKV_TILES = 26
HD = 64
GN_EPS = 64e-5
DECAY_FACTOR = 0.6065306597126334

ATT_HEADS = 16
KV_HEADS = 4
WINDOW = 128
OUT_OF_BAND = -1.0e30

EXPERTS = 32
GROUPS = 4
PER_GROUP = 8
HIDDEN = 512
KH = HIDDEN // P
SLOTS = 32
EXTRA_MAX = 16
NW = 2

COLS = 256
RING = 4
Z_CHUNKS = SSD_INNER // COLS
CONV_CHUNKS = CONV_DIM // COLS
RWKV_CHUNKS = RWKV_TILES * P // COLS
DT_COL = SSD_INNER + CONV_DIM
RWKV_COL = DT_COL + SSD_HEADS
ODD_CHUNKS = 6
TILES_PER_RING = RING * COLS // P


class Arena:

    def __init__(self, tensor, size, start=0):
        self.tensor, self.size, self.at = tensor, size, start

    def take(self, *dims):
        n = 1
        for d in dims:
            n *= d
        view = self.tensor[:, self.at:self.at + n]
        self.at += n
        assert self.at <= self.size, self.at
        if len(dims) == 2:
            view = view.rearrange("p (a b) -> p a b", b=dims[1])
        elif len(dims) == 3:
            view = view.rearrange("p (a b c) -> p a b c", b=dims[1], c=dims[2])
        elif len(dims) == 4:
            view = view.rearrange("p (a b c d) -> p a b c d", b=dims[1], c=dims[2], d=dims[3])
        return view


def bc(ap, *shape):
    return ap.to_broadcast([ap.shape[0], *shape])


def trunk(nc, a, out, stop_after=99):
    with ExitStack() as ctx:
        def sb(name, shape, dt=F32):
            return ctx.enter_context(nc.sbuf_tensor(name, shape, dt))

        sems = {}

        def S(name):
            if name not in sems:
                sems[name] = ctx.enter_context(nc.semaphore(name))
            return sems[name]

        h = sb("h", [P, NT, D])
        ident = sb("ident", [P, P])
        head_sum = sb("head_sum", [P, P])
        head_mean = sb("head_mean", [P, P])
        ones = sb("ones", [P, P])
        group_mean = sb("group_mean", [P, P])
        upper = sb("upper", [P, P])
        upper_strict = sb("upper_strict", [P, P])
        fold = sb("fold", [P, SLOTS])
        dup_even = sb("dup_even", [P, P])
        dup_odd = sb("dup_odd", [P, P])
        iota = sb("iota", [P, 4, SLOTS])
        mask_ar = sb("mask_ar", [P, NT, 2, P])
        mask_level = sb("mask_level", [P, 6, P])
        mask_pair = sb("mask_pair", [P, P])
        band = sb("band", [P, 2 * P])
        par = sb("par", [P, 2, P])
        gains = sb("gains", [P, 4, KD])
        router_w = sb("router_w", [P, 2, KD, GROUPS + EXPERTS])
        router_b = sb("router_b", [P, 2, GROUPS + EXPERTS])
        dt_bias = sb("dt_bias", [P, SSD_HEADS])
        a_log = sb("a_log", [P, SSD_HEADS])
        d_skip = sb("d_skip", [P, KD])
        sinks = sb("sinks", [P, ATT_HEADS])
        qk_gain = sb("qk_gain", [P, 2])
        eps = sb("eps", [P, 2])
        ss = sb("ss", [P, NT])
        rstd = sb("rstd", [P, NT])
        lists = sb("lists", [1, 2, EXTRA_MAX], I32)

        ARENA = 41800
        arena = sb("arena", [P, ARENA])
        ps = ctx.enter_context(nc.psum_tensor("ps", [P, 8, BANK], F32))

        m0 = Arena(arena, ARENA)
        hnT = m0.take(KD, T)
        ring = m0.take(RING, KD, COLS)
        zs = m0.take(KD, T)
        xbc = m0.take(CONV_DIM // P, T)
        u = m0.take(RWKV_TILES, T)
        dec = m0.take(KD, T)
        agate = m0.take(KD, T)
        gate = m0.take(KD, T)
        mixT = m0.take(2 * KD, T)
        work = m0.at
        hn = Arena(arena, ARENA, work).take(NT, D)
        wdt = Arena(arena, ARENA, work + NT * D).take(KD, SSD_HEADS)
        lora_w = Arena(arena, ARENA, work + NT * D + P).take(3, D)
        rows = Arena(arena, ARENA, work + NT * D + P + 3 * D).take(2, P)
        cbuf = Arena(arena, ARENA, work + NT * D + P + 3 * D + 2 * P).take(4, T)
        dtp = sb("dtp", [P, 8, NT, SSD_HEADS])
        CW, CB, NW_, MU = 0, 64, 80, 88
        W0, A0, KK, KA, RK, LNW, LNB = (8 * i for i in range(7))

        s0 = Arena(arena, ARENA, work)
        sx = s0.take(2, T)
        sB = s0.take(T)
        sC = s0.take(T)
        btok = s0.take(P)
        xdt = s0.take(NT, HPG, HD)
        xst = s0.take(HPG, HD)
        tria = s0.take(NT, HPG, P)
        mm = s0.take(NT, HPG, P)
        cbm = s0.take(NT, P)
        cs = s0.take(HPG, P)
        state = s0.take(HPG, HD)
        sy = s0.take(2, T)
        ssq = s0.take(2, T)
        sr = s0.take(T)

        r0 = Arena(arena, ARENA, work)
        kar = r0.take(2, NT, 2, P)
        bar = r0.take(2, NT, 2, P)
        X = r0.take(NT * 2, P)
        XT = r0.take(NT * 2, P)
        TX = r0.take(NT * 2, P)
        ar = r0.take(NT, 2, P)
        kt = r0.take(NT, P)
        bt = r0.take(NT, P)
        cum = r0.take(NT, P + 1)
        e1 = r0.take(NT, P + 1)
        e2 = r0.take(NT, P)
        kp = r0.take(T)
        tmp = r0.take(T)
        vtok = r0.take(NT, P)
        ktok = r0.take(P)
        btk = r0.take(P)
        rhs = r0.take(2, NT, HD)
        us = r0.take(2, NT, HD)
        s0T = r0.take(HD)
        edge = r0.take(8)
        vst = r0.take(T)
        kk = zs
        bonus = Arena(arena, ARENA, KD * T * 2 + RING * KD * COLS).take(KD, T)
        tmp8 = Arena(arena, ARENA, KD * T * 3 + RING * KD * COLS).take(KD, T)
        rv = u[:, 0:KD, :]
        kv_ = u[:, KD:2 * KD, :]
        vv = u[:, 2 * KD:3 * KD, :]
        wo_ring = ring.rearrange("p a b c -> p (a b c)").rearrange("p (a c) -> p a c", c=D)
        WO = RING * KD * COLS // D

        mo = Arena(arena, ARENA)
        wgu = mo.take(NW, 2, KD, HIDDEN)
        wdn = mo.take(NW, KH, D)
        hf = mo.take(NT, D)
        hfT = mo.take(KD, T)
        gus = mo.take(2, HIDDEN)
        ys = mo.take(D)
        zero = mo.take(BANK)
        xg = mo.take(KD, SLOTS)
        hidT = mo.take(KH, SLOTS)
        sil = mo.take(KH, SLOTS)
        sel = mo.take(NT, SLOTS)
        selg = mo.take(NT, P)
        selt = mo.take(NT, P)
        gT = mo.take(NT, P)
        lg = mo.take(NT, GROUPS + EXPERTS)
        c8 = mo.take(NT, 8)
        mx = mo.take(NT, 8)
        fine = mo.take(NT, PER_GROUP, GROUPS)
        fsel = mo.take(NT, 8)
        fmx = mo.take(NT, 8)
        sc = mo.take(16, NT)
        pick = mo.take(4, EXPERTS)
        both = mo.take(NT, EXPERTS)
        rank = mo.take(NT, EXPERTS)
        cnt = mo.take(6, EXPERTS)
        prod = mo.take(4, EXPERTS)
        slot = mo.take(12, 4)
        lst = mo.take(EXTRA_MAX, EXPERTS)
        lsti = mo.take(2, EXTRA_MAX)
        idx = sb("idx", [P, 2, NT, 8], U32)

        m1 = Arena(arena, ARENA)
        m1.take(KD, T)
        m1.take(RING, KD, COLS)
        qkv = m1.take(12, T)
        sqs = m1.take(12, T)
        kdup = m1.take(KV_HEADS, T)
        vtk = m1.take(NT, 2, P)
        attT = m1.take(KD, T)
        qs = m1.take(2, T)
        pr = m1.take(4, 2 * P)
        pT = m1.take(4, 2, P)
        vs = m1.take(NT, HD)
        ks = m1.take(T)
        st = m1.take(8, 4)

        block = ctx.enter_context(nc.Block())

        @block.sync
        def _(sp):
            sp.dma_start(h[:], a["x"].rearrange("b (t p) d -> p (b t) d", p=P)).then_inc(S("x_loaded"), 16)
            n = 0

            def small(dst, src):
                nonlocal n
                sp.dma_start(dst, src, allow_slow_non_contiguous=True).then_inc(S("params_loaded"), 16)
                n += 1
            row = lambda ap: ap.rearrange("(r f) -> r f", f=P)
            small(rows[0:64, 0, :], a["ssd_conv_w"][0].rearrange("t (j f) -> (t j) f", f=P))
            small(rows[64:80, 0, :], row(a["ssd_conv_b"][0]))
            small(rows[80:88, 0, :], row(a["ssd_norm"][0]))
            small(rows[88:114, 0, :], row(a["rwkv_mu"][0]))
            for i, name in enumerate(("rwkv_w0", "rwkv_a0", "rwkv_k_k", "rwkv_k_a")):
                small(rows[8 * i:8 * i + 8, 1, :], row(a[name][0]))
            small(rows[32:40, 1, :], a["rwkv_r_k"][0].rearrange("(r b) f -> r (b f)", b=2))
            small(rows[40:48, 1, :], row(a["rwkv_ln_w"][0]))
            small(rows[48:56, 1, :], row(a["rwkv_ln_b"][0]))
            for i, (name, l) in enumerate((("ln_mix", 0), ("ln_ffn", 0), ("ln_mix", 1), ("ln_ffn", 1))):
                small(gains[:, i, :], a[name][l].rearrange("(p k) -> p k", k=KD))
            for l in range(2):
                small(router_w[:, l, :, 0:GROUPS], a["moe_w_coarse"][l].rearrange("(p k) e -> p k e", k=KD))
                for g in range(GROUPS):
                    small(router_w[:, l, :, GROUPS + 8 * g:GROUPS + 8 * g + 8],
                          a["moe_w_fine"][l, g].rearrange("(p k) e -> p k e", k=KD))
                small(router_b[:, l, 0:GROUPS], a["moe_b_coarse"][l].partition_broadcast(P))
                small(router_b[:, l, GROUPS:], a["moe_b_fine"][l].rearrange("g e -> (g e)").partition_broadcast(P))
            small(dt_bias[:], a["ssd_dt_bias"][0].partition_broadcast(P))
            small(a_log[:], a["ssd_a_log"][0].partition_broadcast(P))
            small(sinks[:], a["attn_sinks"][0].partition_broadcast(P))
            for half in range(2):
                small(d_skip[64 * half:64 * half + 64, :],
                      a["ssd_d"][0].rearrange("(j e) -> e j", e=2)[half].partition_broadcast(64))
                small(qk_gain[64 * half:64 * half + 64, 0:1], a["attn_q_norm"][0].rearrange("(p k) -> p k", k=1))
                small(qk_gain[64 * half:64 * half + 64, 1:2], a["attn_k_norm"][0].rearrange("(p k) -> p k", k=1))
            small(wdt, a["e_w_in"][0].rearrange("(p k) c -> p k c", k=KD)[:, :, DT_COL:RWKV_COL])
            small(lora_w[0:64, 0, :], a["rwkv_w2"][0])
            small(lora_w[64:128, 1, :], a["rwkv_a2"][0])
            small(lora_w[:, 2, :], a["rwkv_g2"][0])
            assert n == PARAM_LOADS, n

            w_in = a["e_w_in"][0].rearrange("(p k) c -> p k c", k=KD)

            def chunk(s, col):
                sp.dma_start(ring[:, s], w_in[:, :, bass.ds(col, COLS)]).then_inc(S(f"ring_loaded{s}"), 16)
            for s in range(Z_CHUNKS):
                chunk(s, s * COLS)
            with sp.Fori(0, CONV_CHUNKS // RING) as i:
                for s in range(RING):
                    sp.wait_ge(S("projected"), 2 * (i * RING + s) + 2)
                    chunk(s, (i * RING + Z_CHUNKS + s) * COLS)
            with sp.Fori(0, RWKV_CHUNKS // RING) as i:
                for s in range(RING):
                    sp.wait_ge(S("projected"), 2 * (i * RING + CONV_CHUNKS + s) + 2)
                    chunk(s, (i * RING + s) * COLS + RWKV_COL)
            sp.wait_ge(S("projected"), 2 * (CONV_CHUNKS + 3 * RING) + 2)
            chunk(0, 3 * RING * COLS + RWKV_COL)

            def out_weights(w, tiles, prefix, used_before):
                sp.wait_ge(S("projected"), used_before)
                for j in range(tiles):
                    if j >= WO:
                        sp.wait_ge(S(f"{prefix}_used"), j - WO + 1)
                    sp.dma_start(wo_ring[:, j % WO, :], w.rearrange("(j p) d -> j p d", p=P)[j]).then_inc(
                        S(f"wo_loaded{j % WO}"), 16)
            out_weights(a["e_w_out"][0], 2 * KD, "wo0", 2 * (Z_CHUNKS + CONV_CHUNKS + RWKV_CHUNKS))

            def experts(l):
                wg = a["moe_w_gate"][l].rearrange("e (p k) f -> e p k f", k=KD)
                wu = a["moe_w_up"][l].rearrange("e (p k) f -> e p k f", k=KD)
                wd = a["moe_w_down"][l].rearrange("e (p k) d -> e p k d", k=KH)
                n_items = EXPERTS
                sp.wait_ge(S("h_mixed"), l + 1)
                with sp.Fori(0, EXPERTS // NW) as i:
                    for s in range(NW):
                        sp.wait_ge(S(f"gu_used_l{l}"), i * NW + s + 1)
                        sp.dma_start(wgu[:, s, 0], wg[bass.ds(i * NW + s, 1)]).then_inc(S(f"gu_loaded{s}_l{l}"), 16)
                        sp.dma_start(wgu[:, s, 1], wu[bass.ds(i * NW + s, 1)]).then_inc(S(f"gu_loaded{s}_l{l}"), 16)
                        sp.wait_ge(S(f"dn_used_l{l}"), i * NW + s + 1)
                        sp.dma_start(wdn[:, s], wd[bass.ds(i * NW + s, 1)]).then_inc(S(f"dn_loaded{s}_l{l}"), 16)
                sp.wait_ge(S("lists_ready"), l + 1)
                extra = sp.value_load(lists[0:1, l, EXTRA_MAX - 1:EXTRA_MAX], min_val=0, max_val=EXTRA_MAX - 1)
                with sp.If(extra > 0):
                    with sp.Fori(0, extra) as o:
                        e = sp.value_load(lists[0:1, l, bass.ds(o, 1)], min_val=0, max_val=EXPERTS - 1)
                        sp.wait_ge(S(f"gu_used_l{l}"), o + n_items + NW)
                        sp.dma_start(wgu[:, 0, 0], wg[bass.ds(e, 1)]).then_inc(S(f"gu_loaded0_l{l}"), 16)
                        sp.dma_start(wgu[:, 0, 1], wu[bass.ds(e, 1)]).then_inc(S(f"gu_loaded0_l{l}"), 16)
                        sp.wait_ge(S(f"dn_used_l{l}"), o + n_items + NW)
                        sp.dma_start(wdn[:, 0], wd[bass.ds(e, 1)]).then_inc(S(f"dn_loaded0_l{l}"), 16)
            experts(0)

            w_odd = a["o_w_in"][0].rearrange("(p k) c -> p k c", k=KD)
            sp.wait_ge(S("moe_added"), 1)
            for c in range(ODD_CHUNKS):
                if c >= RING:
                    sp.wait_ge(S("qkv_ready"), 2 * (c - RING) + 2)
                sp.dma_start(ring[:, c % RING], w_odd[:, :, c * COLS:(c + 1) * COLS]).then_inc(
                    S(f"ring_loaded{c % RING}"), 16)
            sp.wait_ge(S("qkv_ready"), 2 * ODD_CHUNKS)
            for j in range(KD):
                sp.dma_start(wo_ring[:, j, :], a["o_w_out"][0].rearrange("(j p) d -> j p d", p=P)[j]).then_inc(
                    S(f"wo_loaded{j}"), 16)
            experts(1)
            sp.wait_ge(S("moe_added"), 2)
            sp.dma_start(out.rearrange("b (t p) d -> p (b t) d", p=P), h[:]).then_inc(S("stored"), 16)
            sp.wait_ge(S("stored"), 16)

        @block.gpsimd
        def _(pool):
            for t, v in ((ident, 1.0), (ones, 1.0), (head_sum, 0.0), (head_mean, 0.0), (group_mean, 1.0 / 256),
                         (upper, 1.0), (upper_strict, 1.0), (mask_level, 0.0), (mask_pair, 0.0), (mask_ar, 1.0)):
                pool.memset(t[:], v)
            pool.memset(eps[:, 0:1], NORM_EPS)
            pool.memset(eps[:, 1:2], GN_EPS)
            pool.drain()
            for half in range(2):
                q = slice(64 * half, 64 * half + 64)
                pool.memset(head_sum[q, q], 1.0)
                pool.memset(head_mean[q, q], 1.0 / HD)
            pool.drain()
            pool.affine_select(ident[:], ident[:], [[1, P]], ALU.is_equal, 0.0, base=0, channel_multiplier=-1)
            pool.affine_select(upper[:], upper[:], [[1, P]], ALU.is_ge, 0.0, base=0, channel_multiplier=-1)
            pool.affine_select(upper_strict[:], upper_strict[:], [[1, P]], ALU.is_gt, 0.0, base=0,
                               channel_multiplier=-1)
            pool.affine_select(mask_ar[:, :, 0, :], mask_ar[:, :, 0, :], [[0, NT], [1, P]], ALU.is_gt, 0.0, base=0,
                               channel_multiplier=-1)
            pool.affine_select(mask_ar[:, :, 1, :], mask_ar[:, :, 1, :], [[0, NT], [1, P]], ALU.is_ge, 0.0, base=0,
                               channel_multiplier=-1)
            pair = mask_pair[:].rearrange("p (b r) -> p b r", r=2)[:, :, 1:2]
            pool.affine_select(pair, bc(ones[:, 0:1].unsqueeze(2), P // 2, 1), [[2, P // 2], [0, 1]], ALU.is_equal, 0.0,
                               base=0, channel_multiplier=-1)
            for n in range(6):
                m = 2 << n
                v = mask_level[:, n, :].rearrange("p (b r) -> p b r", r=2 * m)[:, :, 0:m]
                one = bc(ones[:, 0:1].unsqueeze(2), P // (2 * m), m)
                pool.affine_select(v, one, [[-2 * m, P // (2 * m)], [0, m]], ALU.is_ge, 0.0, base=-m,
                                   channel_multiplier=1)
                pool.drain()
                pool.affine_select(v, v, [[2 * m, P // (2 * m)], [0, m]], ALU.is_ge, 0.0, base=2 * m - 1,
                                   channel_multiplier=-1)
            pool.iota(band[:], [[1, 2 * P]], base=-P, channel_multiplier=-1, allow_small_or_imprecise_dtypes=True)
            pool.iota(iota[:], [[0, 4], [1, SLOTS]], base=0, channel_multiplier=0, allow_small_or_imprecise_dtypes=True)
            pool.drain()
            pool.affine_select(band[:], band[:], [[-1, 2 * P]], ALU.is_ge, OUT_OF_BAND, base=P, channel_multiplier=1)
            pool.drain()
            pool.affine_select(band[:], band[:], [[1, 2 * P]], ALU.is_gt, OUT_OF_BAND, base=0, channel_multiplier=-1)
            pool.drain()
            for dup, half in ((dup_even, 0), (dup_odd, 1)):
                for to in range(2):
                    pool.tensor_copy(dup[:, 64 * to:64 * to + 64], ident[:, 64 * half:64 * half + 64])
            pool.drain().then_inc(S("consts_ready"), 1)

            with pool.Fori(0, SSD_GROUPS) as g:
                pool.wait_ge(S("silu_done"), 4 + CONV_DIM // P)
                pool.wait_ge(S("ssd_free"), g + 1)
                pool.sem_inc(S("pool_waited"), 1)
                pool.tensor_copy(sB, xbc[:, bass.ds(g + 8, 1), :].rearrange("p a t -> p (a t)"))
                pool.tensor_copy(sC, xbc[:, bass.ds(g + 12, 1), :].rearrange("p a t -> p (a t)"))
                pool.tensor_copy(sx, xbc[:, bass.ds(g * 2, 2), :]).then_inc(S("ssd_staged"), 1)

            with pool.Fori(0, KD) as j:
                pool.wait_ge(S("x_free"), j + 1)
                pool.sem_inc(S("pool_waited"), 1)
                pool.tensor_copy(XT, bc(ident[:].unsqueeze(1), 4, P))
                pool.tensor_copy(X, bc(ident[:].unsqueeze(1), 4, P)).then_inc(S("x_reset"), 1)

            with pool.Fori(0, KV_HEADS) as g:
                pool.wait_ge(S("att_inputs"), 1)
                pool.wait_ge(S("att_free"), g + 1)
                pool.sem_inc(S("pool_waited"), 1)
                pool.tensor_copy(vs, vtk.rearrange("p t a b -> p t (a b)")[:, :, bass.ds(g * HD, HD)])
                pool.tensor_copy(ks, kdup[:, bass.ds(g, 1), :].rearrange("p a t -> p (a t)"))
                pool.tensor_copy(qs, qkv[:, bass.ds(g * 2, 2), :]).then_inc(S("att_staged"), 1)

        @block.tensor
        def _(pe):
            def transposes(n):
                src = hn if n % 2 == 0 else hf
                pe.wait_ge(S("hn_ready"), n + 1)
                for b in range(4):
                    for q in range(4):
                        k, t = (4 * b + q) // NT, q % NT
                        i = pe.transpose(ps[:, b, q * P:(q + 1) * P],
                                         src[:, t, :].rearrange("p (f k) -> p k f", k=KD)[:, k, :], ident[:])
                    i.then_inc(S("hn_turned"), 1)
                pe.wait_ge(S("hnT_ready"), n + 1)

            for l in range(2):
                pe.sem_inc(S(f"gu_used_l{l}"), NW)
                pe.sem_inc(S(f"dn_used_l{l}"), NW)
            pe.wait_ge(S("consts_ready"), 1)
            pe.wait_ge(S("params_loaded"), 16 * PARAM_LOADS)
            pe.transpose(ps[:, 7, 0:114], rows[0:114, 0, :], ident[0:114, 0:114])
            pe.transpose(ps[:, 7, P:P + 56], rows[0:56, 1, :], ident[0:56, 0:56]).then_inc(S("par_turned"), 1)
            transposes(0)
            for t in range(NT):
                for k in range(KD):
                    i = pe.matmul(ps[:, 6, t * SSD_HEADS:(t + 1) * SSD_HEADS], hnT[:, k, t * P:(t + 1) * P],
                                  wdt[:, k, :], start=(k == 0), stop=(k == KD - 1))
            i.then_inc(S("dt_ready"), 1)
            pe.wait_ge(S("dt_taken"), 1)
            pe.wait_ge(S("par_ready"), 1)

            def project(s, half, done):
                b = 2 * s + half
                for k in range(KD):
                    i = pe.matmul(ps[:, b, 0:T], ring[:, s, k, half * P:(half + 1) * P], hnT[:, k, :],
                                  start=(k == 0), stop=(k == KD - 1))
                i.then_inc(done, 1)
            for s in range(RING):
                pe.wait_ge(S(f"ring_loaded{s}"), 16)
                for half in range(2):
                    project(s, half, S("projected"))
            pe.wait_ge(S("z_done"), 2 * Z_CHUNKS)
            with pe.Fori(0, CONV_CHUNKS // RING) as i:
                for s in range(RING):
                    pe.wait_ge(S(f"ring_loaded{s}"), i * 16 + 32)
                    for half in range(2):
                        pe.wait_ge(S("conv_done"), i * TILES_PER_RING + 2 * s + half + 1)
                        project(s, half, S("projected"))
            with pe.Fori(0, RWKV_CHUNKS // RING) as i:
                for s in range(RING):
                    pe.wait_ge(S(f"ring_loaded{s}"), i * 16 + 64)
                    for half in range(2):
                        pe.wait_ge(S("conv_done"), i * TILES_PER_RING + 16 + 2 * s + half + 1)
                        project(s, half, S("projected"))
            pe.wait_ge(S("ring_loaded0"), 16 * 7)
            for half in range(2):
                pe.wait_ge(S("conv_done"), 40 + half + 1)
                project(0, half, S("projected"))

            pe.wait_ge(S("lora_ready"), 1)
            pe.wait_ge(S("conv_done"), 8 + 16 + RWKV_TILES)
            n = 0
            for kind, (lo, hi, src) in enumerate(((0, 64, 24), (64, 128, 24), (0, 128, 25))):
                for j in range(KD):
                    b = n // 2 % 8
                    if n >= 16 and n % 2 == 0:
                        pe.wait_ge(S("lora_taken"), (n - 16) // 2 + 1)
                    i = pe.matmul(ps[:, b, (n % 2) * T:(n % 2 + 1) * T], lora_w[lo:hi, kind, j * P:(j + 1) * P],
                                  u[lo:hi, src, :], start=True, stop=True)
                    if n % 2:
                        i.then_inc(S("lora_out"), 1)
                    n += 1
            pe.wait_ge(S("lora_taken"), 12)

            pe.wait_ge(S("adt_ready"), 1)
            for c in range(NT):
                pe.matmul(ps[:, 0, c * SSD_HEADS:(c + 1) * SSD_HEADS], upper[:], dtp[:, 1, c, :], start=True, stop=True)
                i = pe.matmul(ps[:, 1, c * SSD_HEADS:(c + 1) * SSD_HEADS], ones[:], dtp[:, 1, c, :],
                              start=True, stop=True)
            i.then_inc(S("acum_ready"), 1)
            pe.wait_ge(S("acum_taken"), 1)

            with pe.Fori(0, SSD_GROUPS) as g:
                pe.wait_ge(S("ssd_staged"), g + 1)
                for c in range(NT):
                    for t in range(2):
                        pe.transpose(ps[:, 0, (2 * c + t) * P:(2 * c + t + 1) * P], sx[:, t, c * P:(c + 1) * P],
                                     ident[:])
                pe.transpose(ps[:, 1, 0:P], sB[:, 0:P], ident[:])
                for c in range(NT):
                    i = pe.matmul(ps[:, 2, c * P:(c + 1) * P], sB[:, c * P:(c + 1) * P], sC[:, c * P:(c + 1) * P],
                                  start=True, stop=True)
                i.then_inc(S("ssd_cb"), 1)
                pe.wait_ge(S("ssd_tria"), g + 1)
                for c in range(NT):
                    i = pe.matmul(ps[:, 3 + c, :], ones[:], tria[:, c].rearrange("p a b -> p (a b)"),
                                  start=True, stop=True)
                i.then_inc(S("ssd_acum"), 1)
                pe.wait_ge(S("ssd_tok"), g + 1)
                pe.matmul(ps[:, 5, 0:HPG * HD], btok, xst.rearrange("p a b -> p (a b)"), start=True,
                          stop=True).then_inc(S("ssd_state"), 1)
                pe.wait_ge(S("ssd_m"), g + 1)
                for c in range(NT):
                    for hh in range(HPG):
                        t, half = hh // 2, hh % 2
                        o = ps[64 * half:64 * half + 64, 6, t * T + c * P:t * T + (c + 1) * P]
                        i = pe.matmul(o, xdt[:, c, hh, :], mm[:, c, hh, :], start=True, stop=(c == 0),
                                      skip_group_check=True)
                        if c == 1:
                            i = pe.matmul(o, state[:, hh, :], cs[:, hh, :], start=False, stop=True,
                                          skip_group_check=True)
                i.then_inc(S("ssd_y"), 1)
                pe.wait_ge(S("ssd_sq"), g + 1)
                for t in range(2):
                    i = pe.matmul(ps[:, 7, 0:T], group_mean[:], ssq[:, t, :], start=(t == 0), stop=(t == 1))
                i.then_inc(S("ssd_var"), 1)
            pe.wait_ge(S("kk_sq"), 1)
            for j in range(KD):
                i = pe.matmul(ps[:, j // 2, (j % 2) * T:(j % 2 + 1) * T], head_sum[:], tmp8[:, j, :], start=True,
                              stop=True)
            i.then_inc(S("kk_len"), 1)

            with pe.Fori(0, KD) as j:
                pe.wait_ge(S("rk_ready"), j + 1)
                pe.matmul(ps[:, 4, 0:T], head_sum[:], tmp, start=True, stop=True).then_inc(S("rk_sum"), 1)
                pe.wait_ge(S("decayed"), j + 1)
                for c in range(NT):
                    pe.transpose(ps[:, 5, c * P:(c + 1) * P], vst[:, c * P:(c + 1) * P], ident[:])
                pe.transpose(ps[:, 5, 2 * P:3 * P], kt[:, 0, :], ident[:])
                pe.transpose(ps[:, 5, 3 * P:4 * P], bt[:, 0, :], ident[:]).then_inc(S("tok_turned"), 1)
                for n, src in enumerate((kt, bt)):
                    for hh in range(2):
                        q = slice(64 * hh, 64 * hh + 64)
                        for c in range(NT):
                            i = pe.matmul(ps[:, 2 * n + hh, c * 2 * P:(c + 1) * 2 * P], src[q, c, :],
                                          ar[q, c].rearrange("p a b -> p (a b)"), start=True, stop=True)
                i.then_inc(S("scores"), 1)
                pe.wait_ge(S("xt_pairs"), j + 1)
                for m in range(4):
                    i = pe.transpose(ps[:, 6, m * P:(m + 1) * P], XT[:, m, :], ident[:])
                i.then_inc(S("x_turned"), 1)
                for n in range(6):
                    pe.wait_ge(S("x_level"), j * 7 + n + 1)
                    for m in range(4):
                        c, hh = m // 2, m % 2
                        i = pe.matmul(ps[:, 7, m * P:(m + 1) * P], bar[:, hh, c, 0, :], X[:, m, :], start=True,
                                      stop=True)
                    i.then_inc(S("lx"), 1)
                    pe.wait_ge(S("lx_taken"), j * 6 + n + 1)
                    for m in range(4):
                        i = pe.matmul(ps[:, 6, m * P:(m + 1) * P], XT[:, m, :], TX[:, m, :], start=True, stop=True)
                    i.then_inc(S("xlx"), 1)
                    pe.wait_ge(S("x_level"), j * 7 + n + 2)
                    for m in range(4):
                        i = pe.transpose(ps[:, 7, m * P:(m + 1) * P], X[:, m, :], ident[:])
                    i.then_inc(S("x_back"), 1)
                    pe.wait_ge(S("xt_taken"), j * 6 + n + 1)
                pe.wait_ge(S("tok_ready"), j + 1)
                for c in range(NT):
                    for hh in range(2):
                        q = slice(64 * hh, 64 * hh + 64)
                        o = ps[:, hh, 0:HD]
                        i = pe.matmul(o, kar[:, hh, c, 0, :], vtok[:, c, q], start=True, stop=(c == 0))
                        if c:
                            i = pe.matmul(o, ar[q, c, 0, :], s0T[q, :], start=False, stop=True)
                    i.then_inc(S("rhs_out"), 1)
                    pe.wait_ge(S("rhs_ready"), j * 2 + c + 1)
                    for hh in range(2):
                        i = pe.matmul(ps[:, 2 + hh, 0:HD], XT[:, 2 * c + hh, :], rhs[:, hh, c, :], start=True,
                                      stop=True)
                    i.then_inc(S("u_out"), 1)
                    pe.wait_ge(S("u_ready"), j * 2 + c + 1)
                    if c == 0:
                        for hh in range(2):
                            q = slice(64 * hh, 64 * hh + 64)
                            pe.matmul(ps[q, 4, 0:HD], ktok[:, q], vtok[:, 0, q], start=True, stop=False,
                                      skip_group_check=True)
                            i = pe.matmul(ps[q, 4, 0:HD], btk[:, q], us[:, hh, 0, :], start=False, stop=True,
                                          skip_group_check=True)
                        i.then_inc(S("s0_out"), 1)
                        pe.wait_ge(S("s0_ready"), j + 1)
                    for hh in range(2):
                        q = slice(64 * hh, 64 * hh + 64)
                        o = ps[q, 5, c * P:(c + 1) * P]
                        pe.matmul(o, vtok[:, c, q], kar[:, hh, c, 1, :], start=True, stop=False, skip_group_check=True)
                        i = pe.matmul(o, us[:, hh, c, :], bar[:, hh, c, 1, :], start=False, stop=(c == 0),
                                      skip_group_check=True)
                        if c:
                            i = pe.matmul(o, s0T[q, :], ar[q, c, 1, :], start=False, stop=True, skip_group_check=True)
                i.then_inc(S("y_out"), 1)
                pe.wait_ge(S("y_taken"), j + 1)
            for j in range(KD):
                i = pe.matmul(ps[:, j // 2, (j % 2) * T:(j % 2 + 1) * T], head_mean[:], mixT[:, KD + j, :],
                              start=True, stop=True)
            i.then_inc(S("gn_mean"), 1)
            pe.wait_ge(S("gn_sq"), 1)
            for j in range(KD):
                i = pe.matmul(ps[:, 4 + j // 2, (j % 2) * T:(j % 2 + 1) * T], head_mean[:], tmp8[:, j, :],
                              start=True, stop=True)
            i.then_inc(S("gn_var"), 1)

            def project_out(src, tiles, prefix, loaded_before):
                for j in range(tiles):
                    pe.wait_ge(S(f"wo_loaded{j % WO}"), 16 * (loaded_before + j // WO + 1))
                    for t in range(NT):
                        for half in range(2):
                            i = pe.matmul(ps[:, 2 * t + half, :], src[:, j, t * P:(t + 1) * P],
                                          wo_ring[:, j % WO, half * BANK:(half + 1) * BANK], start=(j == 0),
                                          stop=(j == tiles - 1))
                    i.then_inc(S(f"{prefix}_used"), 1)
            pe.wait_ge(S("mixed"), 1)
            project_out(mixT, 2 * KD, "wo0", 0)

            def gather(n_done):
                for k in range(KD):
                    for t in range(NT):
                        i = pe.matmul(ps[:, 6, k * SLOTS:(k + 1) * SLOTS],
                                      hf[:, t, :].rearrange("p (f k) -> p k f", k=KD)[:, k, :], sel[:, t, :],
                                      start=(t == 0), stop=(t == NT - 1))
                return i

            def moe(l):
                transposes(2 * l + 1)
                for t in range(NT):
                    for k in range(KD):
                        i = pe.matmul(ps[:, 4, t * 64:t * 64 + GROUPS + EXPERTS], hfT[:, k, t * P:(t + 1) * P],
                                      router_w[:, l, k, :], start=(k == 0), stop=(k == KD - 1))
                i.then_inc(S("logits"), 1)
                pe.wait_ge(S("picked"), l + 1)
                pe.matmul(ps[:, 5, 0:EXPERTS], upper_strict[:], both[:, 0, :], start=True, stop=True)
                pe.matmul(ps[:, 5, EXPERTS:2 * EXPERTS], upper_strict[:], both[:, 1, :], start=True, stop=False)
                pe.matmul(ps[:, 5, EXPERTS:2 * EXPERTS], ones[:], both[:, 0, :], start=False, stop=True)
                for t in range(NT):
                    i = pe.matmul(ps[:, 5, 2 * EXPERTS:3 * EXPERTS], ones[:], both[:, t, :], start=(t == 0),
                                  stop=(t == 1))
                i.then_inc(S("ranked"), 1)
                pe.wait_ge(S("lists_ready"), l + 1)
                for b in range(4):
                    pe.matmul(ps[:, b, :], zero[:, 0:P], zero, start=True, stop=False, skip_group_check=True)
                pe.wait_ge(S(f"sel_ready_l{l}"), 1)
                gather(l).then_inc(S(f"gathered_l{l}"), 1)

                def scatter():
                    for t in range(NT):
                        for half in range(2):
                            i = pe.matmul(ps[:, 2 * t + half, :], gT[:, t, :], ys[:, half * BANK:(half + 1) * BANK],
                                          start=False, stop=False, skip_group_check=True)
                    return i

                def item(n, s, loaded):
                    pe.wait_ge(S(f"xg_ready_l{l}"), n + 1)
                    pe.wait_ge(S(f"gu_loaded{s}_l{l}"), loaded * 32 + 32)
                    for w in range(2):
                        for kk2 in range(2):
                            for q in range(4):
                                i = pe.matmul(ps[32 * q:32 * q + 32, 4 + w, :], xg[:, 2 * q + kk2, :],
                                              wgu[:, s, w, 2 * q + kk2, :], start=(kk2 == 0), stop=(kk2 == 1),
                                              skip_group_check=True)
                    i.then_inc(S(f"gu_used_l{l}"), 1)
                    scatter()
                    pe.wait_ge(S(f"selg_ready_l{l}"), n + 1)
                    for t in range(NT):
                        i = pe.transpose(ps[:, 6, t * P:(t + 1) * P], selg[:, t, :], ident[:])
                    i.then_inc(S(f"selg_turned_l{l}"), 1)
                    pe.wait_ge(S(f"gate_copied_l{l}"), n + 1)
                    pe.wait_ge(S(f"up_copied_l{l}"), n + 1)
                    for w in range(2):
                        for k in range(KH):
                            c = T + (w * KH + k) * SLOTS
                            i = pe.matmul(ps[:, 7, c:c + SLOTS],
                                          gus[:, w, :].rearrange("p (f k) -> p k f", k=KH)[:, k, :], fold[:],
                                          start=True, stop=True)
                    i.then_inc(S(f"folded_l{l}"), 1)
                    pe.wait_ge(S(f"gT_copied_l{l}"), n + 1)
                    pe.wait_ge(S(f"sel_ready_l{l}"), n + 2)
                    gather(l).then_inc(S(f"gathered_l{l}"), 1)
                    pe.wait_ge(S(f"hid_ready_l{l}"), n + 1)
                    pe.wait_ge(S(f"dn_loaded{s}_l{l}"), loaded * 16 + 16)
                    for half in range(2):
                        for q in range(4):
                            i = pe.matmul(ps[32 * q:32 * q + 32, 4 + half, :], hidT[:, q, :],
                                          wdn[:, s, q, half * BANK:(half + 1) * BANK], start=True, stop=True,
                                          skip_group_check=True)
                    i.then_inc(S(f"dn_used_l{l}"), 1)
                    pe.wait_ge(S(f"y0_copied_l{l}"), n + 1)
                    pe.wait_ge(S(f"y1_copied_l{l}"), n + 1)

                with pe.Fori(0, EXPERTS // NW) as i:
                    for s in range(NW):
                        item(i * NW + s, s, i)
                extra = pe.value_load(lists[0:1, l, EXTRA_MAX - 1:EXTRA_MAX], min_val=0, max_val=EXTRA_MAX - 1)
                with pe.If(extra > 0):
                    with pe.Fori(0, extra) as o:
                        item(o + EXPERTS, 0, o + EXPERTS // NW)
                for b in range(4):
                    t, half = b // 2, b % 2
                    i = pe.matmul(ps[:, b, :], gT[:, t, :], ys[:, half * BANK:(half + 1) * BANK], start=False,
                                  stop=True, skip_group_check=True)
                i.then_inc(S("moe_summed"), 1)
            moe(0)

            transposes(2)
            for c in range(ODD_CHUNKS):
                s = c % RING
                pe.wait_ge(S(f"ring_loaded{s}"), 16 * (c // RING + 1 + (7 if s == 0 else 6)))
                for half in range(2):
                    if c >= RING:
                        pe.wait_ge(S("qkv_taken"), 2 * (c - RING) + half + 1)
                    project(s, half, S("qkv_ready"))
            pe.wait_ge(S("qk_sq"), 1)
            for j in range(10):
                i = pe.matmul(ps[:, j // 2, (j % 2) * T:(j % 2 + 1) * T], head_mean[:], sqs[:, j, :], start=True,
                              stop=True)
            i.then_inc(S("qk_ms"), 1)
            pe.wait_ge(S("qk_normed"), 1)
            for g in range(KV_HEADS):
                pe.matmul(ps[:, g // 2, (g % 2) * T:(g % 2 + 1) * T], (dup_even, dup_odd)[g % 2][:], qkv[:, 8 + g // 2, :],
                          start=True, stop=True)
            for j in range(2):
                for t in range(NT):
                    i = pe.transpose(ps[:, 2, (2 * t + j) * P:(2 * t + j + 1) * P], qkv[:, 10 + j, t * P:(t + 1) * P],
                                     ident[:])
            i.then_inc(S("kv_out"), 1)
            with pe.Fori(0, KV_HEADS) as g:
                pe.wait_ge(S("att_staged"), g + 1)
                for t in range(NT):
                    n_keys = P if t == 0 else 2 * P
                    for hh in range(4):
                        q = slice(64 * (hh % 2), 64 * (hh % 2) + 64)
                        i = pe.matmul(ps[:, hh, 0:n_keys], qs[q, hh // 2, t * P:(t + 1) * P],
                                      ks[q, 0:n_keys],
                                      start=True, stop=True)
                    i.then_inc(S("qk_out"), 1)
                    pe.wait_ge(S("probs"), g * 2 + t + 1)
                    for hh in range(4):
                        for kb in range(t + 1):
                            i = pe.transpose(ps[:, 4 + kb, hh * P:(hh + 1) * P], pr[:, hh, kb * P:(kb + 1) * P],
                                             ident[:])
                    i.then_inc(S("probs_turned"), 1)
                    pe.wait_ge(S("pT_ready"), g * 2 + t + 1)
                    for hh in range(4):
                        half = hh % 2
                        for kb in range(t + 1):
                            i = pe.matmul(ps[64 * half:64 * half + 64, 6, (hh // 2) * P:(hh // 2 + 1) * P],
                                          vs[:, kb, :], pT[:, hh, kb, :], start=(kb == 0), stop=(kb == t),
                                          skip_group_check=True)
                    i.then_inc(S("att_out"), 1)
                    pe.wait_ge(S("att_taken"), g * 2 + t + 1)
            project_out(attT, KD, "wo1", 2 * KD // WO)
            moe(1)

        @block.scalar
        def _(act):
            def norm_squares(n):
                dst = hn if n % 2 == 0 else hf
                if n == 0:
                    act.wait_ge(S("x_loaded"), 16)
                    act.wait_ge(S("consts_ready"), 1)
                elif n % 2:
                    act.wait_ge(S("h_mixed"), n // 2 + 1)
                else:
                    act.wait_ge(S("moe_added"), n // 2)
                for t in range(NT):
                    act.activation(dst[:, t, :], h[:, t, :], ACT.Square, accum_out=ss[:, t:t + 1])
                act.drain()
                act.activation(ss[:], ss[:], ACT.Sqrt, bias=eps[:, 0:1], scale=1.0 / D).then_inc(S("rms_ready"), 1)
            act.sem_inc(S("silu_done"), 4)
            norm_squares(0)
            for t in range(2 * Z_CHUNKS):
                act.wait_ge(S("projected"), t + 1)
                act.activation(zs[:, t, :], ps[:, t, 0:T], ACT.Silu).then_inc(S("z_done"), 1)
            with act.Fori(0, CONV_DIM // P // 4) as i:
                for s in range(4):
                    act.wait_ge(S("conv_done"), i * 4 + 8 + s + 1)
                    act.activation(xbc[:, bass.ds(i * 4 + s, 1), :].rearrange("p a t -> p (a t)"), cbuf[:, s, :],
                                   ACT.Silu).then_inc(S("silu_done"), 1)
            act.wait_ge(S("conv_done"), 8 + 16 + RWKV_TILES)
            act.activation(u[0:64, 24, :], u[0:64, 24, :], ACT.Tanh)
            act.activation(u[:, 25, :], u[:, 25, :], ACT.Sigmoid)
            act.drain().then_inc(S("lora_ready"), 1)
            act.wait_ge(S("par_ready"), 1)
            for n in range(0, 3 * KD, 2):
                kind, j = n // KD, n % KD
                act.wait_ge(S("lora_out"), n // 2 + 1)
                for half in range(2):
                    src = ps[:, n // 2 % 8, half * T:(half + 1) * T]
                    if kind == 2:
                        i = act.activation(gate[:, j + half, :], src, ACT.Copy)
                    else:
                        dst, col = ((dec, W0), (agate, A0))[kind]
                        i = act.activation(dst[:, j + half, :], src, ACT.Sigmoid,
                                           bias=par[:, 1, col + j + half:col + j + half + 1])
                i.then_inc(S("lora_taken"), 1)
            act.wait_ge(S("dt_abs"), 1)
            act.activation(dtp[:, 6], dtp[:, 6], ACT.Exp, scale=-1.0)
            act.activation(dtp[:, 7, 0, :], a_log[:], ACT.Exp)
            act.drain()
            act.activation(dtp[:, 6], dtp[:, 6], ACT.Ln, bias=ones[:, 0:1]).then_inc(S("dt_log"), 1)
            act.wait_ge(S("dst_ready"), 1)
            act.activation(dtp[:, 4], dtp[:, 4], ACT.Exp).then_inc(S("dst_exp"), 1)
            with act.Fori(0, SSD_GROUPS) as g:
                act.wait_ge(S("ssd_diff"), g + 1)
                act.activation(mm.rearrange("p a b c -> p (a b c)"), mm.rearrange("p a b c -> p (a b c)"), ACT.Exp)
                act.activation(cs.rearrange("p a b -> p (a b)"), ps[:, 4, :], ACT.Exp).then_inc(S("ssd_exp"), 1)
                act.wait_ge(S("ssd_var_eps"), g + 1)
                act.activation(sr, sr, ACT.Sqrt).then_inc(S("ssd_root"), 1)
            act.wait_ge(S("kk_len"), 1)
            for b in range(4):
                i = act.activation(tmp8[:, 2 * b:2 * b + 2, :].rearrange("p a t -> p (a t)"), ps[:, b, :], ACT.Sqrt)
            i.then_inc(S("kk_root"), 1)

            with act.Fori(0, KD) as j:
                act.wait_ge(S("cum_ready"), j + 1)
                for c in range(NT):
                    act.activation(e1[:, c, :], cum[:, c, :], ACT.Exp, scale=-DECAY_FACTOR, bias=edge[:, c:c + 1])
                    act.activation(e2[:, c, :], cum[:, c, 1:], ACT.Exp, scale=DECAY_FACTOR, bias=edge[:, 2 + c:3 + c])
                act.activation(edge[:, 5:6], edge[:, 4:5], ACT.Exp).then_inc(S("decay_exp"), 1)
                act.wait_ge(S("tok_turned"), j + 1)
                act.activation(vtok.rearrange("p a b -> p (a b)"), ps[:, 5, 0:2 * P], ACT.Copy)
                act.activation(ktok, ps[:, 5, 2 * P:3 * P], ACT.Copy)
                act.activation(btk, ps[:, 5, 3 * P:4 * P], ACT.Copy).then_inc(S("tok_ready"), 1)
                for n in range(6):
                    act.wait_ge(S("lx"), j * 6 + n + 1)
                    act.activation(TX.rearrange("p a b -> p (a b)"), ps[:, 7, :], ACT.Copy).then_inc(S("lx_taken"), 1)
                    act.wait_ge(S("x_back"), j * 6 + n + 1)
                    act.activation(XT.rearrange("p a b -> p (a b)"), ps[:, 7, :], ACT.Copy).then_inc(S("xt_taken"), 1)

            act.wait_ge(S("gn_centred"), 1)
            act.activation(tmp8.rearrange("p a t -> p (a t)"), mixT[:, KD:, :].rearrange("p a t -> p (a t)"),
                           ACT.Square).then_inc(S("gn_sq"), 1)
            act.wait_ge(S("gn_var"), 1)
            for b in range(4):
                i = act.activation(tmp8[:, 2 * b:2 * b + 2, :].rearrange("p a t -> p (a t)"), ps[:, 4 + b, :],
                                   ACT.Sqrt, bias=eps[:, 1:2])
            i.then_inc(S("gn_root"), 1)

            def moe(l):
                norm_squares(2 * l + 1)
                act.wait_ge(S("coarse_shifted"), l + 1)
                for t in range(NT):
                    act.activation(c8[:, t, 0:GROUPS], c8[:, t, 0:GROUPS], ACT.Exp, accum_out=sc[:, 0, t:t + 1])
                act.activation(sc[:, 1, :], sc[:, 1, :], ACT.Exp).then_inc(S("gates_exp"), 1)

                def item(n):
                    act.wait_ge(S(f"gu_used_l{l}"), n + NW + 1)
                    act.activation(gus[:, 0, :], ps[:, 4, :], ACT.Copy).then_inc(S(f"gate_copied_l{l}"), 1)
                    act.wait_ge(S(f"selg_turned_l{l}"), n + 1)
                    act.activation(gT.rearrange("p a b -> p (a b)"), ps[:, 6, 0:T],
                                   ACT.Copy).then_inc(S(f"gT_copied_l{l}"), 1)
                    act.wait_ge(S(f"folded_l{l}"), n + 1)
                    act.activation(sil.rearrange("p a b -> p (a b)"), ps[:, 7, T:T + P],
                                   ACT.Silu).then_inc(S(f"silu_l{l}"), 1)
                    act.wait_ge(S(f"dn_used_l{l}"), n + NW + 1)
                    act.activation(ys[:, 0:BANK], ps[:, 4, :], ACT.Copy).then_inc(S(f"y0_copied_l{l}"), 1)
                with act.Fori(0, EXPERTS // NW) as i:
                    for s in range(NW):
                        item(i * NW + s)
                act.wait_ge(S("lists_ready"), l + 1)
                extra = act.value_load(lists[0:1, l, EXTRA_MAX - 1:EXTRA_MAX], min_val=0, max_val=EXTRA_MAX - 1)
                with act.If(extra > 0):
                    with act.Fori(0, extra) as o:
                        item(o + EXPERTS)
            moe(0)

            norm_squares(2)
            for j in range(12):
                act.wait_ge(S("qkv_ready"), j + 1)
                act.activation(qkv[:, j, :], ps[:, j % 8, 0:T], ACT.Copy)
                if j < 10:
                    act.activation(sqs[:, j, :], ps[:, j % 8, 0:T], ACT.Square)
                act.drain().then_inc(S("qkv_taken"), 1)
            act.sem_inc(S("qk_sq"), 1)
            act.wait_ge(S("qk_ms"), 1)
            for b in range(5):
                i = act.activation(sqs[:, 2 * b:2 * b + 2, :].rearrange("p a t -> p (a t)"), ps[:, b, :], ACT.Sqrt,
                                   bias=eps[:, 0:1])
            i.then_inc(S("qk_root"), 1)
            with act.Fori(0, KV_HEADS) as g:
                for t in range(NT):
                    n_keys = P if t == 0 else 2 * P
                    act.wait_ge(S("shifted"), g * 2 + t + 1)
                    for hh in range(4):
                        act.activation(pr[:, hh, 0:n_keys], pr[:, hh, 0:n_keys], ACT.Exp, bias=st[:, 1, hh:hh + 1],
                                       accum_out=st[:, 2, hh:hh + 1])
                    act.activation(st[:, 3, :], st[:, 3, :], ACT.Exp).then_inc(S("exped"), 1)
                    act.wait_ge(S("probs_turned"), g * 2 + t + 1)
                    for kb in range(t + 1):
                        i = act.activation(pT[:, :, kb, :], ps[:, 4 + kb, :].rearrange("p (a b) -> p a b", b=P),
                                           ACT.Copy)
                    i.then_inc(S("pT_ready"), 1)
            moe(1)

        @block.vector
        def _(dve):
            tt, tsc, stt, cp = dve.tensor_tensor, dve.tensor_scalar, dve.scalar_tensor_tensor, dve.tensor_copy

            def normalise(n):
                dst = hn if n % 2 == 0 else hf
                dstT = hnT if n % 2 == 0 else hfT
                dve.wait_ge(S("rms_ready"), n + 1)
                dve.reciprocal(rstd[:], ss[:])
                dve.drain()
                for t in range(NT):
                    i = tsc(dst[:, t, :], h[:, t, :], rstd[:, t:t + 1], None, ALU.mult)
                i.then_inc(S("hn_ready"), 1)
                for b in range(4):
                    dve.wait_ge(S("hn_turned"), 4 * n + b + 1)
                    i = tt(dstT[:, 2 * b:2 * b + 2, :], ps[:, b, :].rearrange("p (k t) -> p k t", t=T),
                           bc(gains[:, n, 2 * b:2 * b + 2].unsqueeze(2), 2, T), ALU.mult)
                i.then_inc(S("hnT_ready"), 1)

            dve.wait_ge(S("consts_ready"), 1)
            dve.tensor_reduce(fold[:], ident[:].rearrange("p (q j) -> p j q", q=4), AX.X, ALU.add)
            dve.wait_ge(S("params_loaded"), 16 * PARAM_LOADS)
            normalise(0)
            dve.wait_ge(S("par_turned"), 1)
            cp(par[:, 0, 0:114], ps[:, 7, 0:114])
            cp(par[:, 1, 0:56], ps[:, 7, P:P + 56])
            dve.drain()
            tsc(par[:, 1, 64:64 + RWKV_TILES], par[:, 0, MU:MU + RWKV_TILES], -1.0, 1.0, ALU.mult, ALU.add)
            dve.drain().then_inc(S("par_ready"), 1)
            dve.wait_ge(S("dt_ready"), 1)
            tt(dtp[:, 0], ps[:, 6, 0:NT * SSD_HEADS].rearrange("p (c h) -> p c h", c=NT),
               bc(dt_bias[:].unsqueeze(1), NT, SSD_HEADS), ALU.add).then_inc(S("dt_taken"), 1)
            dve.drain()
            tsc(dtp[:, 6], dtp[:, 0], -1.0, None, ALU.mult)
            dve.drain()
            tt(dtp[:, 6], dtp[:, 0], dtp[:, 6], ALU.max).then_inc(S("dt_abs"), 1)
            dve.sem_inc(S("conv_done"), 8)

            with dve.Fori(0, CONV_CHUNKS // RING) as i:
                for b in range(TILES_PER_RING):
                    dve.wait_ge(S("projected"), i * TILES_PER_RING + 2 * Z_CHUNKS + b + 1)
                    dve.wait_ge(S("silu_done"), i * TILES_PER_RING + b + 1)
                    tile = i * TILES_PER_RING + b
                    buf = cbuf[:, b % 4, :]
                    tsc(buf, ps[:, b, 0:T], par[:, 0, bass.ds(tile + CW + 48, 1)], par[:, 0, bass.ds(tile + CB, 1)],
                        ALU.mult, ALU.add)
                    for s in range(1, CONV_TAPS):
                        dve.drain()
                        ins = stt(buf[:, s:], ps[:, b, 0:T - s], par[:, 0, bass.ds(tile + CW + 16 * (3 - s), 1)],
                                  buf[:, s:], ALU.mult, ALU.add)
                    ins.then_inc(S("conv_done"), 1)

            def token_shift(b, tile, ready):
                dve.wait_ge(S("projected"), ready + 2 * (Z_CHUNKS + CONV_CHUNKS))
                dst = u[:, bass.ds(tile, 1), :].rearrange("p a t -> p (a t)")
                tsc(dst, ps[:, b, 0:T], par[:, 1, bass.ds(tile + 64, 1)], None, ALU.mult)
                dve.drain()
                dst = u[:, bass.ds(tile, 1), 1:].rearrange("p a t -> p (a t)")
                stt(dst, ps[:, b, 0:T - 1], par[:, 0, bass.ds(tile + MU, 1)], dst, ALU.mult,
                    ALU.add).then_inc(S("conv_done"), 1)
            with dve.Fori(0, RWKV_CHUNKS // RING) as i:
                for b in range(TILES_PER_RING):
                    token_shift(b, i * TILES_PER_RING + b, i * TILES_PER_RING + b + 1)
            for b in range(2):
                token_shift(b, 24 + b, 24 + b + 1)

            dve.wait_ge(S("dt_log"), 1)
            tsc(dtp[:, 0], dtp[:, 0], 0.0, None, ALU.max)
            dve.drain()
            tt(dtp[:, 0], dtp[:, 0], dtp[:, 6], ALU.add)
            dve.drain()
            stt(dtp[:, 1], dtp[:, 0], -1.0, bc(dtp[:, 7, 0:1, :], NT, SSD_HEADS), ALU.mult,
                ALU.mult).then_inc(S("adt_ready"), 1)
            dve.wait_ge(S("acum_ready"), 1)
            cp(dtp[:, 2], ps[:, 0, 0:NT * SSD_HEADS].rearrange("p (c h) -> p c h", c=NT))
            dve.drain()
            tt(dtp[:, 4], ps[:, 1, 0:NT * SSD_HEADS].rearrange("p (c h) -> p c h", c=NT), dtp[:, 2],
               ALU.subtract).then_inc(S("acum_taken"), 1)
            dve.drain().then_inc(S("dst_ready"), 1)
            dve.wait_ge(S("dst_exp"), 1)
            dve.sem_inc(S("ssd_free"), 1)

            with dve.Fori(0, SSD_GROUPS) as g:
                def per_head(row, c):
                    return dtp[:, row, c, bass.ds(g * HPG, HPG)]
                for c in range(NT):
                    i = tt(tria[:, c], bc(upper[:].unsqueeze(1), HPG, P), bc(per_head(1, c).unsqueeze(2), HPG, P),
                           ALU.mult)
                i.then_inc(S("ssd_tria"), 1)
                dve.wait_ge(S("ssd_cb"), g + 1)
                for c in range(NT):
                    tt(xdt[:, c], ps[:, 0, c * 2 * P:(c + 1) * 2 * P].rearrange("p (h d) -> p h d", d=HD),
                       bc(per_head(0, c).unsqueeze(2), HPG, HD), ALU.mult)
                cp(btok, ps[:, 1, 0:P])
                tt(cbm, ps[:, 2, 0:T].rearrange("p (c t) -> p c t", c=NT), bc(upper[:].unsqueeze(1), NT, P), ALU.mult)
                dve.drain()
                tt(xst, xdt[:, 0], bc(per_head(4, 0).unsqueeze(2), HPG, HD), ALU.mult).then_inc(S("ssd_tok"), 1)
                dve.wait_ge(S("ssd_acum"), g + 1)
                for c in range(NT):
                    tt(mm[:, c], ps[:, 3 + c, :].rearrange("p (h t) -> p h t", t=P),
                       bc(per_head(2, c).unsqueeze(2), HPG, P), ALU.subtract)
                dve.drain()
                tsc(mm, mm, 0.0, None, ALU.min).then_inc(S("ssd_diff"), 1)
                dve.wait_ge(S("ssd_state"), g + 1)
                cp(state.rearrange("p a b -> p (a b)"), ps[:, 5, 0:HPG * HD])
                dve.wait_ge(S("ssd_exp"), g + 1)
                for c in range(NT):
                    tt(mm[:, c], mm[:, c], bc(cbm[:, c:c + 1, :], HPG, P), ALU.mult)
                tt(cs, cs, bc(sC[:, P:].unsqueeze(1), HPG, P), ALU.mult)
                dve.drain().then_inc(S("ssd_m"), 1)
                dve.wait_ge(S("ssd_y"), g + 1)
                for t in range(2):
                    stt(sy[:, t, :], sx[:, t, :], d_skip[:, bass.ds(g * 2 + t, 1)], ps[:, 6, t * T:(t + 1) * T],
                        ALU.mult, ALU.add)
                dve.drain()
                tt(sy, sy, zs[:, bass.ds(g * 2, 2), :], ALU.mult)
                dve.drain()
                tt(ssq, sy, sy, ALU.mult).then_inc(S("ssd_sq"), 1)
                dve.wait_ge(S("ssd_var"), g + 1)
                tsc(sr, ps[:, 7, 0:T], 1e-5, None, ALU.add).then_inc(S("ssd_var_eps"), 1)
                dve.wait_ge(S("ssd_root"), g + 1)
                dve.reciprocal(sr, sr)
                dve.drain()
                for t in range(2):
                    stt(mixT[:, bass.ds(g * 2 + t, 1), :].rearrange("p a t -> p (a t)"), sy[:, t, :],
                        par[:, 0, bass.ds(g * 2 + t + NW_, 1)], sr, ALU.mult, ALU.mult)
                dve.drain().then_inc(S("ssd_free"), 1)

            for j in range(KD):
                tsc(kk[:, j, :], kv_[:, j, :], par[:, 1, KK + j:KK + j + 1], None, ALU.mult)
            dve.drain()
            tt(tmp8, kk, kk, ALU.mult).then_inc(S("kk_sq"), 1)
            dve.memset(kar, 0.0)
            dve.memset(bar, 0.0)
            dve.memset(cum, 0.0)
            dve.wait_ge(S("kk_root"), 1)
            tsc(tmp8, tmp8, 1e-12, None, ALU.max)
            dve.drain()
            dve.reciprocal(tmp8, tmp8)
            dve.drain()
            tt(kk, kk, tmp8, ALU.mult)
            dve.drain().then_inc(S("x_free"), 1)

            with dve.Fori(0, KD) as j:
                def tile(x, lo=None, hi=None):
                    return x[:, bass.ds(j, 1), slice(lo, hi)].rearrange("p a t -> p (a t)")

                def col(c):
                    return par[:, 1, bass.ds(j + c, 1)]
                tsc(kp, tile(agate), -1.0, col(KA), ALU.add, ALU.mult)
                for c in range(NT):
                    dve.tensor_tensor_scan(cum[:, c, 1:], ones[:], tile(dec, c * P, (c + 1) * P), 0.0, ALU.mult,
                                           ALU.add)
                dve.drain()
                stt(kp, kp, 1.0, tile(kv_), ALU.add, ALU.mult)
                for c in range(NT):
                    tsc(edge[:, c:c + 1], cum[:, c, HD:HD + 1], DECAY_FACTOR, None, ALU.mult)
                    tsc(edge[:, 2 + c:3 + c], cum[:, c, HD:HD + 1], -DECAY_FACTOR, None, ALU.mult)
                tt(edge[:, 4:5], cum[:, 0, HD:HD + 1], cum[:, 0, P:P + 1], ALU.subtract)
                dve.drain()
                stt(edge[:, 4:5], cum[:, 1, HD:HD + 1], -1.0, edge[:, 4:5], ALU.mult, ALU.add)
                dve.drain()
                tsc(edge[:, 4:5], edge[:, 4:5], DECAY_FACTOR, None, ALU.mult).then_inc(S("cum_ready"), 1)
                stt(tmp, tile(rv), col(RK), kp, ALU.mult, ALU.mult).then_inc(S("rk_ready"), 1)
                dve.wait_ge(S("decay_exp"), j + 1)
                for c in range(NT):
                    t0, t1 = c * P, (c + 1) * P
                    stt(ar[:, c, 0, :], tile(kk, t0, t1), -1.0, e1[:, c, 0:P], ALU.mult, ALU.mult)
                    tt(ar[:, c, 1, :], tile(rv, t0, t1), e1[:, c, 1:], ALU.mult)
                    tt(kt[:, c, :], kp[:, t0:t1], e2[:, c, :], ALU.mult)
                    tt(bt[:, c, :], tile(agate, t0, t1), e2[:, c, :], ALU.mult)
                cp(vst, tile(vv))
                dve.drain()
                tt(bt, bt, kk[:, bass.ds(j, 1), :].rearrange("p a (c t) -> p (a c) t", c=NT),
                   ALU.mult).then_inc(S("decayed"), 1)
                dve.wait_ge(S("rk_sum"), j + 1)
                tt(tile(bonus), ps[:, 4, 0:T], vst, ALU.mult)
                dve.wait_ge(S("scores"), j + 1)
                dve.sem_inc(S("dve_waited"), 1)
                for n, dst in enumerate((kar, bar)):
                    for hh in range(2):
                        dve.copy_predicated(dst[:, hh], mask_ar[:].bitcast(I32),
                                            ps[:, 2 * n + hh, :].rearrange("p (c a t) -> p c a t", c=NT, a=2))
                dve.drain()
                dve.wait_ge(S("x_reset"), j + 1)
                dve.sem_inc(S("dve_waited"), 1)
                for hh in range(2):
                    dve.copy_predicated(XT.rearrange("p (c h) t -> p h c t", h=2)[:, hh],
                                        bc(mask_pair[:].bitcast(I32).unsqueeze(1), NT, P), bar[:, hh, :, 0, :])
                dve.drain().then_inc(S("xt_pairs"), 1)
                dve.wait_ge(S("x_turned"), j + 1)
                cp(X.rearrange("p a b -> p (a b)"), ps[:, 6, :]).then_inc(S("x_level"), 1)
                for n in range(6):
                    dve.wait_ge(S("xlx"), j * 6 + n + 1)
                    dve.sem_inc(S("dve_waited"), 1)
                    dve.copy_predicated(X, bc(mask_level[:, n:n + 1, :].bitcast(I32), 4, P),
                                        ps[:, 6, :].rearrange("p (m t) -> p m t", m=4)).then_inc(S("x_level"), 1)
                for c in range(NT):
                    dve.wait_ge(S("rhs_out"), j * 2 + c + 1)
                    cp(rhs[:, :, c, :], ps[:, 0:2, 0:HD]).then_inc(S("rhs_ready"), 1)
                    dve.wait_ge(S("u_out"), j * 2 + c + 1)
                    cp(us[:, :, c, :], ps[:, 2:4, 0:HD]).then_inc(S("u_ready"), 1)
                    if c == 0:
                        dve.wait_ge(S("s0_out"), j + 1)
                        tsc(s0T, ps[:, 4, 0:HD], edge[:, 5:6], None, ALU.mult).then_inc(S("s0_ready"), 1)
                dve.wait_ge(S("y_out"), j + 1)
                cp(mixT[:, bass.ds(j + KD, 1), :].rearrange("p a t -> p (a t)"),
                   ps[:, 5, 0:T]).then_inc(S("y_taken"), 1)
                dve.drain().then_inc(S("x_free"), 1)

            my = mixT[:, KD:, :]
            dve.wait_ge(S("gn_mean"), 1)
            for b in range(4):
                v = my[:, 2 * b:2 * b + 2, :]
                tt(v, v, ps[:, b, :].rearrange("p (a t) -> p a t", a=2), ALU.subtract)
            dve.drain().then_inc(S("gn_centred"), 1)
            dve.wait_ge(S("gn_root"), 1)
            dve.reciprocal(tmp8, tmp8)
            dve.drain()
            tt(my, my, tmp8, ALU.mult)
            dve.drain()
            for j in range(KD):
                tsc(my[:, j, :], my[:, j, :], par[:, 1, LNW + j:LNW + j + 1], par[:, 1, LNB + j:LNB + j + 1], ALU.mult,
                    ALU.add)
            dve.drain()
            tt(my, my, bonus, ALU.add)
            dve.drain()
            tt(my, my, gate, ALU.mult).then_inc(S("mixed"), 1)

            def residual(used, n):
                dve.wait_ge(used, n)
                for t in range(NT):
                    tt(h[:, t, :].rearrange("p (a b) -> p a b", a=2), h[:, t, :].rearrange("p (a b) -> p a b", a=2),
                       ps[:, 2 * t:2 * t + 2, :], ALU.add)
                return dve.drain()
            residual(S("wo0_used"), 2 * KD).then_inc(S("h_mixed"), 1)

            def moe(l):
                dve.wait_ge(S("rms_ready"), 2 * l + 2)
                dve.memset(c8, -1.0e30)
                dve.memset(ys, 0.0)
                dve.memset(gT, 0.0)
                dve.memset(zero, 0.0)
                normalise(2 * l + 1)
                dve.wait_ge(S("logits"), l + 1)
                tt(lg, ps[:, 4, 0:NT * 64].rearrange("p (t e) -> p t e", t=NT)[:, :, 0:GROUPS + EXPERTS],
                   bc(router_b[:, l:l + 1, :], NT, GROUPS + EXPERTS), ALU.add)
                dve.drain()
                cp(c8[:, :, 0:GROUPS], lg[:, :, 0:GROUPS])
                dve.drain()
                for t in range(NT):
                    dve.max(mx[:, t, :], c8[:, t, :])
                dve.drain()
                for t in range(NT):
                    dve.max_index(idx[:, 0, t, :], mx[:, t, :], c8[:, t, :])
                dve.drain()
                cp(sc[:, 2, :], idx[:, 0, :, 0])
                tt(c8[:, :, 0:GROUPS], c8[:, :, 0:GROUPS], bc(mx[:, :, 0:1], NT, GROUPS), ALU.subtract)
                dve.drain()
                for t in range(NT):
                    stt(fine[:, t], bc(iota[:, 0:1, 0:GROUPS], PER_GROUP, GROUPS), sc[:, 2, t:t + 1],
                        lg[:, t, GROUPS:].rearrange("p (g e) -> p e g", g=GROUPS), ALU.is_equal, ALU.mult)
                dve.drain()
                dve.tensor_reduce(fsel, fine, AX.X, ALU.add)
                dve.drain()
                for t in range(NT):
                    dve.max(fmx[:, t, :], fsel[:, t, :])
                dve.drain()
                for t in range(NT):
                    dve.max_index(idx[:, 1, t, :], fmx[:, t, :], fsel[:, t, :])
                tt(sc[:, 1, :], fmx[:, :, 1], fmx[:, :, 0], ALU.subtract)
                dve.drain().then_inc(S("coarse_shifted"), 1)
                cp(sc[:, 4, :], idx[:, 1, :, 0])
                cp(sc[:, 5, :], idx[:, 1, :, 1])
                dve.drain()
                for r in (4, 5):
                    stt(sc[:, r, :], sc[:, 2, :], float(PER_GROUP), sc[:, r, :], ALU.mult, ALU.add)
                dve.drain()
                for r in range(2):
                    for t in range(NT):
                        tsc(pick[:, 2 * r + t, :], iota[:, 0, :], sc[:, 4 + r, t:t + 1], None, ALU.is_equal)
                dve.drain()
                tt(both, pick[:, 0:2, :], pick[:, 2:4, :], ALU.add).then_inc(S("picked"), 1)
                dve.wait_ge(S("gates_exp"), l + 1)
                tsc(sc[:, 6, :], sc[:, 1, :], 1.0, None, ALU.add)
                dve.drain()
                tt(sc[:, 6, :], sc[:, 6, :], sc[:, 0, :], ALU.mult)
                dve.drain()
                dve.reciprocal(sc[:, 7, :], sc[:, 6, :])
                dve.drain()
                tt(sc[:, 8, :], sc[:, 7, :], sc[:, 1, :], ALU.mult)
                dve.wait_ge(S("ranked"), l + 1)
                cp(rank, ps[:, 5, 0:2 * EXPERTS].rearrange("p (t e) -> p t e", t=NT))
                cp(cnt[:, 0, :], ps[:, 5, 2 * EXPERTS:3 * EXPERTS])
                dve.drain()
                tsc(cnt[:, 1, :], cnt[:, 0, :], float(SLOTS), None, ALU.is_gt)
                for k in range(2, T // SLOTS):
                    dve.drain()
                    stt(cnt[:, 1, :], cnt[:, 0, :], float(SLOTS * k), cnt[:, 1, :], ALU.is_gt, ALU.add)
                dve.drain()
                dve.tensor_tensor_scan(cnt[:, 2, :], ones[:, 0:EXPERTS], cnt[:, 1, :], 0.0, ALU.mult, ALU.add)
                dve.drain()
                tt(cnt[:, 3, :], cnt[:, 2, :], cnt[:, 1, :], ALU.subtract)
                tt(prod.rearrange("p (r t) e -> p r t e", r=2), pick.rearrange("p (r t) e -> p r t e", r=2),
                   bc(rank.unsqueeze(1), 2, NT, EXPERTS), ALU.mult)
                dve.drain()
                dve.tensor_reduce(slot[:, 0, :], prod, AX.X, ALU.add)
                dve.drain()
                tt(prod, pick, bc(cnt[:, 3:4, :], 4, EXPERTS), ALU.mult)
                tsc(slot[:, 2, :], slot[:, 0, :], float(SLOTS), None, ALU.is_ge)
                dve.drain()
                dve.tensor_reduce(slot[:, 1, :], prod, AX.X, ALU.add)
                for k in range(2, T // SLOTS):
                    stt(slot[:, 2, :], slot[:, 0, :], float(SLOTS * k), slot[:, 2, :], ALU.is_ge, ALU.add)
                    dve.drain()
                cp(slot[:, 3, :].rearrange("p (r t) -> p r t", r=2), sc[:, 4:6, :])
                tsc(slot[:, 4, :], slot[:, 2, :], 1.0, None, ALU.min)
                stt(slot[:, 5, :], slot[:, 1, :], float(EXPERTS - 1), slot[:, 2, :], ALU.add, ALU.add)
                stt(slot[:, 6, :], slot[:, 2, :], -float(SLOTS), slot[:, 0, :], ALU.mult, ALU.add)
                dve.drain()
                tt(slot[:, 5, :], slot[:, 5, :], slot[:, 3, :], ALU.subtract)
                dve.drain()
                tt(slot[:, 5, :], slot[:, 5, :], slot[:, 4, :], ALU.mult)
                dve.drain()
                tt(slot[:, 5, :], slot[:, 5, :], slot[:, 3, :], ALU.add)
                dve.drain()
                stt(slot[:, 7, :], slot[:, 5, :], float(SLOTS), slot[:, 6, :], ALU.mult, ALU.add)
                tt(lst[0:1], bc(cnt[0:1, 2:3, :], EXTRA_MAX, EXPERTS),
                   bc(iota[0:1, 0, 0:EXTRA_MAX].unsqueeze(2), EXTRA_MAX, EXPERTS), ALU.is_le)
                dve.drain()
                dve.tensor_reduce(lsti[0:1, 0, :], lst[0:1], AX.X, ALU.add)
                dve.drain()
                cp(lsti[0:1, 0, EXTRA_MAX - 1:EXTRA_MAX], cnt[0:1, 2, EXPERTS - 1:EXPERTS])
                dve.drain()
                cp(lists[0:1, l, :], lsti[0:1, 0, :])
                dve.drain().then_inc(S("lists_ready"), 1)

                def select(n):
                    for t in range(NT):
                        tsc(sel[:, t, :], iota[:, 0, :], slot[:, 7, t:t + 1], None, ALU.is_equal)
                    dve.drain()
                    for t in range(NT):
                        i = stt(sel[:, t, :], iota[:, 0, :], slot[:, 7, 2 + t:3 + t], sel[:, t, :], ALU.is_equal,
                                ALU.add)
                    i.then_inc(S(f"sel_ready_l{l}"), 1)

                def select_gated():
                    for t in range(NT):
                        tsc(selg[:, t, :], iota[:].rearrange("p a b -> p (a b)"), slot[:, 7, t:t + 1],
                            sc[:, 7, t:t + 1], ALU.is_equal, ALU.mult)
                        tsc(selt[:, t, :], iota[:].rearrange("p a b -> p (a b)"), slot[:, 7, 2 + t:3 + t],
                            sc[:, 8, t:t + 1], ALU.is_equal, ALU.mult)
                    dve.drain()
                    tt(selg, selg, selt, ALU.add).then_inc(S(f"selg_ready_l{l}"), 1)
                    tsc(slot[:, 7, :], slot[:, 7, :], -float(SLOTS), None, ALU.add)
                    dve.drain()

                def gathered(n):
                    dve.wait_ge(S(f"gathered_l{l}"), n)
                    tt(xg, ps[:, 6, 0:KD * SLOTS].rearrange("p (k s) -> p k s", k=KD),
                       bc(gains[:, 2 * l + 1, :].unsqueeze(2), KD, SLOTS), ALU.mult).then_inc(S(f"xg_ready_l{l}"), 1)
                select(0)
                gathered(1)

                def item(n):
                    dve.wait_ge(S(f"gu_used_l{l}"), n + NW + 1)
                    cp(gus[:, 1, :], ps[:, 5, :]).then_inc(S(f"up_copied_l{l}"), 1)
                    select_gated()
                    select(n)
                    dve.wait_ge(S(f"silu_l{l}"), n + 1)
                    tt(hidT.rearrange("p a b -> p (a b)"), sil.rearrange("p a b -> p (a b)"),
                       ps[:, 7, T + P:T + 2 * P], ALU.mult).then_inc(S(f"hid_ready_l{l}"), 1)
                    gathered(n + 2)
                    dve.wait_ge(S(f"dn_used_l{l}"), n + NW + 1)
                    cp(ys[:, BANK:], ps[:, 5, :]).then_inc(S(f"y1_copied_l{l}"), 1)
                with dve.Fori(0, EXPERTS // NW) as i:
                    for s in range(NW):
                        item(i * NW + s)
                extra = dve.value_load(lists[0:1, l, EXTRA_MAX - 1:EXTRA_MAX], min_val=0, max_val=EXTRA_MAX - 1)
                with dve.If(extra > 0):
                    with dve.Fori(0, extra) as o:
                        item(o + EXPERTS)
                residual(S("moe_summed"), l + 1).then_inc(S("moe_added"), 1)
            moe(0)

            normalise(2)
            dve.wait_ge(S("qk_root"), 1)
            for n, (lo, hi, scale) in enumerate(((0, 8, HD ** -0.5), (8, 10, 1.0))):
                dve.reciprocal(sqs[:, lo:hi, :], sqs[:, lo:hi, :])
                dve.drain()
                tsc(qkv[:, lo:hi, :], qkv[:, lo:hi, :], qk_gain[:, n:n + 1], scale, ALU.mult, ALU.mult)
                dve.drain()
                tt(qkv[:, lo:hi, :], qkv[:, lo:hi, :], sqs[:, lo:hi, :], ALU.mult)
            dve.drain().then_inc(S("qk_normed"), 1)
            dve.wait_ge(S("kv_out"), 1)
            for b in range(2):
                cp(kdup[:, 2 * b:2 * b + 2, :].rearrange("p a t -> p (a t)"), ps[:, b, :])
            cp(vtk.rearrange("p t a b -> p (t a b)"), ps[:, 2, :])
            dve.drain().then_inc(S("att_inputs"), 1)
            dve.sem_inc(S("att_free"), 1)
            slopes = st[:, 4, :]
            for hh in range(4):
                dve.memset(st[:, 4, hh:hh + 1], 2.0 ** (-8.0 * (hh + 1) / ATT_HEADS))
            dve.drain()
            with dve.Fori(0, KV_HEADS) as g:
                for t in range(NT):
                    n_keys = P if t == 0 else 2 * P
                    p_ = pr[:, :, 0:n_keys]
                    dve.wait_ge(S("qk_out"), g * 2 + t + 1)
                    for hh in range(4):
                        stt(pr[:, hh, 0:n_keys], band[:, 2 * P - n_keys:], slopes[:, hh:hh + 1], ps[:, hh, 0:n_keys],
                            ALU.mult, ALU.add)
                    dve.drain()
                    dve.tensor_reduce(st[:, 0, :], p_, AX.X, ALU.max)
                    dve.drain()
                    tt(st[:, 0, :], st[:, 0, :], sinks[:, bass.ds(g * 4, 4)], ALU.max)
                    dve.drain()
                    tsc(st[:, 1, :], st[:, 0, :], -1.0, None, ALU.mult)
                    tt(st[:, 3, :], sinks[:, bass.ds(g * 4, 4)], st[:, 0, :], ALU.subtract)
                    dve.drain().then_inc(S("shifted"), 1)
                    dve.wait_ge(S("exped"), g * 2 + t + 1)
                    tt(st[:, 2, :], st[:, 2, :], st[:, 3, :], ALU.add)
                    dve.drain()
                    dve.reciprocal(st[:, 2, :], st[:, 2, :])
                    dve.drain()
                    tt(p_, p_, bc(st[:, 2, :].unsqueeze(2), 4, n_keys), ALU.mult).then_inc(S("probs"), 1)
                    dve.wait_ge(S("att_out"), g * 2 + t + 1)
                    cp(attT[:, bass.ds(g * 2, 2), t * P:(t + 1) * P],
                       ps[:, 6, 0:2 * P].rearrange("p (a b) -> p a b", a=2)).then_inc(S("att_taken"), 1)
                tsc(slopes, slopes, 0.25, None, ALU.mult)
                dve.drain().then_inc(S("att_free"), 1)
            residual(S("wo1_used"), KD).then_inc(S("h_mixed"), 1)
            moe(1)


PARAM_LOADS = 42


def kernel(**inputs):
    import numpy as np
    import concourse.bacc as bacc
    from concourse.bass_utils import run_bass_kernel_spmd

    nc = bacc.Bacc("TRN2", target_bir_lowering=False, num_devices=1)
    arrays, args = {}, {}
    for name, value in inputs.items():
        array = np.ascontiguousarray(value)
        arrays[f"in_{name}"] = array
        args[name] = nc.dram_tensor(f"in_{name}", array.shape, mybir.dt.from_np(array.dtype), kind="ExternalInput").ap()
    out = nc.dram_tensor("out_h", inputs["x"].shape, F32, kind="ExternalOutput").ap()
    trunk(nc, args, out)
    result = run_bass_kernel_spmd(nc, [arrays], core_ids=[0])
    return result.results[0]["out_h"]
```

```python
from contextlib import ExitStack

import concourse.bass as bass
from concourse import mybir

P = 128
F32 = mybir.dt.float32
I32 = mybir.dt.int32
U32 = mybir.dt.uint32
ALU = mybir.AluOpType
ACT = mybir.ActivationFunctionType
AX = mybir.AxisListType

D = 1024
T = 256
NT = T // P
KD = D // P
BANK = 512
NORM_EPS = 1e-6

SSD_INNER = 1024
SSD_STATE = 128
SSD_GROUPS = 4
SSD_HEADS = 16
HPG = SSD_HEADS // SSD_GROUPS
CONV_DIM = SSD_INNER + 2 * SSD_GROUPS * SSD_STATE
CONV_TAPS = 4
RWKV_DIM = 1024
RWKV_TILES = 26
HD = 64
GN_EPS = 64e-5
DECAY_FACTOR = 0.6065306597126334

ATT_HEADS = 16
KV_HEADS = 4
WINDOW = 128
OUT_OF_BAND = -1.0e30

EXPERTS = 32
GROUPS = 4
PER_GROUP = 8
HIDDEN = 512
KH = HIDDEN // P
SLOTS = 32
EXTRA_MAX = 16
NW = 2

COLS = 256
RING = 4
Z_CHUNKS = SSD_INNER // COLS
CONV_CHUNKS = CONV_DIM // COLS
RWKV_CHUNKS = RWKV_TILES * P // COLS
DT_COL = SSD_INNER + CONV_DIM
RWKV_COL = DT_COL + SSD_HEADS
ODD_CHUNKS = 6
TILES_PER_RING = RING * COLS // P


class Arena:

    def __init__(self, tensor, size, start=0):
        self.tensor, self.size, self.at = tensor, size, start

    def take(self, *dims):
        n = 1
        for d in dims:
            n *= d
        view = self.tensor[:, self.at:self.at + n]
        self.at += n
        assert self.at <= self.size, self.at
        if len(dims) == 2:
            view = view.rearrange("p (a b) -> p a b", b=dims[1])
        elif len(dims) == 3:
            view = view.rearrange("p (a b c) -> p a b c", b=dims[1], c=dims[2])
        elif len(dims) == 4:
            view = view.rearrange("p (a b c d) -> p a b c d", b=dims[1], c=dims[2], d=dims[3])
        return view


def bc(ap, *shape):
    return ap.to_broadcast([ap.shape[0], *shape])


def trunk(nc, a, out, stop_after=99):
    with ExitStack() as ctx:
        def sb(name, shape, dt=F32):
            return ctx.enter_context(nc.sbuf_tensor(name, shape, dt))

        sems = {}

        def S(name):
            if name not in sems:
                sems[name] = ctx.enter_context(nc.semaphore(name))
            return sems[name]

        h = sb("h", [P, NT, D])
        ident = sb("ident", [P, P])
        head_sum = sb("head_sum", [P, P])
        head_mean = sb("head_mean", [P, P])
        ones = sb("ones", [P, P])
        group_mean = sb("group_mean", [P, P])
        upper = sb("upper", [P, P])
        upper_strict = sb("upper_strict", [P, P])
        fold = sb("fold", [P, SLOTS])
        dup_even = sb("dup_even", [P, P])
        dup_odd = sb("dup_odd", [P, P])
        iota = sb("iota", [P, 4, SLOTS])
        mask_ar = sb("mask_ar", [P, NT, 2, P])
        mask_level = sb("mask_level", [P, 6, P])
        mask_level_t = sb("mask_level_t", [P, 6, P])
        mask_pair = sb("mask_pair", [P, P])
        band = sb("band", [P, 2 * P])
        par = sb("par", [P, 2, P])
        gains = sb("gains", [P, 4, KD])
        router_w = sb("router_w", [P, 2, KD, GROUPS + EXPERTS])
        router_b = sb("router_b", [P, 2, GROUPS + EXPERTS])
        dt_bias = sb("dt_bias", [P, SSD_HEADS])
        a_log = sb("a_log", [P, SSD_HEADS])
        d_skip = sb("d_skip", [P, KD])
        sinks = sb("sinks", [P, ATT_HEADS])
        qk_gain = sb("qk_gain", [P, 2])
        eps = sb("eps", [P, 2])
        ss = sb("ss", [P, NT])
        rstd = sb("rstd", [P, NT])
        lists = sb("lists", [1, 2, EXTRA_MAX], I32)

        ARENA = 44600
        arena = sb("arena", [P, ARENA])
        ps = ctx.enter_context(nc.psum_tensor("ps", [P, 8, BANK], F32))

        m0 = Arena(arena, ARENA)
        hnT = m0.take(KD, T)
        ring = m0.take(RING, KD, COLS)
        zs = m0.take(KD, T)
        xbc = m0.take(CONV_DIM // P, T)
        u = m0.take(RWKV_TILES, T)
        dec = m0.take(KD, T)
        agate = m0.take(KD, T)
        gate = m0.take(KD, T)
        mixT = m0.take(2 * KD, T)
        work = m0.at
        hn = Arena(arena, ARENA, work).take(NT, D)
        wdt = Arena(arena, ARENA, work + NT * D).take(KD, SSD_HEADS)
        lora_w = Arena(arena, ARENA, work + NT * D + P).take(3, D)
        rows = Arena(arena, ARENA, work + NT * D + P + 3 * D).take(2, P)
        cbuf = Arena(arena, ARENA, work + NT * D + P + 3 * D + 2 * P).take(4, T)
        dtp = sb("dtp", [P, 8, NT, SSD_HEADS])
        CW, CB, NW_, MU = 0, 64, 80, 88
        W0, A0, KK, KA, RK, LNW, LNB = (8 * i for i in range(7))

        s0 = Arena(arena, ARENA, work)
        sx = s0.take(2, T)
        sB = s0.take(T)
        sC = s0.take(T)
        btok = s0.take(P)
        xdt = s0.take(NT, HPG, HD)
        xst = s0.take(HPG, HD)
        tria = s0.take(NT, HPG, P)
        mm = s0.take(NT, HPG, P)
        cbm = s0.take(NT, P)
        cs = s0.take(HPG, P)
        state = s0.take(HPG, HD)
        sy = s0.take(2, T)
        ssq = s0.take(2, T)
        sr = s0.take(T)

        rh = Arena(arena, KD * T)
        ra = Arena(arena, KD * T + RING * KD * COLS, KD * T)
        rb = Arena(arena, ARENA, work)
        kar = [rb.take(2, NT, 2, P) for _ in range(2)]
        bar = [rb.take(2, NT, 2, P) for _ in range(2)]
        X = [rb.take(NT * 2, P) for _ in range(2)]
        XT = [rb.take(NT * 2, P) for _ in range(2)]
        TX = [rb.take(NT * 2, P) for _ in range(2)]
        vtok = [rb.take(NT, P) for _ in range(2)]
        ktok = [rb.take(P) for _ in range(2)]
        btk = [rb.take(P) for _ in range(2)]
        ar = [x.take(NT, 2, P) for x in (rh, rh, ra, ra)]
        kt = [x.take(NT, P) for x in (rh, rh, ra, ra)]
        bt = [x.take(NT, P) for x in (rh, rh, ra, ra)]
        edge = [rb.take(8) for _ in range(4)]
        cum = [rb.take(NT, P + 1) for _ in range(2)]
        e1 = [rb.take(NT, P + 1) for _ in range(2)]
        e2 = [rb.take(NT, P) for _ in range(2)]
        kp = [rb.take(T) for _ in range(2)]
        tmp = [rb.take(T) for _ in range(2)]
        rhs = [ra.take(2, NT, HD) for _ in range(2)]
        us = [ra.take(2, NT, HD) for _ in range(2)]
        s0T = [ra.take(HD) for _ in range(2)]
        kk = zs
        bonus = Arena(arena, ARENA, KD * T * 2 + RING * KD * COLS).take(KD, T)
        tmp8 = Arena(arena, ARENA, KD * T * 3 + RING * KD * COLS).take(KD, T)
        rv = u[:, 0:KD, :]
        kv_ = u[:, KD:2 * KD, :]
        vv = u[:, 2 * KD:3 * KD, :]
        wo_ring = ring.rearrange("p a b c -> p (a b c)").rearrange("p (a c) -> p a c", c=D)
        WO = RING * KD * COLS // D

        mo = Arena(arena, ARENA)
        wgu = mo.take(NW, 2, KD, HIDDEN)
        wdn = mo.take(NW, KH, D)
        hf = mo.take(NT, D)
        hfT = mo.take(KD, T)
        gus = mo.take(2, HIDDEN)
        ys = mo.take(D)
        zero = mo.take(BANK)
        xg = mo.take(KD, SLOTS)
        hidT = mo.take(KH, SLOTS)
        sil = mo.take(KH, SLOTS)
        sel = mo.take(NT, SLOTS)
        selg = mo.take(NT, P)
        selt = mo.take(NT, P)
        gT = mo.take(NT, P)
        lg = mo.take(NT, GROUPS + EXPERTS)
        c8 = mo.take(NT, 8)
        mx = mo.take(NT, 8)
        fine = mo.take(NT, PER_GROUP, GROUPS)
        fsel = mo.take(NT, 8)
        fmx = mo.take(NT, 8)
        sc = mo.take(16, NT)
        pick = mo.take(4, EXPERTS)
        both = mo.take(NT, EXPERTS)
        rank = mo.take(NT, EXPERTS)
        cnt = mo.take(6, EXPERTS)
        prod = mo.take(4, EXPERTS)
        slot = mo.take(12, 4)
        lst = mo.take(EXTRA_MAX, EXPERTS)
        lsti = mo.take(2, EXTRA_MAX)
        idx = sb("idx", [P, 2, NT, 8], U32)

        m1 = Arena(arena, ARENA)
        m1.take(KD, T)
        m1.take(RING, KD, COLS)
        qkv = m1.take(12, T)
        sqs = m1.take(12, T)
        kdup = m1.take(KV_HEADS, T)
        vtk = m1.take(NT, 2, P)
        attT = m1.take(KD, T)
        qs = m1.take(2, T)
        pr = m1.take(4, 2 * P)
        pT = m1.take(4, 2, P)
        vs = m1.take(NT, HD)
        ks = m1.take(T)
        st = m1.take(8, 4)

        block = ctx.enter_context(nc.Block())

        @block.sync
        def _(sp):
            sp.dma_start(h[:], a["x"].rearrange("b (t p) d -> p (b t) d", p=P)).then_inc(S("x_loaded"), 16)
            n = 0

            def small(dst, src):
                nonlocal n
                sp.dma_start(dst, src, allow_slow_non_contiguous=True).then_inc(S("params_loaded"), 16)
                n += 1
            row = lambda ap: ap.rearrange("(r f) -> r f", f=P)
            small(rows[0:64, 0, :], a["ssd_conv_w"][0].rearrange("t (j f) -> (t j) f", f=P))
            small(rows[64:80, 0, :], row(a["ssd_conv_b"][0]))
            small(rows[80:88, 0, :], row(a["ssd_norm"][0]))
            small(rows[88:114, 0, :], row(a["rwkv_mu"][0]))
            for i, name in enumerate(("rwkv_w0", "rwkv_a0", "rwkv_k_k", "rwkv_k_a")):
                small(rows[8 * i:8 * i + 8, 1, :], row(a[name][0]))
            small(rows[32:40, 1, :], a["rwkv_r_k"][0].rearrange("(r b) f -> r (b f)", b=2))
            small(rows[40:48, 1, :], row(a["rwkv_ln_w"][0]))
            small(rows[48:56, 1, :], row(a["rwkv_ln_b"][0]))
            for i, (name, l) in enumerate((("ln_mix", 0), ("ln_ffn", 0), ("ln_mix", 1), ("ln_ffn", 1))):
                small(gains[:, i, :], a[name][l].rearrange("(p k) -> p k", k=KD))
            for l in range(2):
                small(router_w[:, l, :, 0:GROUPS], a["moe_w_coarse"][l].rearrange("(p k) e -> p k e", k=KD))
                for g in range(GROUPS):
                    small(router_w[:, l, :, GROUPS + 8 * g:GROUPS + 8 * g + 8],
                          a["moe_w_fine"][l, g].rearrange("(p k) e -> p k e", k=KD))
                small(router_b[:, l, 0:GROUPS], a["moe_b_coarse"][l].partition_broadcast(P))
                small(router_b[:, l, GROUPS:], a["moe_b_fine"][l].rearrange("g e -> (g e)").partition_broadcast(P))
            small(dt_bias[:], a["ssd_dt_bias"][0].partition_broadcast(P))
            small(a_log[:], a["ssd_a_log"][0].partition_broadcast(P))
            small(sinks[:], a["attn_sinks"][0].partition_broadcast(P))
            for half in range(2):
                small(d_skip[64 * half:64 * half + 64, :],
                      a["ssd_d"][0].rearrange("(j e) -> e j", e=2)[half].partition_broadcast(64))
                small(qk_gain[64 * half:64 * half + 64, 0:1], a["attn_q_norm"][0].rearrange("(p k) -> p k", k=1))
                small(qk_gain[64 * half:64 * half + 64, 1:2], a["attn_k_norm"][0].rearrange("(p k) -> p k", k=1))
            small(wdt, a["e_w_in"][0].rearrange("(p k) c -> p k c", k=KD)[:, :, DT_COL:RWKV_COL])
            small(lora_w[0:64, 0, :], a["rwkv_w2"][0])
            small(lora_w[64:128, 1, :], a["rwkv_a2"][0])
            small(lora_w[:, 2, :], a["rwkv_g2"][0])
            assert n == PARAM_LOADS, n

            w_in = a["e_w_in"][0].rearrange("(p k) c -> p k c", k=KD)

            def chunk(s, col):
                sp.dma_start(ring[:, s], w_in[:, :, bass.ds(col, COLS)]).then_inc(S(f"ring_loaded{s}"), 16)
            for s in range(Z_CHUNKS):
                chunk(s, s * COLS)
            with sp.Fori(0, CONV_CHUNKS // RING) as i:
                for s in range(RING):
                    sp.wait_ge(S("projected"), 2 * (i * RING + s) + 2)
                    chunk(s, (i * RING + Z_CHUNKS + s) * COLS)
            with sp.Fori(0, RWKV_CHUNKS // RING) as i:
                for s in range(RING):
                    sp.wait_ge(S("projected"), 2 * (i * RING + CONV_CHUNKS + s) + 2)
                    chunk(s, (i * RING + s) * COLS + RWKV_COL)
            sp.wait_ge(S("projected"), 2 * (CONV_CHUNKS + 3 * RING) + 2)
            chunk(0, 3 * RING * COLS + RWKV_COL)

            def out_weights(w, first):
                for half in range(2):
                    j = first + half * WO // 2
                    sp.dma_start(wo_ring[:, half * WO // 2:(half + 1) * WO // 2, :],
                                 w.rearrange("(j p) d -> p j d", p=P)[:, j:j + WO // 2]).then_inc(
                        S(f"wo_loaded{half}"), 16)
            sp.wait_ge(S("projected"), 2 * (Z_CHUNKS + CONV_CHUNKS + RWKV_CHUNKS))
            out_weights(a["e_w_out"][0], 0)
            for w in range(2):
                sp.wait_ge(S(f"solved{w}"), KD // 2 + 1)
            out_weights(a["e_w_out"][0], KD)

            def experts(l):
                wg = a["moe_w_gate"][l].rearrange("e (p k) f -> e p k f", k=KD)
                wu = a["moe_w_up"][l].rearrange("e (p k) f -> e p k f", k=KD)
                wd = a["moe_w_down"][l].rearrange("e (p k) d -> e p k d", k=KH)
                n_items = EXPERTS
                sp.wait_ge(S("h_mixed"), l + 1)
                with sp.Fori(0, EXPERTS // NW) as i:
                    for s in range(NW):
                        sp.wait_ge(S(f"gu_used_l{l}"), i * NW + s + 1)
                        sp.dma_start(wgu[:, s, 0], wg[bass.ds(i * NW + s, 1)]).then_inc(S(f"gu_loaded{s}_l{l}"), 16)
                        sp.dma_start(wgu[:, s, 1], wu[bass.ds(i * NW + s, 1)]).then_inc(S(f"gu_loaded{s}_l{l}"), 16)
                        sp.wait_ge(S(f"dn_used_l{l}"), i * NW + s + 1)
                        sp.dma_start(wdn[:, s], wd[bass.ds(i * NW + s, 1)]).then_inc(S(f"dn_loaded{s}_l{l}"), 16)
                sp.wait_ge(S("lists_ready"), l + 1)
                extra = sp.value_load(lists[0:1, l, EXTRA_MAX - 1:EXTRA_MAX], min_val=0, max_val=EXTRA_MAX - 1)
                with sp.If(extra > 0):
                    with sp.Fori(0, extra) as o:
                        e = sp.value_load(lists[0:1, l, bass.ds(o, 1)], min_val=0, max_val=EXPERTS - 1)
                        sp.wait_ge(S(f"gu_used_l{l}"), o + n_items + NW)
                        sp.dma_start(wgu[:, 0, 0], wg[bass.ds(e, 1)]).then_inc(S(f"gu_loaded0_l{l}"), 16)
                        sp.dma_start(wgu[:, 0, 1], wu[bass.ds(e, 1)]).then_inc(S(f"gu_loaded0_l{l}"), 16)
                        sp.wait_ge(S(f"dn_used_l{l}"), o + n_items + NW)
                        sp.dma_start(wdn[:, 0], wd[bass.ds(e, 1)]).then_inc(S(f"dn_loaded0_l{l}"), 16)
            experts(0)

            w_odd = a["o_w_in"][0].rearrange("(p k) c -> p k c", k=KD)
            sp.wait_ge(S("moe_added"), 1)
            for c in range(ODD_CHUNKS):
                if c >= RING:
                    sp.wait_ge(S("qkv_ready"), 2 * (c - RING) + 2)
                sp.dma_start(ring[:, c % RING], w_odd[:, :, c * COLS:(c + 1) * COLS]).then_inc(
                    S(f"ring_loaded{c % RING}"), 16)
            sp.wait_ge(S("qkv_ready"), 2 * ODD_CHUNKS)
            out_weights(a["o_w_out"][0], 0)
            experts(1)
            sp.wait_ge(S("moe_added"), 2)
            sp.dma_start(out.rearrange("b (t p) d -> p (b t) d", p=P), h[:]).then_inc(S("stored"), 16)
            sp.wait_ge(S("stored"), 16)

        @block.gpsimd
        def _(pool):
            for t, v in ((ident, 1.0), (ones, 1.0), (head_sum, 0.0), (head_mean, 0.0), (group_mean, 1.0 / 256),
                         (upper, 1.0), (upper_strict, 1.0), (mask_level, 0.0), (mask_level_t, 0.0), (mask_pair, 0.0), (mask_ar, 1.0)):
                pool.memset(t[:], v)
            pool.memset(eps[:, 0:1], NORM_EPS)
            pool.memset(eps[:, 1:2], GN_EPS)
            pool.drain()
            for half in range(2):
                q = slice(64 * half, 64 * half + 64)
                pool.memset(head_sum[q, q], 1.0)
                pool.memset(head_mean[q, q], 1.0 / HD)
            pool.drain()
            pool.affine_select(ident[:], ident[:], [[1, P]], ALU.is_equal, 0.0, base=0, channel_multiplier=-1)
            pool.affine_select(upper[:], upper[:], [[1, P]], ALU.is_ge, 0.0, base=0, channel_multiplier=-1)
            pool.affine_select(upper_strict[:], upper_strict[:], [[1, P]], ALU.is_gt, 0.0, base=0,
                               channel_multiplier=-1)
            pool.affine_select(mask_ar[:, :, 0, :], mask_ar[:, :, 0, :], [[0, NT], [1, P]], ALU.is_gt, 0.0, base=0,
                               channel_multiplier=-1)
            pool.affine_select(mask_ar[:, :, 1, :], mask_ar[:, :, 1, :], [[0, NT], [1, P]], ALU.is_ge, 0.0, base=0,
                               channel_multiplier=-1)
            pair = mask_pair[:].rearrange("p (b r) -> p b r", r=2)[:, :, 1:2]
            pool.affine_select(pair, bc(ones[:, 0:1].unsqueeze(2), P // 2, 1), [[2, P // 2], [0, 1]], ALU.is_equal, 0.0,
                               base=0, channel_multiplier=-1)
            for n in range(6):
                m = 2 << n
                v = mask_level[:, n, :].rearrange("p (b r) -> p b r", r=2 * m)[:, :, 0:m]
                one = bc(ones[:, 0:1].unsqueeze(2), P // (2 * m), m)
                pool.affine_select(v, one, [[-2 * m, P // (2 * m)], [0, m]], ALU.is_ge, 0.0, base=-m,
                                   channel_multiplier=1)
                pool.drain()
                pool.affine_select(v, v, [[2 * m, P // (2 * m)], [0, m]], ALU.is_ge, 0.0, base=2 * m - 1,
                                   channel_multiplier=-1)
                v = mask_level_t[:, n, :].rearrange("p (b r) -> p b r", r=2 * m)[:, :, m:2 * m]
                pool.affine_select(v, one, [[-2 * m, P // (2 * m)], [0, m]], ALU.is_ge, 0.0, base=0,
                                   channel_multiplier=1)
                pool.drain()
                pool.affine_select(v, v, [[2 * m, P // (2 * m)], [0, m]], ALU.is_ge, 0.0, base=m - 1,
                                   channel_multiplier=-1)
            pool.iota(band[:], [[1, 2 * P]], base=-P, channel_multiplier=-1, allow_small_or_imprecise_dtypes=True)
            pool.iota(iota[:], [[0, 4], [1, SLOTS]], base=0, channel_multiplier=0, allow_small_or_imprecise_dtypes=True)
            pool.drain()
            pool.affine_select(band[:], band[:], [[-1, 2 * P]], ALU.is_ge, OUT_OF_BAND, base=P, channel_multiplier=1)
            pool.drain()
            pool.affine_select(band[:], band[:], [[1, 2 * P]], ALU.is_gt, OUT_OF_BAND, base=0, channel_multiplier=-1)
            pool.drain()
            for dup, half in ((dup_even, 0), (dup_odd, 1)):
                for to in range(2):
                    pool.tensor_copy(dup[:, 64 * to:64 * to + 64], ident[:, 64 * half:64 * half + 64])
            pool.drain().then_inc(S("consts_ready"), 1)

            with pool.Fori(0, SSD_GROUPS) as g:
                pool.wait_ge(S("silu_done"), 4 + CONV_DIM // P)
                pool.wait_ge(S("ssd_free"), g + 1)
                pool.sem_inc(S("pool_waited"), 1)
                pool.tensor_copy(sB, xbc[:, bass.ds(g + 8, 1), :].rearrange("p a t -> p (a t)"))
                pool.tensor_copy(sC, xbc[:, bass.ds(g + 12, 1), :].rearrange("p a t -> p (a t)"))
                pool.tensor_copy(sx, xbc[:, bass.ds(g * 2, 2), :]).then_inc(S("ssd_staged"), 1)

            for pair in range(KD // 2):
                for w in range(2):
                    pool.wait_ge(S(f"solved{w}"), pair + 1)
                    pool.tensor_copy(XT[w], bc(ident[:].unsqueeze(1), 4, P)).then_inc(S(f"x_reset{w}"), 1)

            with pool.Fori(0, KV_HEADS) as g:
                pool.wait_ge(S("att_inputs"), 1)
                pool.wait_ge(S("att_free"), g + 1)
                pool.sem_inc(S("pool_waited"), 1)
                pool.tensor_copy(vs, vtk.rearrange("p t a b -> p t (a b)")[:, :, bass.ds(g * HD, HD)])
                pool.tensor_copy(ks, kdup[:, bass.ds(g, 1), :].rearrange("p a t -> p (a t)"))
                pool.tensor_copy(qs, qkv[:, bass.ds(g * 2, 2), :]).then_inc(S("att_staged"), 1)

        @block.tensor
        def _(pe):
            def transposes(n):
                src = hn if n % 2 == 0 else hf
                pe.wait_ge(S("hn_ready"), n + 1)
                for b in range(4):
                    for q in range(4):
                        k, t = (4 * b + q) // NT, q % NT
                        i = pe.transpose(ps[:, b, q * P:(q + 1) * P],
                                         src[:, t, :].rearrange("p (f k) -> p k f", k=KD)[:, k, :], ident[:])
                    i.then_inc(S("hn_turned"), 1)
                pe.wait_ge(S("hnT_ready"), n + 1)

            for l in range(2):
                pe.sem_inc(S(f"gu_used_l{l}"), NW)
                pe.sem_inc(S(f"dn_used_l{l}"), NW)
            pe.wait_ge(S("consts_ready"), 1)
            pe.wait_ge(S("params_loaded"), 16 * PARAM_LOADS)
            pe.transpose(ps[:, 7, 0:114], rows[0:114, 0, :], ident[0:114, 0:114])
            pe.transpose(ps[:, 7, P:P + 56], rows[0:56, 1, :], ident[0:56, 0:56]).then_inc(S("par_turned"), 1)
            transposes(0)
            for t in range(NT):
                for k in range(KD):
                    i = pe.matmul(ps[:, 6, t * SSD_HEADS:(t + 1) * SSD_HEADS], hnT[:, k, t * P:(t + 1) * P],
                                  wdt[:, k, :], start=(k == 0), stop=(k == KD - 1))
            i.then_inc(S("dt_ready"), 1)
            pe.wait_ge(S("dt_abs"), 1)

            def project(s, half, done):
                b = 2 * s + half
                for k in range(KD):
                    i = pe.matmul(ps[:, b, 0:T], ring[:, s, k, half * P:(half + 1) * P], hnT[:, k, :],
                                  start=(k == 0), stop=(k == KD - 1))
                i.then_inc(done, 1)
            for s in range(RING):
                pe.wait_ge(S(f"ring_loaded{s}"), 16)
                for half in range(2):
                    project(s, half, S("projected"))
            pe.wait_ge(S("z_done"), 2 * Z_CHUNKS)
            with pe.Fori(0, CONV_CHUNKS // RING) as i:
                for s in range(RING):
                    pe.wait_ge(S(f"ring_loaded{s}"), i * 16 + 32)
                    for half in range(2):
                        pe.wait_ge(S("conv_done"), i * TILES_PER_RING + 2 * s + half + 1)
                        project(s, half, S("projected"))
            with pe.Fori(0, RWKV_CHUNKS // RING) as i:
                for s in range(RING):
                    pe.wait_ge(S(f"ring_loaded{s}"), i * 16 + 64)
                    for half in range(2):
                        pe.wait_ge(S("conv_done"), i * TILES_PER_RING + 16 + 2 * s + half + 1)
                        project(s, half, S("projected"))
            pe.wait_ge(S("ring_loaded0"), 16 * 7)
            for half in range(2):
                pe.wait_ge(S("conv_done"), 40 + half + 1)
                project(0, half, S("projected"))

            pe.wait_ge(S("lora_ready"), 1)
            pe.wait_ge(S("conv_done"), 8 + 16 + RWKV_TILES)
            n = 0
            for kind, (lo, hi, src) in enumerate(((0, 64, 24), (64, 128, 24), (0, 128, 25))):
                for j in range(KD):
                    b = n // 2 % 8
                    if n >= 16 and n % 2 == 0:
                        pe.wait_ge(S("lora_taken"), (n - 16) // 2 + 1)
                    i = pe.matmul(ps[:, b, (n % 2) * T:(n % 2 + 1) * T], lora_w[lo:hi, kind, j * P:(j + 1) * P],
                                  u[lo:hi, src, :], start=True, stop=True)
                    if n % 2:
                        i.then_inc(S("lora_out"), 1)
                    n += 1
            pe.wait_ge(S("lora_taken"), 12)

            pe.wait_ge(S("adt_ready"), 1)
            for c in range(NT):
                pe.matmul(ps[:, 0, c * SSD_HEADS:(c + 1) * SSD_HEADS], upper[:], dtp[:, 1, c, :], start=True, stop=True)
                i = pe.matmul(ps[:, 1, c * SSD_HEADS:(c + 1) * SSD_HEADS], ones[:], dtp[:, 1, c, :],
                              start=True, stop=True)
            i.then_inc(S("acum_ready"), 1)
            pe.wait_ge(S("acum_taken"), 1)

            with pe.Fori(0, SSD_GROUPS) as g:
                pe.wait_ge(S("ssd_staged"), g + 1)
                for c in range(NT):
                    for t in range(2):
                        pe.transpose(ps[:, 0, (2 * c + t) * P:(2 * c + t + 1) * P], sx[:, t, c * P:(c + 1) * P],
                                     ident[:])
                pe.transpose(ps[:, 1, 0:P], sB[:, 0:P], ident[:])
                for c in range(NT):
                    i = pe.matmul(ps[:, 2, c * P:(c + 1) * P], sB[:, c * P:(c + 1) * P], sC[:, c * P:(c + 1) * P],
                                  start=True, stop=True)
                i.then_inc(S("ssd_products"), 1)
                pe.wait_ge(S("ssd_factors"), g * 4 + 1)
                for c in range(NT):
                    i = pe.matmul(ps[:, 3 + c, :], ones[:], tria[:, c].rearrange("p a b -> p (a b)"),
                                  start=True, stop=True)
                i.then_inc(S("ssd_products"), 1)
                pe.wait_ge(S("ssd_factors"), g * 4 + 2)
                pe.matmul(ps[:, 5, 0:HPG * HD], btok, xst.rearrange("p a b -> p (a b)"), start=True,
                          stop=True).then_inc(S("ssd_products"), 1)
                pe.wait_ge(S("ssd_factors"), g * 4 + 3)
                for c in range(NT):
                    for hh in range(HPG):
                        t, half = hh // 2, hh % 2
                        o = ps[64 * half:64 * half + 64, 6, t * T + c * P:t * T + (c + 1) * P]
                        i = pe.matmul(o, xdt[:, c, hh, :], mm[:, c, hh, :], start=True, stop=(c == 0),
                                      skip_group_check=True)
                        if c == 1:
                            i = pe.matmul(o, state[:, hh, :], cs[:, hh, :], start=False, stop=True,
                                          skip_group_check=True)
                i.then_inc(S("ssd_products"), 1)
                pe.wait_ge(S("ssd_factors"), g * 4 + 4)
                for t in range(2):
                    i = pe.matmul(ps[:, 7, 0:T], group_mean[:], ssq[:, t, :], start=(t == 0), stop=(t == 1))
                i.then_inc(S("ssd_products"), 1)
            def project_out(src, before):
                for j in range(KD):
                    if j % (WO // 2) == 0:
                        pe.wait_ge(S(f"wo_loaded{j // (WO // 2)}"), 16 * (before + 1))
                    for t in range(NT):
                        for half in range(2):
                            i = pe.matmul(ps[:, 2 * t + half, :], src[:, j, t * P:(t + 1) * P],
                                          wo_ring[:, j, half * BANK:(half + 1) * BANK], start=(j == 0),
                                          stop=(j == KD - 1))
                i.then_inc(S("projected_out"), 1)

            pe.wait_ge(S("kk_sq"), 1)
            for j in range(KD):
                i = pe.matmul(ps[:, 4 + j // 2, (j % 2) * T:(j % 2 + 1) * T], head_sum[:], tmp8[:, j, :], start=True,
                              stop=True)
            i.then_inc(S("kk_len"), 1)
            project_out(mixT, 0)

            for pair in range(KD // 2):
                for w in range(2):
                    j, b0 = 2 * pair + w, 4 * w
                    n4 = j % 4
                    pe.wait_ge(S(f"solved{w}"), pair + 1)
                    pe.wait_ge(S(f"decayed{w}"), pair + 1)
                    pe.matmul(ps[:, b0 + 3, 0:T], head_sum[:], tmp[w], start=True, stop=True).then_inc(
                        S(f"tok_turned{w}"), 1)
                    for c in range(NT):
                        pe.transpose(ps[:, b0 + 2, c * P:(c + 1) * P], vv[:, j, c * P:(c + 1) * P], ident[:])
                    pe.transpose(ps[:, b0 + 2, 2 * P:3 * P], kt[n4][:, 0, :], ident[:])
                    pe.transpose(ps[:, b0 + 2, 3 * P:4 * P], bt[n4][:, 0, :], ident[:]).then_inc(
                        S(f"tok_turned{w}"), 1)
                for w in range(2):
                    j, b0 = 2 * pair + w, 4 * w
                    n4 = j % 4
                    for n, src in enumerate((bt[n4], kt[n4])):
                        if n == 1:
                            pe.wait_ge(S(f"bonus_done{w}"), pair + 1)
                            pe.wait_ge(S(f"tok_ready{w}"), pair + 1)
                        for hh in range(2):
                            q = slice(64 * hh, 64 * hh + 64)
                            for c in range(NT):
                                i = pe.matmul(ps[:, b0 + 2 * n + hh, c * 2 * P:(c + 1) * 2 * P], src[q, c, :],
                                              ar[n4][q, c].rearrange("p a b -> p (a b)"), start=True, stop=True)
                        i.then_inc(S(f"scores{w}"), 1)
                for w in range(2):
                    b0 = 4 * w
                    pe.wait_ge(S(f"xt_pairs{w}"), pair + 1)
                    for m in range(4):
                        i = pe.transpose(ps[:, b0, m * P:(m + 1) * P], XT[w][:, m, :], ident[:])
                    i.then_inc(S(f"x_turned{w}"), 1)
                for n in range(6):
                    for w in range(2):
                        b0 = 4 * w
                        pe.wait_ge(S(f"x_level{w}"), pair * 13 + 2 * n + 1)
                        for m in range(4):
                            c, hh = m // 2, m % 2
                            i = pe.matmul(ps[:, b0 + 1, m * P:(m + 1) * P], bar[w][:, hh, c, 0, :], X[w][:, m, :],
                                          start=True, stop=True)
                        i.then_inc(S(f"lx{w}"), 1)
                    for w in range(2):
                        b0 = 4 * w
                        pe.wait_ge(S(f"lx_taken{w}"), pair * 6 + n + 1)
                        for m in range(4):
                            i = pe.matmul(ps[:, b0 + 2, m * P:(m + 1) * P], XT[w][:, m, :], TX[w][:, m, :],
                                          start=True, stop=True)
                        i.then_inc(S(f"xlx{w}"), 1)
                        for m in range(4):
                            i = pe.matmul(ps[:, b0 + 3, m * P:(m + 1) * P], TX[w][:, m, :], XT[w][:, m, :],
                                          start=True, stop=True)
                        i.then_inc(S(f"xlx{w}"), 1)
                for c in range(NT):
                    for w in range(2):
                        n4, b0 = (2 * pair + w) % 4, 4 * w
                        if c == 0:
                            pe.wait_ge(S(f"x_level{w}"), pair * 13 + 13)
                        for hh in range(2):
                            q = slice(64 * hh, 64 * hh + 64)
                            o = ps[:, b0 + hh, 0:HD]
                            i = pe.matmul(o, kar[w][:, hh, c, 0, :], vtok[w][:, c, q], start=True, stop=(c == 0))
                            if c:
                                i = pe.matmul(o, ar[n4][q, c, 0, :], s0T[w][q, :], start=False, stop=True)
                        i.then_inc(S(f"solve_out{w}"), 1)
                    for w in range(2):
                        b0 = 4 * w
                        pe.wait_ge(S(f"solve_in{w}"), pair * 5 + 3 * c + 1)
                        for hh in range(2):
                            i = pe.matmul(ps[:, b0 + 2 + hh, 0:HD], XT[w][:, 2 * c + hh, :], rhs[w][:, hh, c, :],
                                          start=True, stop=True)
                        i.then_inc(S(f"solve_out{w}"), 1)
                    for w in range(2):
                        b0 = 4 * w
                        pe.wait_ge(S(f"solve_in{w}"), pair * 5 + 3 * c + 2)
                        if c == 0:
                            for hh in range(2):
                                q = slice(64 * hh, 64 * hh + 64)
                                pe.matmul(ps[q, b0, 0:HD], ktok[w][:, q], vtok[w][:, 0, q], start=True, stop=False,
                                          skip_group_check=True)
                                i = pe.matmul(ps[q, b0, 0:HD], btk[w][:, q], us[w][:, hh, 0, :], start=False,
                                              stop=True, skip_group_check=True)
                            i.then_inc(S(f"solve_out{w}"), 1)
                    if c == 0:
                        for w in range(2):
                            pe.wait_ge(S(f"solve_in{w}"), pair * 5 + 3)
                for w in range(2):
                    n4, b0 = (2 * pair + w) % 4, 4 * w
                    for c in range(NT):
                        for hh in range(2):
                            q = slice(64 * hh, 64 * hh + 64)
                            o = ps[q, b0, c * P:(c + 1) * P]
                            pe.matmul(o, vtok[w][:, c, q], kar[w][:, hh, c, 1, :], start=True, stop=False,
                                      skip_group_check=True)
                            i = pe.matmul(o, us[w][:, hh, c, :], bar[w][:, hh, c, 1, :], start=False,
                                          stop=(c == 0), skip_group_check=True)
                            if c:
                                i = pe.matmul(o, s0T[w][q, :], ar[n4][q, c, 1, :], start=False, stop=True,
                                              skip_group_check=True)
                    i.then_inc(S(f"solve_out{w}"), 1)
            for w in range(2):
                pe.wait_ge(S(f"solved{w}"), KD // 2 + 1)
            for j in range(KD):
                i = pe.matmul(ps[:, j // 2, (j % 2) * T:(j % 2 + 1) * T], head_mean[:], mixT[:, KD + j, :],
                              start=True, stop=True)
            i.then_inc(S("gn_out"), 1)
            pe.wait_ge(S("gn_sq"), 1)
            for j in range(KD):
                i = pe.matmul(ps[:, 4 + j // 2, (j % 2) * T:(j % 2 + 1) * T], head_mean[:], tmp8[:, j, :],
                              start=True, stop=True)
            i.then_inc(S("gn_out"), 1)

            pe.wait_ge(S("mixed"), 1)
            project_out(mixT[:, KD:, :], 1)

            def gather(n_done):
                for k in range(KD):
                    for t in range(NT):
                        i = pe.matmul(ps[:, 6, k * SLOTS:(k + 1) * SLOTS],
                                      hf[:, t, :].rearrange("p (f k) -> p k f", k=KD)[:, k, :], sel[:, t, :],
                                      start=(t == 0), stop=(t == NT - 1))
                return i

            def moe(l):
                transposes(2 * l + 1)
                for t in range(NT):
                    for k in range(KD):
                        i = pe.matmul(ps[:, 4, t * 64:t * 64 + GROUPS + EXPERTS], hfT[:, k, t * P:(t + 1) * P],
                                      router_w[:, l, k, :], start=(k == 0), stop=(k == KD - 1))
                i.then_inc(S("logits"), 1)
                pe.wait_ge(S("picked"), l + 1)
                pe.matmul(ps[:, 5, 0:EXPERTS], upper_strict[:], both[:, 0, :], start=True, stop=True)
                pe.matmul(ps[:, 5, EXPERTS:2 * EXPERTS], upper_strict[:], both[:, 1, :], start=True, stop=False)
                pe.matmul(ps[:, 5, EXPERTS:2 * EXPERTS], ones[:], both[:, 0, :], start=False, stop=True)
                for t in range(NT):
                    i = pe.matmul(ps[:, 5, 2 * EXPERTS:3 * EXPERTS], ones[:], both[:, t, :], start=(t == 0),
                                  stop=(t == 1))
                i.then_inc(S("ranked"), 1)
                pe.wait_ge(S("lists_ready"), l + 1)
                for b in range(4):
                    pe.matmul(ps[:, b, :], zero[:, 0:P], zero, start=True, stop=False, skip_group_check=True)
                pe.wait_ge(S(f"sel_ready_l{l}"), 1)
                gather(l).then_inc(S(f"gathered_l{l}"), 1)

                def scatter():
                    for t in range(NT):
                        for half in range(2):
                            i = pe.matmul(ps[:, 2 * t + half, :], gT[:, t, :], ys[:, half * BANK:(half + 1) * BANK],
                                          start=False, stop=False, skip_group_check=True)
                    return i

                def item(n, s, loaded):
                    pe.wait_ge(S(f"xg_ready_l{l}"), n + 1)
                    pe.wait_ge(S(f"gu_loaded{s}_l{l}"), loaded * 32 + 32)
                    for w in range(2):
                        for kk2 in range(2):
                            for q in range(4):
                                i = pe.matmul(ps[32 * q:32 * q + 32, 4 + w, :], xg[:, 2 * q + kk2, :],
                                              wgu[:, s, w, 2 * q + kk2, :], start=(kk2 == 0), stop=(kk2 == 1),
                                              skip_group_check=True)
                    i.then_inc(S(f"gu_used_l{l}"), 1)
                    scatter()
                    pe.wait_ge(S(f"selg_ready_l{l}"), n + 1)
                    for t in range(NT):
                        i = pe.transpose(ps[:, 6, t * P:(t + 1) * P], selg[:, t, :], ident[:])
                    i.then_inc(S(f"selg_turned_l{l}"), 1)
                    pe.wait_ge(S(f"gate_copied_l{l}"), n + 1)
                    pe.wait_ge(S(f"up_copied_l{l}"), n + 1)
                    for w in range(2):
                        for k in range(KH):
                            c = T + (w * KH + k) * SLOTS
                            i = pe.matmul(ps[:, 7, c:c + SLOTS],
                                          gus[:, w, :].rearrange("p (f k) -> p k f", k=KH)[:, k, :], fold[:],
                                          start=True, stop=True)
                    i.then_inc(S(f"folded_l{l}"), 1)
                    pe.wait_ge(S(f"gT_copied_l{l}"), n + 1)
                    pe.wait_ge(S(f"sel_ready_l{l}"), n + 2)
                    gather(l).then_inc(S(f"gathered_l{l}"), 1)
                    pe.wait_ge(S(f"hid_ready_l{l}"), n + 1)
                    pe.wait_ge(S(f"dn_loaded{s}_l{l}"), loaded * 16 + 16)
                    for half in range(2):
                        for q in range(4):
                            i = pe.matmul(ps[32 * q:32 * q + 32, 4 + half, :], hidT[:, q, :],
                                          wdn[:, s, q, half * BANK:(half + 1) * BANK], start=True, stop=True,
                                          skip_group_check=True)
                    i.then_inc(S(f"dn_used_l{l}"), 1)
                    pe.wait_ge(S(f"y0_copied_l{l}"), n + 1)
                    pe.wait_ge(S(f"y1_copied_l{l}"), n + 1)

                with pe.Fori(0, EXPERTS // NW) as i:
                    for s in range(NW):
                        item(i * NW + s, s, i)
                extra = pe.value_load(lists[0:1, l, EXTRA_MAX - 1:EXTRA_MAX], min_val=0, max_val=EXTRA_MAX - 1)
                with pe.If(extra > 0):
                    with pe.Fori(0, extra) as o:
                        item(o + EXPERTS, 0, o + EXPERTS // NW)
                for b in range(4):
                    t, half = b // 2, b % 2
                    i = pe.matmul(ps[:, b, :], gT[:, t, :], ys[:, half * BANK:(half + 1) * BANK], start=False,
                                  stop=True, skip_group_check=True)
                i.then_inc(S("moe_summed"), 1)
            moe(0)

            transposes(2)
            for c in range(ODD_CHUNKS):
                s = c % RING
                pe.wait_ge(S(f"ring_loaded{s}"), 16 * (c // RING + 1 + (7 if s == 0 else 6)))
                for half in range(2):
                    if c >= RING:
                        pe.wait_ge(S("qkv_taken"), 2 * (c - RING) + half + 1)
                    project(s, half, S("qkv_ready"))
            pe.wait_ge(S("qk_sq"), 1)
            for j in range(10):
                i = pe.matmul(ps[:, j // 2, (j % 2) * T:(j % 2 + 1) * T], head_mean[:], sqs[:, j, :], start=True,
                              stop=True)
            i.then_inc(S("qk_ms"), 1)
            pe.wait_ge(S("qk_normed"), 1)
            for g in range(KV_HEADS):
                pe.matmul(ps[:, g // 2, (g % 2) * T:(g % 2 + 1) * T], (dup_even, dup_odd)[g % 2][:], qkv[:, 8 + g // 2, :],
                          start=True, stop=True)
            for j in range(2):
                for t in range(NT):
                    i = pe.transpose(ps[:, 2, (2 * t + j) * P:(2 * t + j + 1) * P], qkv[:, 10 + j, t * P:(t + 1) * P],
                                     ident[:])
            i.then_inc(S("kv_out"), 1)
            with pe.Fori(0, KV_HEADS) as g:
                pe.wait_ge(S("att_staged"), g + 1)
                for t in range(NT):
                    n_keys = P if t == 0 else 2 * P
                    for hh in range(4):
                        q = slice(64 * (hh % 2), 64 * (hh % 2) + 64)
                        i = pe.matmul(ps[:, hh, 0:n_keys], qs[q, hh // 2, t * P:(t + 1) * P],
                                      ks[q, 0:n_keys],
                                      start=True, stop=True)
                    i.then_inc(S("qk_out"), 1)
                    pe.wait_ge(S("probs"), g * 2 + t + 1)
                    for hh in range(4):
                        for kb in range(t + 1):
                            i = pe.transpose(ps[:, 4 + kb, hh * P:(hh + 1) * P], pr[:, hh, kb * P:(kb + 1) * P],
                                             ident[:])
                    i.then_inc(S("probs_turned"), 1)
                    pe.wait_ge(S("pT_ready"), g * 2 + t + 1)
                    for hh in range(4):
                        half = hh % 2
                        for kb in range(t + 1):
                            i = pe.matmul(ps[64 * half:64 * half + 64, 6, (hh // 2) * P:(hh // 2 + 1) * P],
                                          vs[:, kb, :], pT[:, hh, kb, :], start=(kb == 0), stop=(kb == t),
                                          skip_group_check=True)
                    i.then_inc(S("att_out"), 1)
                    pe.wait_ge(S("att_taken"), g * 2 + t + 1)
            project_out(attT, 2)
            moe(1)

        @block.scalar
        def _(act):
            def norm_squares(n):
                dst = hn if n % 2 == 0 else hf
                if n == 0:
                    act.wait_ge(S("x_loaded"), 16)
                    act.wait_ge(S("consts_ready"), 1)
                elif n % 2:
                    act.wait_ge(S("h_mixed"), n // 2 + 1)
                else:
                    act.wait_ge(S("moe_added"), n // 2)
                for t in range(NT):
                    act.activation(dst[:, t, :], h[:, t, :], ACT.Square, accum_out=ss[:, t:t + 1])
                act.drain()
                act.activation(ss[:], ss[:], ACT.Sqrt, bias=eps[:, 0:1], scale=1.0 / D).then_inc(S("rms_ready"), 1)
            act.sem_inc(S("silu_done"), 4)
            norm_squares(0)
            for t in range(2 * Z_CHUNKS):
                act.wait_ge(S("projected"), t + 1)
                act.activation(zs[:, t, :], ps[:, t, 0:T], ACT.Silu).then_inc(S("z_done"), 1)
            with act.Fori(0, CONV_DIM // P // 4) as i:
                for s in range(4):
                    act.wait_ge(S("conv_done"), i * 4 + 8 + s + 1)
                    act.activation(xbc[:, bass.ds(i * 4 + s, 1), :].rearrange("p a t -> p (a t)"), cbuf[:, s, :],
                                   ACT.Silu).then_inc(S("silu_done"), 1)
            act.wait_ge(S("conv_done"), 8 + 16 + RWKV_TILES)
            act.activation(u[0:64, 24, :], u[0:64, 24, :], ACT.Tanh)
            act.activation(u[:, 25, :], u[:, 25, :], ACT.Sigmoid)
            act.drain().then_inc(S("lora_ready"), 1)
            act.wait_ge(S("par_ready"), 1)
            for n in range(0, 3 * KD, 2):
                kind, j = n // KD, n % KD
                act.wait_ge(S("lora_out"), n // 2 + 1)
                for half in range(2):
                    src = ps[:, n // 2 % 8, half * T:(half + 1) * T]
                    if kind == 2:
                        i = act.activation(gate[:, j + half, :], src, ACT.Copy)
                    else:
                        dst, col = ((dec, W0), (agate, A0))[kind]
                        i = act.activation(dst[:, j + half, :], src, ACT.Sigmoid,
                                           bias=par[:, 1, col + j + half:col + j + half + 1])
                i.then_inc(S("lora_taken"), 1)
            act.wait_ge(S("dt_abs"), 1)
            act.activation(dtp[:, 6], dtp[:, 6], ACT.Exp, scale=-1.0)
            act.activation(dtp[:, 7, 0, :], a_log[:], ACT.Exp)
            act.drain()
            act.activation(dtp[:, 6], dtp[:, 6], ACT.Ln, bias=ones[:, 0:1]).then_inc(S("dt_log"), 1)
            act.wait_ge(S("acum_taken"), 1)
            act.activation(dtp[:, 4], dtp[:, 4], ACT.Exp).then_inc(S("dst_exp"), 1)
            with act.Fori(0, SSD_GROUPS) as g:
                act.wait_ge(S("ssd_diff"), g + 1)
                act.activation(mm.rearrange("p a b c -> p (a b c)"), mm.rearrange("p a b c -> p (a b c)"), ACT.Exp)
                act.activation(cs.rearrange("p a b -> p (a b)"), ps[:, 4, :], ACT.Exp).then_inc(S("ssd_exp"), 1)
                act.wait_ge(S("ssd_var_eps"), g + 1)
                act.activation(sr, sr, ACT.Sqrt).then_inc(S("ssd_root"), 1)
            act.wait_ge(S("kk_len"), 1)
            for b in range(4):
                i = act.activation(tmp8[:, 2 * b:2 * b + 2, :].rearrange("p a t -> p (a t)"), ps[:, 4 + b, :], ACT.Sqrt)
            i.then_inc(S("kk_root"), 1)

            def decays(pair):
                for w in range(2):
                    n4 = (2 * pair + w) % 4
                    act.wait_ge(S(f"cum_ready{w}"), pair + 1)
                    for c in range(NT):
                        act.activation(e1[w][:, c, :], cum[w][:, c, :], ACT.Exp, scale=-DECAY_FACTOR,
                                       bias=edge[n4][:, c:c + 1])
                        act.activation(e2[w][:, c, :], cum[w][:, c, 1:], ACT.Exp, scale=DECAY_FACTOR,
                                       bias=edge[n4][:, 2 + c:3 + c])
                    act.activation(edge[n4][:, 5:6], edge[n4][:, 4:5], ACT.Exp).then_inc(S(f"decay_exp{w}"), 1)
            decays(0)
            for pair in range(KD // 2):
                for w in range(2):
                    act.wait_ge(S(f"tok_turned{w}"), 2 * pair + 2)
                    act.activation(vtok[w].rearrange("p a b -> p (a b)"), ps[:, 4 * w + 2, 0:2 * P], ACT.Copy)
                    act.activation(ktok[w], ps[:, 4 * w + 2, 2 * P:3 * P], ACT.Copy)
                    act.activation(btk[w], ps[:, 4 * w + 2, 3 * P:4 * P], ACT.Copy).then_inc(S(f"tok_ready{w}"), 1)
                for n in range(6):
                    for w in range(2):
                        act.wait_ge(S(f"lx{w}"), pair * 6 + n + 1)
                        act.activation(TX[w].rearrange("p a b -> p (a b)"), ps[:, 4 * w + 1, :],
                                       ACT.Copy).then_inc(S(f"lx_taken{w}"), 1)
                    if n == 2 and pair < KD // 2 - 1:
                        decays(pair + 1)

            act.wait_ge(S("gn_centred"), 1)
            act.activation(tmp8.rearrange("p a t -> p (a t)"), mixT[:, KD:, :].rearrange("p a t -> p (a t)"),
                           ACT.Square).then_inc(S("gn_sq"), 1)
            act.wait_ge(S("gn_out"), 2)
            for b in range(4):
                i = act.activation(tmp8[:, 2 * b:2 * b + 2, :].rearrange("p a t -> p (a t)"), ps[:, 4 + b, :],
                                   ACT.Sqrt, bias=eps[:, 1:2])
            i.then_inc(S("gn_root"), 1)

            def moe(l):
                norm_squares(2 * l + 1)
                act.wait_ge(S("coarse_shifted"), l + 1)
                for t in range(NT):
                    act.activation(c8[:, t, 0:GROUPS], c8[:, t, 0:GROUPS], ACT.Exp, accum_out=sc[:, 0, t:t + 1])
                act.activation(sc[:, 1, :], sc[:, 1, :], ACT.Exp).then_inc(S("gates_exp"), 1)

                def item(n):
                    act.wait_ge(S(f"gu_used_l{l}"), n + NW + 1)
                    act.activation(gus[:, 0, :], ps[:, 4, :], ACT.Copy).then_inc(S(f"gate_copied_l{l}"), 1)
                    act.wait_ge(S(f"selg_turned_l{l}"), n + 1)
                    act.activation(gT.rearrange("p a b -> p (a b)"), ps[:, 6, 0:T],
                                   ACT.Copy).then_inc(S(f"gT_copied_l{l}"), 1)
                    act.wait_ge(S(f"folded_l{l}"), n + 1)
                    act.activation(sil.rearrange("p a b -> p (a b)"), ps[:, 7, T:T + P],
                                   ACT.Silu).then_inc(S(f"silu_l{l}"), 1)
                    act.wait_ge(S(f"dn_used_l{l}"), n + NW + 1)
                    act.activation(ys[:, 0:BANK], ps[:, 4, :], ACT.Copy).then_inc(S(f"y0_copied_l{l}"), 1)
                with act.Fori(0, EXPERTS // NW) as i:
                    for s in range(NW):
                        item(i * NW + s)
                act.wait_ge(S("lists_ready"), l + 1)
                extra = act.value_load(lists[0:1, l, EXTRA_MAX - 1:EXTRA_MAX], min_val=0, max_val=EXTRA_MAX - 1)
                with act.If(extra > 0):
                    with act.Fori(0, extra) as o:
                        item(o + EXPERTS)
            moe(0)

            norm_squares(2)
            for j in range(12):
                act.wait_ge(S("qkv_ready"), j + 1)
                act.activation(qkv[:, j, :], ps[:, j % 8, 0:T], ACT.Copy)
                if j < 10:
                    act.activation(sqs[:, j, :], ps[:, j % 8, 0:T], ACT.Square)
                act.drain().then_inc(S("qkv_taken"), 1)
            act.sem_inc(S("qk_sq"), 1)
            act.wait_ge(S("qk_ms"), 1)
            for b in range(5):
                i = act.activation(sqs[:, 2 * b:2 * b + 2, :].rearrange("p a t -> p (a t)"), ps[:, b, :], ACT.Sqrt,
                                   bias=eps[:, 0:1])
            i.then_inc(S("qk_root"), 1)
            with act.Fori(0, KV_HEADS) as g:
                for t in range(NT):
                    n_keys = P if t == 0 else 2 * P
                    act.wait_ge(S("shifted"), g * 2 + t + 1)
                    for hh in range(4):
                        act.activation(pr[:, hh, 0:n_keys], pr[:, hh, 0:n_keys], ACT.Exp, bias=st[:, 1, hh:hh + 1],
                                       accum_out=st[:, 2, hh:hh + 1])
                    act.activation(st[:, 3, :], st[:, 3, :], ACT.Exp).then_inc(S("exped"), 1)
                    act.wait_ge(S("probs_turned"), g * 2 + t + 1)
                    for kb in range(t + 1):
                        i = act.activation(pT[:, :, kb, :], ps[:, 4 + kb, :].rearrange("p (a b) -> p a b", b=P),
                                           ACT.Copy)
                    i.then_inc(S("pT_ready"), 1)
            moe(1)

        @block.vector
        def _(dve):
            tt, tsc, stt, cp = dve.tensor_tensor, dve.tensor_scalar, dve.scalar_tensor_tensor, dve.tensor_copy

            def normalise(n):
                dst = hn if n % 2 == 0 else hf
                dstT = hnT if n % 2 == 0 else hfT
                dve.wait_ge(S("rms_ready"), n + 1)
                dve.reciprocal(rstd[:], ss[:])
                dve.drain()
                for t in range(NT):
                    i = tsc(dst[:, t, :], h[:, t, :], rstd[:, t:t + 1], None, ALU.mult)
                i.then_inc(S("hn_ready"), 1)
                for b in range(4):
                    dve.wait_ge(S("hn_turned"), 4 * n + b + 1)
                    i = tt(dstT[:, 2 * b:2 * b + 2, :], ps[:, b, :].rearrange("p (k t) -> p k t", t=T),
                           bc(gains[:, n, 2 * b:2 * b + 2].unsqueeze(2), 2, T), ALU.mult)
                i.then_inc(S("hnT_ready"), 1)

            dve.wait_ge(S("consts_ready"), 1)
            dve.tensor_reduce(fold[:], ident[:].rearrange("p (q j) -> p j q", q=4), AX.X, ALU.add)
            dve.wait_ge(S("params_loaded"), 16 * PARAM_LOADS)
            normalise(0)
            dve.wait_ge(S("par_turned"), 1)
            cp(par[:, 0, 0:114], ps[:, 7, 0:114])
            cp(par[:, 1, 0:56], ps[:, 7, P:P + 56])
            dve.drain()
            tsc(par[:, 1, 64:64 + RWKV_TILES], par[:, 0, MU:MU + RWKV_TILES], -1.0, 1.0, ALU.mult, ALU.add)
            dve.drain().then_inc(S("par_ready"), 1)
            dve.wait_ge(S("dt_ready"), 1)
            tt(dtp[:, 0], ps[:, 6, 0:NT * SSD_HEADS].rearrange("p (c h) -> p c h", c=NT),
               bc(dt_bias[:].unsqueeze(1), NT, SSD_HEADS), ALU.add)
            dve.drain()
            tsc(dtp[:, 6], dtp[:, 0], -1.0, None, ALU.mult)
            dve.drain()
            tt(dtp[:, 6], dtp[:, 0], dtp[:, 6], ALU.max).then_inc(S("dt_abs"), 1)
            dve.sem_inc(S("conv_done"), 8)

            with dve.Fori(0, CONV_CHUNKS // RING) as i:
                for b in range(TILES_PER_RING):
                    dve.wait_ge(S("projected"), i * TILES_PER_RING + 2 * Z_CHUNKS + b + 1)
                    dve.wait_ge(S("silu_done"), i * TILES_PER_RING + b + 1)
                    tile = i * TILES_PER_RING + b
                    buf = cbuf[:, b % 4, :]
                    tsc(buf, ps[:, b, 0:T], par[:, 0, bass.ds(tile + CW + 48, 1)], par[:, 0, bass.ds(tile + CB, 1)],
                        ALU.mult, ALU.add)
                    for s in range(1, CONV_TAPS):
                        dve.drain()
                        ins = stt(buf[:, s:], ps[:, b, 0:T - s], par[:, 0, bass.ds(tile + CW + 16 * (3 - s), 1)],
                                  buf[:, s:], ALU.mult, ALU.add)
                    ins.then_inc(S("conv_done"), 1)

            def token_shift(b, tile, ready):
                dve.wait_ge(S("projected"), ready + 2 * (Z_CHUNKS + CONV_CHUNKS))
                dst = u[:, bass.ds(tile, 1), :].rearrange("p a t -> p (a t)")
                tsc(dst, ps[:, b, 0:T], par[:, 1, bass.ds(tile + 64, 1)], None, ALU.mult)
                dve.drain()
                dst = u[:, bass.ds(tile, 1), 1:].rearrange("p a t -> p (a t)")
                stt(dst, ps[:, b, 0:T - 1], par[:, 0, bass.ds(tile + MU, 1)], dst, ALU.mult,
                    ALU.add).then_inc(S("conv_done"), 1)
            with dve.Fori(0, RWKV_CHUNKS // RING) as i:
                for b in range(TILES_PER_RING):
                    token_shift(b, i * TILES_PER_RING + b, i * TILES_PER_RING + b + 1)
            for b in range(2):
                token_shift(b, 24 + b, 24 + b + 1)

            dve.wait_ge(S("dt_log"), 1)
            tsc(dtp[:, 0], dtp[:, 0], 0.0, None, ALU.max)
            dve.drain()
            tt(dtp[:, 0], dtp[:, 0], dtp[:, 6], ALU.add)
            dve.drain()
            stt(dtp[:, 1], dtp[:, 0], -1.0, bc(dtp[:, 7, 0:1, :], NT, SSD_HEADS), ALU.mult,
                ALU.mult).then_inc(S("adt_ready"), 1)
            dve.wait_ge(S("acum_ready"), 1)
            cp(dtp[:, 2], ps[:, 0, 0:NT * SSD_HEADS].rearrange("p (c h) -> p c h", c=NT))
            dve.drain()
            tt(dtp[:, 4], ps[:, 1, 0:NT * SSD_HEADS].rearrange("p (c h) -> p c h", c=NT), dtp[:, 2],
               ALU.subtract).then_inc(S("acum_taken"), 1)
            dve.wait_ge(S("dst_exp"), 1)
            dve.sem_inc(S("ssd_free"), 1)

            with dve.Fori(0, SSD_GROUPS) as g:
                def per_head(row, c):
                    return dtp[:, row, c, bass.ds(g * HPG, HPG)]
                for c in range(NT):
                    i = tt(tria[:, c], bc(upper[:].unsqueeze(1), HPG, P), bc(per_head(1, c).unsqueeze(2), HPG, P),
                           ALU.mult)
                i.then_inc(S("ssd_factors"), 1)
                dve.wait_ge(S("ssd_products"), g * 5 + 1)
                for c in range(NT):
                    tt(xdt[:, c], ps[:, 0, c * 2 * P:(c + 1) * 2 * P].rearrange("p (h d) -> p h d", d=HD),
                       bc(per_head(0, c).unsqueeze(2), HPG, HD), ALU.mult)
                cp(btok, ps[:, 1, 0:P])
                tt(cbm, ps[:, 2, 0:T].rearrange("p (c t) -> p c t", c=NT), bc(upper[:].unsqueeze(1), NT, P), ALU.mult)
                dve.drain()
                tt(xst, xdt[:, 0], bc(per_head(4, 0).unsqueeze(2), HPG, HD), ALU.mult).then_inc(S("ssd_factors"), 1)
                dve.wait_ge(S("ssd_products"), g * 5 + 2)
                for c in range(NT):
                    tt(mm[:, c], ps[:, 3 + c, :].rearrange("p (h t) -> p h t", t=P),
                       bc(per_head(2, c).unsqueeze(2), HPG, P), ALU.subtract)
                dve.drain()
                tsc(mm, mm, 0.0, None, ALU.min).then_inc(S("ssd_diff"), 1)
                dve.wait_ge(S("ssd_products"), g * 5 + 3)
                cp(state.rearrange("p a b -> p (a b)"), ps[:, 5, 0:HPG * HD])
                dve.wait_ge(S("ssd_exp"), g + 1)
                for c in range(NT):
                    tt(mm[:, c], mm[:, c], bc(cbm[:, c:c + 1, :], HPG, P), ALU.mult)
                tt(cs, cs, bc(sC[:, P:].unsqueeze(1), HPG, P), ALU.mult)
                dve.drain().then_inc(S("ssd_factors"), 1)
                dve.wait_ge(S("ssd_products"), g * 5 + 4)
                for t in range(2):
                    stt(sy[:, t, :], sx[:, t, :], d_skip[:, bass.ds(g * 2 + t, 1)], ps[:, 6, t * T:(t + 1) * T],
                        ALU.mult, ALU.add)
                dve.drain()
                tt(sy, sy, zs[:, bass.ds(g * 2, 2), :], ALU.mult)
                dve.drain()
                tt(ssq, sy, sy, ALU.mult).then_inc(S("ssd_factors"), 1)
                dve.wait_ge(S("ssd_products"), g * 5 + 5)
                tsc(sr, ps[:, 7, 0:T], 1e-5, None, ALU.add).then_inc(S("ssd_var_eps"), 1)
                dve.wait_ge(S("ssd_root"), g + 1)
                dve.reciprocal(sr, sr)
                dve.drain()
                for t in range(2):
                    stt(mixT[:, bass.ds(g * 2 + t, 1), :].rearrange("p a t -> p (a t)"), sy[:, t, :],
                        par[:, 0, bass.ds(g * 2 + t + NW_, 1)], sr, ALU.mult, ALU.mult)
                dve.drain().then_inc(S("ssd_free"), 1)

            def residual(used, n):
                dve.wait_ge(used, n)
                for t in range(NT):
                    tt(h[:, t, :].rearrange("p (a b) -> p a b", a=2), h[:, t, :].rearrange("p (a b) -> p a b", a=2),
                       ps[:, 2 * t:2 * t + 2, :], ALU.add)
                return dve.drain()

            for j in range(KD):
                tsc(kk[:, j, :], kv_[:, j, :], par[:, 1, KK + j:KK + j + 1], None, ALU.mult)
            dve.drain()
            tt(tmp8, kk, kk, ALU.mult).then_inc(S("kk_sq"), 1)
            for w in range(2):
                dve.memset(kar[w], 0.0)
                dve.memset(bar[w], 0.0)
                dve.memset(cum[w], 0.0)
            dve.wait_ge(S("kk_root"), 1)
            tsc(tmp8, tmp8, 1e-12, None, ALU.max)
            dve.drain()
            dve.reciprocal(tmp8, tmp8)
            dve.drain()
            tt(kk, kk, tmp8, ALU.mult)
            dve.drain()

            def prepare(j, step):
                w, n4 = j % 2, j % 4
                e = edge[n4]
                if step == 0:
                    tsc(kp[w], agate[:, j, :], -1.0, par[:, 1, KA + j:KA + j + 1], ALU.add, ALU.mult)
                    for c in range(NT):
                        dve.tensor_tensor_scan(cum[w][:, c, 1:], ones[:], dec[:, j, c * P:(c + 1) * P], 0.0, ALU.mult,
                                               ALU.add)
                elif step == 1:
                    stt(kp[w], kp[w], 1.0, kv_[:, j, :], ALU.add, ALU.mult)
                    for c in range(NT):
                        tsc(e[:, c:c + 1], cum[w][:, c, HD:HD + 1], DECAY_FACTOR, None, ALU.mult)
                        tsc(e[:, 2 + c:3 + c], cum[w][:, c, HD:HD + 1], -DECAY_FACTOR, None, ALU.mult)
                    tt(e[:, 4:5], cum[w][:, 0, HD:HD + 1], cum[w][:, 0, P:P + 1], ALU.subtract)
                    dve.drain()
                    stt(e[:, 4:5], cum[w][:, 1, HD:HD + 1], -1.0, e[:, 4:5], ALU.mult, ALU.add)
                    dve.drain()
                    tsc(e[:, 4:5], e[:, 4:5], DECAY_FACTOR, None, ALU.mult).then_inc(S(f"cum_ready{w}"), 1)
                elif step == 2:
                    stt(tmp[w], rv[:, j, :], par[:, 1, RK + j:RK + j + 1], kp[w], ALU.mult, ALU.mult)
                elif step == 3:
                    dve.wait_ge(S(f"decay_exp{w}"), j // 2 + 1)
                    stt(ar[n4][:, :, 0, :], kk[:, j, :].rearrange("p (c t) -> p c t", c=NT), -1.0, e1[w][:, :, 0:P],
                        ALU.mult, ALU.mult)
                    tt(ar[n4][:, :, 1, :], rv[:, j, :].rearrange("p (c t) -> p c t", c=NT), e1[w][:, :, 1:], ALU.mult)
                elif step == 4:
                    tt(kt[n4].rearrange("p c t -> p (c t)"), kp[w], e2[w].rearrange("p c t -> p (c t)"), ALU.mult)
                    tt(bt[n4].rearrange("p c t -> p (c t)"), agate[:, j, :], e2[w].rearrange("p c t -> p (c t)"),
                       ALU.mult)
                else:
                    tt(bt[n4].rearrange("p c t -> p (c t)"), bt[n4].rearrange("p c t -> p (c t)"), kk[:, j, :],
                       ALU.mult).then_inc(S(f"decayed{w}"), 1)

            for step in range(6):
                for w in range(2):
                    prepare(w, step)
                dve.drain()
            residual(S("projected_out"), 1)
            for w in range(2):
                dve.sem_inc(S(f"solved{w}"), 1)
            for pair in range(KD // 2):
                for w in range(2):
                    j, b0 = 2 * pair + w, 4 * w
                    dve.wait_ge(S(f"tok_turned{w}"), 2 * pair + 1)
                    tt(bonus[:, j, :], ps[:, b0 + 3, 0:T], vv[:, j, :], ALU.mult).then_inc(S(f"bonus_done{w}"), 1)
                for w in range(2):
                    b0 = 4 * w
                    dve.wait_ge(S(f"scores{w}"), 2 * pair + 1)
                    for hh in range(2):
                        dve.copy_predicated(bar[w][:, hh], mask_ar[:].bitcast(I32),
                                            ps[:, b0 + hh, :].rearrange("p (c a t) -> p c a t", c=NT, a=2))
                    dve.drain()
                    dve.wait_ge(S(f"x_reset{w}"), pair + 1)
                    for hh in range(2):
                        i = dve.copy_predicated(XT[w].rearrange("p (c h) t -> p h c t", h=2)[:, hh],
                                                bc(mask_pair[:].bitcast(I32).unsqueeze(1), NT, P),
                                                bar[w][:, hh, :, 0, :])
                    i.then_inc(S(f"xt_pairs{w}"), 1)
                    dve.wait_ge(S(f"scores{w}"), 2 * pair + 2)
                    for hh in range(2):
                        dve.copy_predicated(kar[w][:, hh], mask_ar[:].bitcast(I32),
                                            ps[:, b0 + 2 + hh, :].rearrange("p (c a t) -> p c a t", c=NT, a=2))
                for w in range(2):
                    dve.wait_ge(S(f"x_turned{w}"), pair + 1)
                    cp(X[w].rearrange("p a b -> p (a b)"), ps[:, 4 * w, :]).then_inc(S(f"x_level{w}"), 1)
                for n in range(6):
                    for w in range(2):
                        for which, (dst, mask) in enumerate(((X[w], mask_level), (XT[w], mask_level_t))):
                            dve.wait_ge(S(f"xlx{w}"), (pair * 6 + n) * 2 + 2)
                            dve.copy_predicated(dst, bc(mask[:, n:n + 1, :].bitcast(I32), 4, P),
                                                ps[:, 4 * w + 2 + which, :].rearrange("p (m t) -> p m t", m=4)
                                                ).then_inc(S(f"x_level{w}"), 1)
                    if pair < KD // 2 - 1:
                        for w in range(2):
                            prepare(2 * pair + 2 + w, n)
                        dve.drain()
                for c in range(NT):
                    for w in range(2):
                        dve.wait_ge(S(f"solve_out{w}"), pair * 6 + 3 * c + 1)
                        cp(rhs[w][:, :, c, :], ps[:, 4 * w:4 * w + 2, 0:HD]).then_inc(S(f"solve_in{w}"), 1)
                    for w in range(2):
                        dve.wait_ge(S(f"solve_out{w}"), pair * 6 + 3 * c + 2)
                        cp(us[w][:, :, c, :], ps[:, 4 * w + 2:4 * w + 4, 0:HD]).then_inc(S(f"solve_in{w}"), 1)
                    if c == 0:
                        for w in range(2):
                            dve.wait_ge(S(f"solve_out{w}"), pair * 6 + 3)
                            tsc(s0T[w], ps[:, 4 * w, 0:HD], edge[(2 * pair + w) % 4][:, 5:6], None,
                                ALU.mult).then_inc(S(f"solve_in{w}"), 1)
                for w in range(2):
                    dve.wait_ge(S(f"solve_out{w}"), pair * 6 + 6)
                    cp(mixT[:, KD + 2 * pair + w, :], ps[:, 4 * w, 0:T]).then_inc(S(f"solved{w}"), 1)
            dve.drain()

            my = mixT[:, KD:, :]
            dve.wait_ge(S("gn_out"), 1)
            for b in range(4):
                v = my[:, 2 * b:2 * b + 2, :]
                tt(v, v, ps[:, b, :].rearrange("p (a t) -> p a t", a=2), ALU.subtract)
            dve.drain().then_inc(S("gn_centred"), 1)
            dve.wait_ge(S("gn_root"), 1)
            dve.reciprocal(tmp8, tmp8)
            dve.drain()
            tt(my, my, tmp8, ALU.mult)
            dve.drain()
            for j in range(KD):
                tsc(my[:, j, :], my[:, j, :], par[:, 1, LNW + j:LNW + j + 1], par[:, 1, LNB + j:LNB + j + 1], ALU.mult,
                    ALU.add)
            dve.drain()
            tt(my, my, bonus, ALU.add)
            dve.drain()
            tt(my, my, gate, ALU.mult).then_inc(S("mixed"), 1)

            residual(S("projected_out"), 2).then_inc(S("h_mixed"), 1)

            def moe(l):
                dve.wait_ge(S("rms_ready"), 2 * l + 2)
                dve.memset(c8, -1.0e30)
                dve.memset(ys, 0.0)
                dve.memset(gT, 0.0)
                dve.memset(zero, 0.0)
                normalise(2 * l + 1)
                dve.wait_ge(S("logits"), l + 1)
                tt(lg, ps[:, 4, 0:NT * 64].rearrange("p (t e) -> p t e", t=NT)[:, :, 0:GROUPS + EXPERTS],
                   bc(router_b[:, l:l + 1, :], NT, GROUPS + EXPERTS), ALU.add)
                dve.drain()
                cp(c8[:, :, 0:GROUPS], lg[:, :, 0:GROUPS])
                dve.drain()
                for t in range(NT):
                    dve.max(mx[:, t, :], c8[:, t, :])
                dve.drain()
                for t in range(NT):
                    dve.max_index(idx[:, 0, t, :], mx[:, t, :], c8[:, t, :])
                dve.drain()
                cp(sc[:, 2, :], idx[:, 0, :, 0])
                tt(c8[:, :, 0:GROUPS], c8[:, :, 0:GROUPS], bc(mx[:, :, 0:1], NT, GROUPS), ALU.subtract)
                dve.drain()
                for t in range(NT):
                    stt(fine[:, t], bc(iota[:, 0:1, 0:GROUPS], PER_GROUP, GROUPS), sc[:, 2, t:t + 1],
                        lg[:, t, GROUPS:].rearrange("p (g e) -> p e g", g=GROUPS), ALU.is_equal, ALU.mult)
                dve.drain()
                dve.tensor_reduce(fsel, fine, AX.X, ALU.add)
                dve.drain()
                for t in range(NT):
                    dve.max(fmx[:, t, :], fsel[:, t, :])
                dve.drain()
                for t in range(NT):
                    dve.max_index(idx[:, 1, t, :], fmx[:, t, :], fsel[:, t, :])
                tt(sc[:, 1, :], fmx[:, :, 1], fmx[:, :, 0], ALU.subtract)
                dve.drain().then_inc(S("coarse_shifted"), 1)
                cp(sc[:, 4, :], idx[:, 1, :, 0])
                cp(sc[:, 5, :], idx[:, 1, :, 1])
                dve.drain()
                for r in (4, 5):
                    stt(sc[:, r, :], sc[:, 2, :], float(PER_GROUP), sc[:, r, :], ALU.mult, ALU.add)
                dve.drain()
                for r in range(2):
                    for t in range(NT):
                        tsc(pick[:, 2 * r + t, :], iota[:, 0, :], sc[:, 4 + r, t:t + 1], None, ALU.is_equal)
                dve.drain()
                tt(both, pick[:, 0:2, :], pick[:, 2:4, :], ALU.add).then_inc(S("picked"), 1)
                dve.wait_ge(S("gates_exp"), l + 1)
                tsc(sc[:, 6, :], sc[:, 1, :], 1.0, None, ALU.add)
                dve.drain()
                tt(sc[:, 6, :], sc[:, 6, :], sc[:, 0, :], ALU.mult)
                dve.drain()
                dve.reciprocal(sc[:, 7, :], sc[:, 6, :])
                dve.drain()
                tt(sc[:, 8, :], sc[:, 7, :], sc[:, 1, :], ALU.mult)
                dve.wait_ge(S("ranked"), l + 1)
                cp(rank, ps[:, 5, 0:2 * EXPERTS].rearrange("p (t e) -> p t e", t=NT))
                cp(cnt[:, 0, :], ps[:, 5, 2 * EXPERTS:3 * EXPERTS])
                dve.drain()
                tsc(cnt[:, 1, :], cnt[:, 0, :], float(SLOTS), None, ALU.is_gt)
                for k in range(2, T // SLOTS):
                    dve.drain()
                    stt(cnt[:, 1, :], cnt[:, 0, :], float(SLOTS * k), cnt[:, 1, :], ALU.is_gt, ALU.add)
                dve.drain()
                dve.tensor_tensor_scan(cnt[:, 2, :], ones[:, 0:EXPERTS], cnt[:, 1, :], 0.0, ALU.mult, ALU.add)
                dve.drain()
                tt(cnt[:, 3, :], cnt[:, 2, :], cnt[:, 1, :], ALU.subtract)
                tt(prod.rearrange("p (r t) e -> p r t e", r=2), pick.rearrange("p (r t) e -> p r t e", r=2),
                   bc(rank.unsqueeze(1), 2, NT, EXPERTS), ALU.mult)
                dve.drain()
                dve.tensor_reduce(slot[:, 0, :], prod, AX.X, ALU.add)
                dve.drain()
                tt(prod, pick, bc(cnt[:, 3:4, :], 4, EXPERTS), ALU.mult)
                tsc(slot[:, 2, :], slot[:, 0, :], float(SLOTS), None, ALU.is_ge)
                dve.drain()
                dve.tensor_reduce(slot[:, 1, :], prod, AX.X, ALU.add)
                for k in range(2, T // SLOTS):
                    stt(slot[:, 2, :], slot[:, 0, :], float(SLOTS * k), slot[:, 2, :], ALU.is_ge, ALU.add)
                    dve.drain()
                cp(slot[:, 3, :].rearrange("p (r t) -> p r t", r=2), sc[:, 4:6, :])
                tsc(slot[:, 4, :], slot[:, 2, :], 1.0, None, ALU.min)
                stt(slot[:, 5, :], slot[:, 1, :], float(EXPERTS - 1), slot[:, 2, :], ALU.add, ALU.add)
                stt(slot[:, 6, :], slot[:, 2, :], -float(SLOTS), slot[:, 0, :], ALU.mult, ALU.add)
                dve.drain()
                tt(slot[:, 5, :], slot[:, 5, :], slot[:, 3, :], ALU.subtract)
                dve.drain()
                tt(slot[:, 5, :], slot[:, 5, :], slot[:, 4, :], ALU.mult)
                dve.drain()
                tt(slot[:, 5, :], slot[:, 5, :], slot[:, 3, :], ALU.add)
                dve.drain()
                stt(slot[:, 7, :], slot[:, 5, :], float(SLOTS), slot[:, 6, :], ALU.mult, ALU.add)
                tt(lst[0:1], bc(cnt[0:1, 2:3, :], EXTRA_MAX, EXPERTS),
                   bc(iota[0:1, 0, 0:EXTRA_MAX].unsqueeze(2), EXTRA_MAX, EXPERTS), ALU.is_le)
                dve.drain()
                dve.tensor_reduce(lsti[0:1, 0, :], lst[0:1], AX.X, ALU.add)
                dve.drain()
                cp(lsti[0:1, 0, EXTRA_MAX - 1:EXTRA_MAX], cnt[0:1, 2, EXPERTS - 1:EXPERTS])
                dve.drain()
                cp(lists[0:1, l, :], lsti[0:1, 0, :])
                dve.drain().then_inc(S("lists_ready"), 1)

                def select(n):
                    for t in range(NT):
                        tsc(sel[:, t, :], iota[:, 0, :], slot[:, 7, t:t + 1], None, ALU.is_equal)
                    dve.drain()
                    for t in range(NT):
                        i = stt(sel[:, t, :], iota[:, 0, :], slot[:, 7, 2 + t:3 + t], sel[:, t, :], ALU.is_equal,
                                ALU.add)
                    i.then_inc(S(f"sel_ready_l{l}"), 1)

                def select_gated():
                    for t in range(NT):
                        tsc(selg[:, t, :], iota[:].rearrange("p a b -> p (a b)"), slot[:, 7, t:t + 1],
                            sc[:, 7, t:t + 1], ALU.is_equal, ALU.mult)
                        tsc(selt[:, t, :], iota[:].rearrange("p a b -> p (a b)"), slot[:, 7, 2 + t:3 + t],
                            sc[:, 8, t:t + 1], ALU.is_equal, ALU.mult)
                    dve.drain()
                    tt(selg, selg, selt, ALU.add).then_inc(S(f"selg_ready_l{l}"), 1)
                    tsc(slot[:, 7, :], slot[:, 7, :], -float(SLOTS), None, ALU.add)
                    dve.drain()

                def gathered(n):
                    dve.wait_ge(S(f"gathered_l{l}"), n)
                    tt(xg, ps[:, 6, 0:KD * SLOTS].rearrange("p (k s) -> p k s", k=KD),
                       bc(gains[:, 2 * l + 1, :].unsqueeze(2), KD, SLOTS), ALU.mult).then_inc(S(f"xg_ready_l{l}"), 1)
                select(0)
                gathered(1)

                def item(n):
                    dve.wait_ge(S(f"gu_used_l{l}"), n + NW + 1)
                    cp(gus[:, 1, :], ps[:, 5, :]).then_inc(S(f"up_copied_l{l}"), 1)
                    select_gated()
                    select(n)
                    dve.wait_ge(S(f"silu_l{l}"), n + 1)
                    tt(hidT.rearrange("p a b -> p (a b)"), sil.rearrange("p a b -> p (a b)"),
                       ps[:, 7, T + P:T + 2 * P], ALU.mult).then_inc(S(f"hid_ready_l{l}"), 1)
                    gathered(n + 2)
                    dve.wait_ge(S(f"dn_used_l{l}"), n + NW + 1)
                    cp(ys[:, BANK:], ps[:, 5, :]).then_inc(S(f"y1_copied_l{l}"), 1)
                with dve.Fori(0, EXPERTS // NW) as i:
                    for s in range(NW):
                        item(i * NW + s)
                extra = dve.value_load(lists[0:1, l, EXTRA_MAX - 1:EXTRA_MAX], min_val=0, max_val=EXTRA_MAX - 1)
                with dve.If(extra > 0):
                    with dve.Fori(0, extra) as o:
                        item(o + EXPERTS)
                residual(S("moe_summed"), l + 1).then_inc(S("moe_added"), 1)
            moe(0)

            normalise(2)
            dve.wait_ge(S("qk_root"), 1)
            for n, (lo, hi, scale) in enumerate(((0, 8, HD ** -0.5), (8, 10, 1.0))):
                dve.reciprocal(sqs[:, lo:hi, :], sqs[:, lo:hi, :])
                dve.drain()
                tsc(qkv[:, lo:hi, :], qkv[:, lo:hi, :], qk_gain[:, n:n + 1], scale, ALU.mult, ALU.mult)
                dve.drain()
                tt(qkv[:, lo:hi, :], qkv[:, lo:hi, :], sqs[:, lo:hi, :], ALU.mult)
            dve.drain().then_inc(S("qk_normed"), 1)
            dve.wait_ge(S("kv_out"), 1)
            for b in range(2):
                cp(kdup[:, 2 * b:2 * b + 2, :].rearrange("p a t -> p (a t)"), ps[:, b, :])
            cp(vtk.rearrange("p t a b -> p (t a b)"), ps[:, 2, :])
            dve.drain().then_inc(S("att_inputs"), 1)
            dve.sem_inc(S("att_free"), 1)
            slopes = st[:, 4, :]
            for hh in range(4):
                dve.memset(st[:, 4, hh:hh + 1], 2.0 ** (-8.0 * (hh + 1) / ATT_HEADS))
            dve.drain()
            with dve.Fori(0, KV_HEADS) as g:
                for t in range(NT):
                    n_keys = P if t == 0 else 2 * P
                    p_ = pr[:, :, 0:n_keys]
                    dve.wait_ge(S("qk_out"), g * 2 + t + 1)
                    for hh in range(4):
                        stt(pr[:, hh, 0:n_keys], band[:, 2 * P - n_keys:], slopes[:, hh:hh + 1], ps[:, hh, 0:n_keys],
                            ALU.mult, ALU.add)
                    dve.drain()
                    dve.tensor_reduce(st[:, 0, :], p_, AX.X, ALU.max)
                    dve.drain()
                    tt(st[:, 0, :], st[:, 0, :], sinks[:, bass.ds(g * 4, 4)], ALU.max)
                    dve.drain()
                    tsc(st[:, 1, :], st[:, 0, :], -1.0, None, ALU.mult)
                    tt(st[:, 3, :], sinks[:, bass.ds(g * 4, 4)], st[:, 0, :], ALU.subtract)
                    dve.drain().then_inc(S("shifted"), 1)
                    dve.wait_ge(S("exped"), g * 2 + t + 1)
                    tt(st[:, 2, :], st[:, 2, :], st[:, 3, :], ALU.add)
                    dve.drain()
                    dve.reciprocal(st[:, 2, :], st[:, 2, :])
                    dve.drain()
                    tt(p_, p_, bc(st[:, 2, :].unsqueeze(2), 4, n_keys), ALU.mult).then_inc(S("probs"), 1)
                    dve.wait_ge(S("att_out"), g * 2 + t + 1)
                    cp(attT[:, bass.ds(g * 2, 2), t * P:(t + 1) * P],
                       ps[:, 6, 0:2 * P].rearrange("p (a b) -> p a b", a=2)).then_inc(S("att_taken"), 1)
                tsc(slopes, slopes, 0.25, None, ALU.mult)
                dve.drain().then_inc(S("att_free"), 1)
            residual(S("projected_out"), 3).then_inc(S("h_mixed"), 1)
            moe(1)


PARAM_LOADS = 42


def kernel(**inputs):
    import numpy as np
    import concourse.bacc as bacc
    from concourse.bass_utils import run_bass_kernel_spmd

    nc = bacc.Bacc("TRN2", target_bir_lowering=False, num_devices=1)
    arrays, args = {}, {}
    for name, value in inputs.items():
        array = np.ascontiguousarray(value)
        arrays[f"in_{name}"] = array
        args[name] = nc.dram_tensor(f"in_{name}", array.shape, mybir.dt.from_np(array.dtype), kind="ExternalInput").ap()
    out = nc.dram_tensor("out_h", inputs["x"].shape, F32, kind="ExternalOutput").ap()
    trunk(nc, args, out)
    result = run_bass_kernel_spmd(nc, [arrays], core_ids=[0])
    return result.results[0]["out_h"]
```

```python
from contextlib import ExitStack

import concourse.bass as bass
from concourse import mybir

P = 128
F32 = mybir.dt.float32
I32 = mybir.dt.int32
U32 = mybir.dt.uint32
ALU = mybir.AluOpType
ACT = mybir.ActivationFunctionType
AX = mybir.AxisListType

D = 1024
T = 256
NT = T // P
KD = D // P
BANK = 512
NORM_EPS = 1e-6

SSD_INNER = 1024
SSD_STATE = 128
SSD_GROUPS = 4
SSD_HEADS = 16
HPG = SSD_HEADS // SSD_GROUPS
CONV_DIM = SSD_INNER + 2 * SSD_GROUPS * SSD_STATE
CONV_TAPS = 4
RWKV_TILES = 26
HD = 64
GN_EPS = 64e-5
DECAY_FACTOR = 0.6065306597126334

ATT_HEADS = 16
KV_HEADS = 4
OUT_OF_BAND = -1.0e30

EXPERTS = 32
GROUPS = 4
PER_GROUP = 8
HIDDEN = 512
KH = HIDDEN // P
SLOTS = 32
EXTRA_BLOCKS = T // SLOTS - 1
EXTRA_MAX = 16
BLOCK = KD * HIDDEN
BLOCKS = 8
TURNS = 3 * EXPERTS // BLOCKS

COLS = 256
RING = 4
Z_CHUNKS = SSD_INNER // COLS
CONV_CHUNKS = CONV_DIM // COLS
RWKV_CHUNKS = RWKV_TILES * P // COLS
DT_COL = SSD_INNER + CONV_DIM
RWKV_COL = DT_COL + SSD_HEADS
ODD_CHUNKS = 6
TILES_PER_RING = RING * COLS // P


class Arena:

    def __init__(self, tensor, size, start=0):
        self.tensor, self.size, self.at = tensor, size, start

    def take(self, *dims):
        n = 1
        for d in dims:
            n *= d
        view = self.tensor[:, self.at:self.at + n]
        self.at += n
        assert self.at <= self.size, self.at
        if len(dims) == 2:
            view = view.rearrange("p (a b) -> p a b", b=dims[1])
        elif len(dims) == 3:
            view = view.rearrange("p (a b c) -> p a b c", b=dims[1], c=dims[2])
        elif len(dims) == 4:
            view = view.rearrange("p (a b c d) -> p a b c d", b=dims[1], c=dims[2], d=dims[3])
        return view


def half_blocks(x, n, side):
    return x.rearrange("p (b r t) -> p b r t", r=2, t=2 << n)[:, :, side, :]


def bc(ap, *shape):
    return ap.to_broadcast([ap.shape[0], *shape])


def trunk(nc, a, out):
    with ExitStack() as ctx:
        def sb(name, shape, dt=F32):
            return ctx.enter_context(nc.sbuf_tensor(name, shape, dt))

        sems = {}

        def S(name):
            if name not in sems:
                sems[name] = ctx.enter_context(nc.semaphore(name))
            return sems[name]

        h = sb("h", [P, NT, D])
        ident = sb("ident", [P, P])
        head_sum = sb("head_sum", [P, P])
        head_mean = sb("head_mean", [P, P])
        ones = sb("ones", [P, P])
        group_mean = sb("group_mean", [P, P])
        upper = sb("upper", [P, P])
        upper_strict = sb("upper_strict", [P, P])
        head_pick = sb("head_pick", [P, 10, 32])
        head_spread = sb("head_spread", [P, 10, P])
        lengths = sb("lengths", [P, T])
        iota128 = sb("iota128", [P, P])
        steps = sb("steps", [P, EXTRA_BLOCKS])
        fold = sb("fold", [P, SLOTS])
        dup_even = sb("dup_even", [P, P])
        dup_odd = sb("dup_odd", [P, P])
        mask_ar = sb("mask_ar", [P, 2, P])
        mask_level = sb("mask_level", [P, 6, P])
        mask_level_t = sb("mask_level_t", [P, 6, P])
        mask_pair = sb("mask_pair", [P, P])
        band = sb("band", [P, 2 * P])
        par = sb("par", [P, 2, P])
        gains = sb("gains", [P, 4, KD])
        router_w = sb("router_w", [P, 2, KD, GROUPS + EXPERTS])
        router_b = sb("router_b", [P, 2, GROUPS + EXPERTS])
        dt_bias = sb("dt_bias", [P, SSD_HEADS])
        a_log = sb("a_log", [P, SSD_HEADS])
        d_skip = sb("d_skip", [P, KD])
        sinks = sb("sinks", [P, ATT_HEADS])
        qk_gain = sb("qk_gain", [P, 2])
        eps = sb("eps", [P, 2])
        preloaded = sb("preloaded", [P, 1])
        ss = sb("ss", [P, NT])
        rstd = sb("rstd", [P, NT])
        lists = sb("lists", [1, 2, EXTRA_MAX], I32)

        ARENA = 44688
        arena = sb("arena", [P, ARENA])
        ps = ctx.enter_context(nc.psum_tensor("ps", [P, 8, BANK], F32))

        m0 = Arena(arena, 6 * BLOCK)
        hnT = m0.take(KD, T)
        ring = m0.take(RING, KD, COLS)
        zs = m0.take(KD, T)
        u = m0.take(RWKV_TILES, T)
        dec_at = m0.at
        dec = m0.take(KD, T)
        agate = m0.take(KD, T)
        e2 = [m0.take(NT, P) for _ in range(2)]
        kp = [m0.take(T) for _ in range(2)]
        tmp = [m0.take(T) for _ in range(2)]
        m0 = Arena(arena, ARENA, 6 * BLOCK)
        gate = m0.take(KD, T)
        mixT = m0.take(2 * KD, T)
        xbc_at = m0.at
        xbc = m0.take(CONV_DIM // P, T)
        work = m0.at
        hn = Arena(arena, ARENA, work).take(NT, D)
        wdt = Arena(arena, ARENA, work + NT * D).take(KD, SSD_HEADS)
        rows = Arena(arena, ARENA, work + NT * D + P).take(2, P)
        cbuf = Arena(arena, ARENA, work + NT * D + 3 * P).take(4, T)
        CW, CB, NW_, MU = 0, 64, 80, 88
        W0, A0, KK, KA, RK, LNW, LNB = (8 * i for i in range(7))

        s0 = Arena(arena, ARENA, work)
        btok = s0.take(P)
        xdt = s0.take(NT, HPG, HD)
        xst = s0.take(HPG, HD)
        tria = s0.take(NT, HPG, P)
        mm = s0.take(NT, HPG, P)
        cbm = s0.take(NT, P)
        cs = s0.take(HPG, P)
        state = s0.take(HPG, HD)
        sy = s0.take(2, T)
        ssq = s0.take(2, T)
        sr = s0.take(T)
        dtp = s0.take(8, NT, SSD_HEADS)
        kraw_at = s0.at
        lora_w = s0.take(3, D)
        s0 = Arena(arena, ARENA, kraw_at)
        kraw = s0.take(KD, T)
        ksq = s0.take(KD, T)

        rh = Arena(arena, KD * T)
        ra = Arena(arena, KD * T + RING * KD * COLS, KD * T)
        rb = Arena(arena, ARENA, work)
        kar = [rb.take(2, NT, 2, P) for _ in range(2)]
        bar = [rb.take(2, NT, 2, P) for _ in range(2)]
        X = [rb.take(NT * 2, P) for _ in range(2)]
        XT = [rb.take(NT * 2, P) for _ in range(2)]
        TX = [rb.take(NT * 2, P) for _ in range(2)]
        vtok = [rb.take(NT, P) for _ in range(2)]
        ktok = [rb.take(P) for _ in range(2)]
        btk = [rb.take(P) for _ in range(2)]
        ar = [x.take(NT, 2, P) for x in (rh, rh, ra, ra)]
        kt = [x.take(NT, P) for x in (rh, rh, ra, ra)]
        bt = [x.take(NT, P) for x in (rh, rh, ra, ra)]
        edge = [rb.take(8) for _ in range(4)]
        cum = [rb.take(NT, P + 1) for _ in range(2)]
        e1 = [rb.take(NT, P + 1) for _ in range(2)]
        rhs = [ra.take(2, NT, HD) for _ in range(2)]
        us = [ra.take(2, NT, HD) for _ in range(2)]
        s0T = [ra.take(HD) for _ in range(2)]
        kk = zs
        bonus = Arena(arena, ARENA, xbc_at).take(KD, T)
        tmp8 = Arena(arena, ARENA, xbc_at + KD * T).take(KD, T)
        rv = u[:, 0:KD, :]
        kv_ = u[:, KD:2 * KD, :]
        vv = u[:, 2 * KD:3 * KD, :]
        wo_ssd = [Arena(arena, 6 * BLOCK, at).take(KD // 2, D) for at in (ra.at, dec_at)]
        wo_rwkv = Arena(arena, ARENA, work).take(KD, D)

        SPARE = ARENA - 2 * BLOCK
        places = [i * BLOCK for i in range(6)] + [SPARE, SPARE + BLOCK]
        w_up = [Arena(arena, ARENA, at).take(KD, HIDDEN) for at in places]
        w_down = [Arena(arena, ARENA, at).take(KH, D) for at in places]
        order = ((0, 1, 2, 3, 4, 5, 6, 7), (2, 3, 6, 7, 4, 5, 0, 1))
        mo = Arena(arena, SPARE, 6 * BLOCK)
        hf = mo.take(NT, D)
        hfT = mo.take(KD, T)
        gus = mo.take(2, HIDDEN)
        ys = mo.take(D)
        zero = mo.take(BANK)
        xg = mo.take(KD, P)
        hidT = mo.take(KH, SLOTS)
        sil = mo.take(KH, SLOTS)
        sel = mo.take(NT, P)
        selw = mo.take(NT, P)
        selg = mo.take(NT, P)
        selt = mo.take(NT, P)
        gT = mo.take(NT, P)
        lgT = xg.rearrange("p a b -> p (a b)")[:, 0:2 * T].rearrange("p (a t) -> p a t", a=2)
        lg = mo.take(NT, GROUPS + EXPERTS)
        c8 = mo.take(NT, 8)
        mx = mo.take(NT, 8)
        fine = mo.take(NT, PER_GROUP, GROUPS)
        fsel = mo.take(NT, 8)
        fmx = mo.take(NT, 8)
        sc = mo.take(16, NT)
        pick = mo.take(4, EXPERTS)
        both = mo.take(NT, EXPERTS)
        rank = mo.take(NT, EXPERTS)
        cnt = mo.take(6, EXPERTS)
        prod = mo.take(4, EXPERTS)
        slot = mo.take(12, 4)
        above = mo.take(EXPERTS, EXTRA_BLOCKS)
        lst = mo.take(EXTRA_MAX, EXPERTS)
        lsti = mo.take(2, EXTRA_MAX)
        idx = sb("idx", [P, 2, NT, 8], U32)

        m1 = Arena(arena, SPARE, 6 * BLOCK)
        hnT1 = m1.take(KD, T)
        qkv = m1.take(12, T)
        kdup = m1.take(KV_HEADS, T)
        vtk = m1.take(NT, 2, P)
        attT = m1.take(KD, T)
        pr = [m1.take(4, 2 * P) for _ in range(2)]
        pT = m1.take(4, 2, P)
        st = [m1.take(8, 4) for _ in range(2)]
        ring1 = Arena(arena, ARENA).take(RING, KD, COLS)
        wo_att = Arena(arena, ARENA).take(KD, D)
        m1b = Arena(arena, 6 * BLOCK, 4 * BLOCK)
        hn1 = m1b.take(NT, D)
        sqs = m1b.take(12, T)

        block = ctx.enter_context(nc.Block())

        @block.sync
        def _(sp):
            sp.dma_start(h[:], a["x"].rearrange("b (t p) d -> p (b t) d", p=P)).then_inc(S("x_loaded"), 16)
            for i, (name, l) in enumerate((("ln_mix", 0), ("ln_ffn", 0), ("ln_mix", 1), ("ln_ffn", 1))):
                sp.dma_start(gains[:, i, :], a[name][l].rearrange("(p k) -> p k", k=KD)).then_inc(
                    S("gains_loaded"), 16)
            w_in = a["e_w_in"][0].rearrange("(p k) c -> p k c", k=KD)

            def chunk(s, col):
                sp.dma_start(ring[:, s], w_in[:, :, bass.ds(col, COLS)]).then_inc(S(f"ring_loaded{s}"), 16)
            for s in range(Z_CHUNKS):
                chunk(s, s * COLS)
            n = 0

            def small(dst, src):
                nonlocal n
                sp.dma_start(dst, src, allow_slow_non_contiguous=True).then_inc(S("params_loaded"), 16)
                n += 1
            row = lambda ap: ap.rearrange("(r f) -> r f", f=P)
            small(rows[0:64, 0, :], a["ssd_conv_w"][0].rearrange("t (j f) -> (t j) f", f=P))
            small(rows[64:80, 0, :], row(a["ssd_conv_b"][0]))
            small(rows[80:88, 0, :], row(a["ssd_norm"][0]))
            small(rows[88:114, 0, :], row(a["rwkv_mu"][0]))
            for i, name in enumerate(("rwkv_w0", "rwkv_a0", "rwkv_k_k", "rwkv_k_a")):
                small(rows[8 * i:8 * i + 8, 1, :], row(a[name][0]))
            small(rows[32:40, 1, :], a["rwkv_r_k"][0].rearrange("(r b) f -> r (b f)", b=2))
            small(rows[40:48, 1, :], row(a["rwkv_ln_w"][0]))
            small(rows[48:56, 1, :], row(a["rwkv_ln_b"][0]))
            for l in range(2):
                small(router_w[:, l, :, 0:GROUPS], a["moe_w_coarse"][l].rearrange("(p k) e -> p k e", k=KD))
                for g in range(GROUPS):
                    small(router_w[:, l, :, GROUPS + 8 * g:GROUPS + 8 * g + 8],
                          a["moe_w_fine"][l, g].rearrange("(p k) e -> p k e", k=KD))
                small(router_b[:, l, 0:GROUPS], a["moe_b_coarse"][l].partition_broadcast(P))
                small(router_b[:, l, GROUPS:], a["moe_b_fine"][l].rearrange("g e -> (g e)").partition_broadcast(P))
            small(dt_bias[:], a["ssd_dt_bias"][0].partition_broadcast(P))
            small(a_log[:], a["ssd_a_log"][0].partition_broadcast(P))
            small(sinks[:], a["attn_sinks"][0].partition_broadcast(P))
            for half in range(2):
                small(d_skip[64 * half:64 * half + 64, :],
                      a["ssd_d"][0].rearrange("(j e) -> e j", e=2)[half].partition_broadcast(64))
                small(qk_gain[64 * half:64 * half + 64, 0:1], a["attn_q_norm"][0].rearrange("(p k) -> p k", k=1))
                small(qk_gain[64 * half:64 * half + 64, 1:2], a["attn_k_norm"][0].rearrange("(p k) -> p k", k=1))
            small(wdt, a["e_w_in"][0].rearrange("(p k) c -> p k c", k=KD)[:, :, DT_COL:RWKV_COL])
            small(lora_w[0:64, 0, :], a["rwkv_w2"][0])
            small(lora_w[64:128, 1, :], a["rwkv_a2"][0])
            small(lora_w[:, 2, :], a["rwkv_g2"][0])
            assert n == PARAM_LOADS, n

            with sp.Fori(0, CONV_CHUNKS // RING) as i:
                for s in range(RING):
                    sp.wait_ge(S("projected"), 2 * (i * RING + s) + 2)
                    chunk(s, (i * RING + Z_CHUNKS + s) * COLS)
            sp.wait_ge(S("projected"), 2 * CONV_CHUNKS + 2)
            chunk(0, (RWKV_CHUNKS - 1) * COLS + RWKV_COL)
            with sp.Fori(0, RWKV_CHUNKS // RING) as i:
                for c in range(RING):
                    sp.wait_ge(S("projected"), 2 * (i * RING + CONV_CHUNKS + c + 1) + 2)
                    chunk((c + 1) % RING, (i * RING + c) * COLS + RWKV_COL)

            def out_rows(dst, w, first, loaded):
                sp.dma_start(dst, w.rearrange("(j p) d -> p j d", p=P)[:, first:first + KD // 2]
                             ).then_inc(loaded, 16)

            def out_weights(dst, w, first):
                for half in range(2):
                    q = slice(half * KD // 2, (half + 1) * KD // 2)
                    out_rows(dst[:, q, :], w, first + half * KD // 2, S(f"wo_loaded{half}"))
            sp.wait_ge(S("projected"), 2 * (Z_CHUNKS + CONV_CHUNKS + RWKV_CHUNKS))
            out_rows(wo_ssd[0], a["e_w_out"][0], 0, S("wo_ssd_loaded0"))
            for w in range(2):
                sp.wait_ge(S(f"decayed{w}"), KD // 2)
            out_rows(wo_ssd[1], a["e_w_out"][0], KD // 2, S("wo_ssd_loaded1"))
            for w in range(2):
                sp.wait_ge(S(f"solved{w}"), KD // 2 + 1)
            out_weights(wo_rwkv, a["e_w_out"][0], KD)

            def load(l, which, e, place, loaded):
                if which < 2:
                    w = a[("moe_w_gate", "moe_w_up")[which]][l].rearrange("e (p k) f -> e p k f", k=KD)
                    sp.dma_start(w_up[place], w[bass.ds(e, 1)]).then_inc(loaded, 16)
                else:
                    w = a["moe_w_down"][l].rearrange("e (p k) d -> e p k d", k=KH)
                    sp.dma_start(w_down[place], w[bass.ds(e, 1)]).then_inc(loaded, 16)

            def first_blocks(l, first, count):
                for b in range(first, first + count):
                    load(l, b % 3, b // 3, order[l][b], S(f"block_loaded{order[l][b]}"))

            def other_blocks(l):
                used = [S(f"{name}_l{l}") for name in ("gate_out", "gu_used", "dn_used")]

                def block(i, b):
                    place = order[l][b % BLOCKS]
                    sp.wait_ge(used[(b - BLOCKS) % 3], i * BLOCKS + ((b - BLOCKS) // 3 + 1))
                    load(l, b % 3, i * BLOCKS + b // 3, place, S(f"block_loaded{place}"))
                with sp.Fori(0, TURNS // 3 - 1) as i:
                    for b in range(BLOCKS, 4 * BLOCKS):
                        block(i, b)
                for b in range(3 * EXPERTS - 2 * BLOCKS, 3 * EXPERTS):
                    block(0, b)

            def extra_experts(l):
                sp.wait_ge(S("lists_ready"), l + 1)
                extra = sp.value_load(lists[0:1, l, EXTRA_MAX - 1:EXTRA_MAX], min_val=0, max_val=EXTRA_MAX - 1)
                with sp.If(extra > 0):
                    with sp.Fori(0, extra) as o:
                        e = sp.value_load(lists[0:1, l, bass.ds(o, 1)], min_val=0, max_val=EXPERTS - 1)
                        sp.wait_ge(S(f"dn_used_l{l}"), o + EXPERTS)
                        for which in range(3):
                            load(l, which, e, order[l][5 + which], S(f"extra_loaded_l{l}"))
            sp.wait_ge(S("projected_out"), 1)
            first_blocks(0, 0, 6)
            sp.wait_ge(S("projected_out"), 2)
            first_blocks(0, 6, 2)
            other_blocks(0)

            w_odd = a["o_w_in"][0].rearrange("(p k) c -> p k c", k=KD)
            for c in range(ODD_CHUNKS):
                if c % 2 == 0 and c < RING:
                    b = 3 * EXPERTS - BLOCKS + c // 2
                    sp.wait_ge(S(f"{('gate_out', 'gu_used', 'dn_used')[b % 3]}_l0"), b // 3 + 1)
                if c == RING:
                    extra_experts(0)
                    sp.wait_ge(S("moe_added"), NT)
                    first_blocks(1, 0, 4)
                if c >= RING:
                    sp.wait_ge(S("qkv_ready"), 2 * (c - RING) + 2)
                sp.dma_start(ring1[:, c % RING], w_odd[:, :, c * COLS:(c + 1) * COLS]).then_inc(
                    S(f"ring_loaded{c % RING}"), 16)
            sp.wait_ge(S("qkv_ready"), 2 * ODD_CHUNKS)
            out_weights(wo_att, a["o_w_out"][0], 0)
            sp.wait_ge(S("qk_normed"), 1)
            first_blocks(1, 4, 2)
            sp.wait_ge(S("projected_out"), 3)
            first_blocks(1, 6, 2)
            other_blocks(1)
            extra_experts(1)
            for t in range(NT):
                sp.wait_ge(S("moe_added"), NT + t + 1)
                sp.dma_start(out.rearrange("b (t p) d -> p (b t) d", p=P)[:, t], h[:, t, :]).then_inc(S("stored"), 16)
            sp.wait_ge(S("stored"), 16 * NT)

        @block.gpsimd
        def _(pool):
            pool.memset(eps[:, 0:1], NORM_EPS)
            pool.memset(eps[:, 1:2], GN_EPS)
            pool.memset(ident[:], 1.0)
            pool.drain()
            pool.affine_select(ident[:], ident[:], [[1, P]], ALU.is_equal, 0.0, base=0, channel_multiplier=-1)
            pool.drain().then_inc(S("ident_ready"), 1)
            for t, v in ((ones, 1.0), (head_sum, 0.0), (head_mean, 0.0), (group_mean, 1.0 / 256),
                         (upper, 1.0), (upper_strict, 1.0), (mask_level, 0.0), (mask_level_t, 0.0),
                         (mask_pair, 0.0), (mask_ar, 1.0),
                         (head_pick, 1.0), (head_spread, 1.0)):
                pool.memset(t[:], v)
            pool.drain()
            for half in range(2):
                q = slice(64 * half, 64 * half + 64)
                pool.memset(head_sum[q, q], 1.0)
                pool.memset(head_mean[q, q], 1.0 / HD)
            pool.drain()
            for half in range(2):
                q = slice(64 * half, 64 * half + 64)
                pool.affine_select(head_pick[q], head_pick[q], [[-2, 10], [1, 32]], ALU.is_equal, 0.0, base=-half,
                                   channel_multiplier=0)
            pool.drain()
            for b in range(3):
                v = head_spread[:, 4 * b:min(4 * b + 4, 10), :].rearrange("p q (a f) -> p q a f", a=2)
                pool.affine_select(v, v, [[-34, v.shape[1]], [-1, 2], [0, HD]], ALU.is_equal, 0.0, base=-8 * b,
                                   channel_multiplier=1)
            pool.iota(steps[:], [[SLOTS, EXTRA_BLOCKS]], base=SLOTS, channel_multiplier=0,
                      allow_small_or_imprecise_dtypes=True)
            pool.drain()
            pool.iota(iota128[:], [[1, P]], base=0, channel_multiplier=0, allow_small_or_imprecise_dtypes=True)
            pool.drain()
            pool.affine_select(upper[:], upper[:], [[1, P]], ALU.is_ge, 0.0, base=0, channel_multiplier=-1)
            pool.affine_select(upper_strict[:], upper_strict[:], [[1, P]], ALU.is_gt, 0.0, base=0,
                               channel_multiplier=-1)
            pool.affine_select(mask_ar[:, 0, :], mask_ar[:, 0, :], [[1, P]], ALU.is_gt, 0.0, base=0,
                               channel_multiplier=-1)
            pool.affine_select(mask_ar[:, 1, :], mask_ar[:, 1, :], [[1, P]], ALU.is_ge, 0.0, base=0,
                               channel_multiplier=-1)
            pair = mask_pair[:].rearrange("p (b r) -> p b r", r=2)[:, :, 1:2]
            pool.affine_select(pair, bc(ones[:, 0:1].unsqueeze(2), P // 2, 1), [[2, P // 2], [0, 1]], ALU.is_equal, 0.0,
                               base=0, channel_multiplier=-1)
            for n in range(6):
                m = 2 << n
                v = mask_level[:, n, :].rearrange("p (b r) -> p b r", r=2 * m)[:, :, 0:m]
                one = bc(ones[:, 0:1].unsqueeze(2), P // (2 * m), m)
                pool.affine_select(v, one, [[-2 * m, P // (2 * m)], [0, m]], ALU.is_ge, 0.0, base=-m,
                                   channel_multiplier=1)
                pool.drain()
                pool.affine_select(v, v, [[2 * m, P // (2 * m)], [0, m]], ALU.is_ge, 0.0, base=2 * m - 1,
                                   channel_multiplier=-1)
                v = mask_level_t[:, n, :].rearrange("p (b r) -> p b r", r=2 * m)[:, :, m:2 * m]
                pool.affine_select(v, one, [[-2 * m, P // (2 * m)], [0, m]], ALU.is_ge, 0.0, base=0,
                                   channel_multiplier=1)
                pool.drain()
                pool.affine_select(v, v, [[2 * m, P // (2 * m)], [0, m]], ALU.is_ge, 0.0, base=m - 1,
                                   channel_multiplier=-1)
            pool.iota(band[:], [[1, 2 * P]], base=-P, channel_multiplier=-1, allow_small_or_imprecise_dtypes=True)
            pool.drain()
            pool.affine_select(band[:], band[:], [[-1, 2 * P]], ALU.is_ge, OUT_OF_BAND, base=P, channel_multiplier=1)
            pool.drain()
            pool.affine_select(band[:], band[:], [[1, 2 * P]], ALU.is_gt, OUT_OF_BAND, base=0, channel_multiplier=-1)
            pool.drain()
            for dup, half in ((dup_even, 0), (dup_odd, 1)):
                for to in range(2):
                    pool.tensor_copy(dup[:, 64 * to:64 * to + 64], ident[:, 64 * half:64 * half + 64])
            pool.drain().then_inc(S("consts_ready"), 1)

            pool.wait_ge(S("ssd_out"), SSD_GROUPS)
            for x in (kar[0], kar[1], bar[0]):
                pool.memset(x, 0.0)
            pool.wait_ge(S("kk_ready"), 1)
            for x in (bar[1], TX[0], TX[1]):
                pool.memset(x, 0.0)
            for pair in range(KD // 2):
                for w in range(2):
                    pool.wait_ge(S(f"solved{w}"), pair + 1)
                    pool.tensor_copy(XT[w], bc(ident[:].unsqueeze(1), 4, P)).then_inc(S(f"x_reset{w}"), 1)

        @block.tensor
        def _(pe):
            def transposes(n):
                src = (hn, None, hn1)[n]
                pe.wait_ge(S("hn_ready"), n + 1)
                for b in range(4):
                    for q in range(4):
                        k, t = (4 * b + q) // NT, q % NT
                        i = pe.transpose(ps[:, b, q * P:(q + 1) * P],
                                         src[:, t, :].rearrange("p (f k) -> p k f", k=KD)[:, k, :], ident[:])
                    i.then_inc(S("hn_turned"), 1)
                pe.wait_ge(S("hnT_ready"), n + 1)

            def transposes_before_moe(n):
                for t in range(NT):
                    pe.wait_ge(S("h_mixed"), n - 1 + t + 1)
                    for k in range(KD):
                        i = pe.transpose(ps[:, 4 + k // 2, (k % 2) * T + t * P:(k % 2) * T + (t + 1) * P],
                                         h[:, t, :].rearrange("p (f k) -> p k f", k=KD)[:, k, :], ident[:])
                        if t and k % 2:
                            i.then_inc(S("hn_turned"), 1)
                pe.wait_ge(S("hnT_ready"), n + 1)

            pe.wait_ge(S("ident_ready"), 1)
            transposes(0)

            def project(s, half, done, w=ring, x=hnT):
                b = 2 * s + half
                for k in range(KD):
                    i = pe.matmul(ps[:, b, 0:T], w[:, s, k, half * P:(half + 1) * P], x[:, k, :],
                                  start=(k == 0), stop=(k == KD - 1))
                i.then_inc(done, 1)
            for s in range(RING):
                pe.wait_ge(S(f"ring_loaded{s}"), 16)
                for half in range(2):
                    project(s, half, S("projected"))
            pe.wait_ge(S("z_done"), 2 * Z_CHUNKS)
            pe.wait_ge(S("params_loaded"), 16 * PARAM_LOADS)
            pe.transpose(ps[:, 7, 0:114], rows[0:114, 0, :], ident[0:114, 0:114])
            pe.transpose(ps[:, 7, P:P + 56], rows[0:56, 1, :], ident[0:56, 0:56]).then_inc(S("par_turned"), 1)
            for t in range(NT):
                for k in range(KD):
                    i = pe.matmul(ps[:, 6, t * SSD_HEADS:(t + 1) * SSD_HEADS], hnT[:, k, t * P:(t + 1) * P],
                                  wdt[:, k, :], start=(k == 0), stop=(k == KD - 1))
            i.then_inc(S("dt_ready"), 1)
            pe.wait_ge(S("dt_abs"), 1)
            pe.wait_ge(S("consts_ready"), 1)
            with pe.Fori(0, CONV_CHUNKS // RING) as i:
                for s in range(RING):
                    pe.wait_ge(S(f"ring_loaded{s}"), i * 16 + 32)
                    for half in range(2):
                        pe.wait_ge(S("conv_done"), i * TILES_PER_RING + 2 * s + half + 1)
                        project(s, half, S("projected"))
            def rwkv_tiles(n, count):
                for n in range(n, n + count):
                    q = Z_CHUNKS + CONV_CHUNKS + n // 2
                    if n % 2 == 0:
                        pe.wait_ge(S(f"ring_loaded{q % RING}"), 16 * (q // RING + 1))
                    pe.wait_ge(S("conv_done"), 8 + (16 + n - 1 if n >= 2 else 8 + n + 1))
                    for k in range(KD):
                        i = pe.matmul(ps[:, n % 2, 0:T], ring[:, q % RING, k, n % 2 * P:(n % 2 + 1) * P], hnT[:, k, :],
                                      start=(k == 0), stop=(k == KD - 1))
                    i.then_inc(S("projected"), 1)
            rwkv_tiles(0, 2)

            pe.wait_ge(S("conv_done"), 8 + CONV_DIM // P)
            pe.wait_ge(S("adt_ready"), 1)
            for c in range(NT):
                pe.matmul(ps[:, 7, c * SSD_HEADS:(c + 1) * SSD_HEADS], upper[:], dtp[:, 1, c, :], start=True, stop=True)
                i = pe.matmul(ps[:, 7, (NT + c) * SSD_HEADS:(NT + c + 1) * SSD_HEADS], ones[:], dtp[:, 1, c, :],
                              start=True, stop=True)
            i.then_inc(S("acum_ready"), 1)

            def ssd_turn(g):
                for c in range(NT):
                    for t in range(2):
                        pe.transpose(ps[:, 2, (2 * c + t) * P:(2 * c + t + 1) * P],
                                     xbc[:, 2 * g + t, c * P:(c + 1) * P], ident[:])
                pe.transpose(ps[:, 3, 0:P], xbc[:, 8 + g, 0:P], ident[:])
                for c in range(NT):
                    q = slice(c * P, (c + 1) * P)
                    i = pe.matmul(ps[:, 3, (c + 1) * P:(c + 2) * P], xbc[:, 8 + g, q], xbc[:, 12 + g, q],
                                  start=True, stop=True)
                i.then_inc(S("ssd_turned"), 1)

            def ssd_cumulate(g):
                pe.wait_ge(S("ssd_tria"), g + 1)
                for c in range(NT):
                    i = pe.matmul(ps[:, 4 + c, :], ones[:], tria[:, c].rearrange("p a b -> p (a b)"),
                                  start=True, stop=True)
                i.then_inc(S("ssd_cumulated"), 1)

            pe.wait_ge(S("silu_done"), 4 + CONV_DIM // P)
            ssd_turn(0)
            ssd_cumulate(0)

            pe.wait_ge(S("lora_ready"), 1)
            n = 0
            for kind, (lo, hi, src) in enumerate(((0, 64, 24), (64, 128, 24), (0, 128, 25))):
                for j in range(0, KD, 2):
                    if n >= 2:
                        pe.wait_ge(S("lora_taken"), n - 1)
                    for half in range(2):
                        i = pe.matmul(ps[:, n % 2, half * T:(half + 1) * T],
                                      lora_w[lo:hi, kind, (j + half) * P:(j + half + 1) * P], u[lo:hi, src, :],
                                      start=True, stop=True)
                    i.then_inc(S("lora_out"), 1)
                    n += 1
            pe.wait_ge(S("lora_taken"), 12)

            def per_head_sums(src, tiles, bank):
                for j in range(tiles):
                    q = slice(32 * (j % 4), 32 * (j % 4) + 32)
                    i = pe.matmul(ps[q, bank, 0:T], head_pick[:, j, :], src[:, j, :], start=(j < 4),
                                  stop=(j + 4 >= tiles), skip_group_check=True)
                return i

            def per_head_spread(tiles, banks):
                for n, j in enumerate(tiles):
                    i = pe.matmul(ps[:, banks + n // 2, (n % 2) * T:(n % 2 + 1) * T], head_spread[:, j, :], lengths[:],
                                  start=True, stop=True)
                return i

            for g in range(SSD_GROUPS):
                last = g == SSD_GROUPS - 1
                rwkv_tiles(2 + 6 * g, 2)
                pe.wait_ge(S("ssd_scaled"), g + 1)
                pe.matmul(ps[:, 3, 0:HPG * HD], btok, xst.rearrange("p a b -> p (a b)"), start=True,
                          stop=True).then_inc(S("ssd_state"), 1)
                rwkv_tiles(4 + 6 * g, 1)
                pe.wait_ge(S("ssd_weighted"), g + 1)
                for c in range(NT):
                    for hh, part in ((2 * a + b, part) for a in range(2) for part in range(1 + c) for b in range(2)):
                        t, half = hh // 2, hh % 2
                        x, y = ((xdt[:, c, hh, :], mm[:, c, hh, :]), (state[:, hh, :], cs[:, hh, :]))[part]
                        i = pe.matmul(ps[64 * half:64 * half + 64, 6, t * T + c * P:t * T + (c + 1) * P], x, y,
                                      start=part == 0, stop=part == c, skip_group_check=True)
                i.then_inc(S("ssd_out"), 1)
                if last:
                    pe.wait_ge(S("heads_squared"), 1)
                    per_head_sums(ksq, KD, 2).then_inc(S("head_products"), 1)
                else:
                    ssd_turn(g + 1)
                rwkv_tiles(5 + 6 * g, 1)
                pe.wait_ge(S("ssd_squared"), g + 1)
                for t in range(2):
                    i = pe.matmul(ps[:, 7, 0:T], group_mean[:], ssq[:, t, :], start=(t == 0), stop=(t == 1))
                i.then_inc(S("ssd_mean"), 1)
                rwkv_tiles(6 + 6 * g, 1)
                if last:
                    pe.wait_ge(S("lengths_inverse"), 1)
                    per_head_spread(range(KD), 2).then_inc(S("head_products"), 1)
                rwkv_tiles(7 + 6 * g, 1)
                if not last:
                    ssd_cumulate(g + 1)

            def project_out(src, w, first=False, last=False, part=range(KD // 2)):
                for j in part:
                    for t in range(NT):
                        for cols in range(2):
                            i = pe.matmul(ps[:, 2 * t + cols, :], src[:, j, t * P:(t + 1) * P],
                                          w[:, j, cols * BANK:(cols + 1) * BANK], start=(first and j == 0),
                                          stop=(last and j == KD // 2 - 1))
                return i

            for pair in range(KD // 2):
                for w in range(2):
                    j, b0 = 2 * pair + w, 4 * w
                    n4 = j % 4
                    pe.wait_ge(S(f"solved{w}"), pair + 1)
                    pe.wait_ge(S(f"decayed{w}"), pair + 1)
                    pe.matmul(ps[:, b0 + 3, 0:T], head_sum[:], tmp[w], start=True, stop=True).then_inc(
                        S(f"tok_turned{w}"), 1)
                    for c in range(NT):
                        pe.transpose(ps[:, b0 + 2, c * P:(c + 1) * P], vv[:, j, c * P:(c + 1) * P], ident[:])
                    pe.transpose(ps[:, b0 + 2, 2 * P:3 * P], kt[n4][:, 0, :], ident[:])
                    pe.transpose(ps[:, b0 + 2, 3 * P:4 * P], bt[n4][:, 0, :], ident[:]).then_inc(
                        S(f"tok_turned{w}"), 1)
                for w in range(2):
                    j, b0 = 2 * pair + w, 4 * w
                    n4 = j % 4
                    for n, src in enumerate((bt[n4], kt[n4])):
                        if n == 1:
                            pe.wait_ge(S(f"bonus_done{w}"), pair + 1)
                            pe.wait_ge(S(f"tok_ready{w}"), pair + 1)
                        for c in range(NT):
                            for hh in range(2):
                                q = slice(64 * hh, 64 * hh + 64)
                                i = pe.matmul(ps[:, b0 + 2 * n + hh, c * 2 * P:(c + 1) * 2 * P], src[q, c, :],
                                              ar[n4][q, c].rearrange("p a b -> p (a b)"), start=True, stop=True)
                        i.then_inc(S(f"scores{w}"), 1)
                for w in range(2):
                    b0 = 4 * w
                    pe.wait_ge(S(f"xt_pairs{w}"), pair + 1)
                    for m in range(4):
                        i = pe.transpose(ps[:, b0, m * P:(m + 1) * P], XT[w][:, m, :], ident[:])
                    i.then_inc(S(f"x_turned{w}"), 1)
                for n in range(6):
                    for w in range(2):
                        b0 = 4 * w
                        pe.wait_ge(S(f"x_level{w}"), pair * 12 + max(2 * n, 1))
                        for m in range(4):
                            c, hh = m // 2, m % 2
                            i = pe.matmul(ps[:, b0 + 1, m * P:(m + 1) * P], bar[w][:, hh, c, 0, :], X[w][:, m, :],
                                          start=True, stop=True)
                        i.then_inc(S(f"lx{w}"), 1)
                    for w in range(2):
                        b0 = 4 * w
                        pe.wait_ge(S(f"lx_taken{w}"), pair * 6 + n + 1)
                        pe.wait_ge(S(f"x_level{w}"), pair * 12 + 2 * n + 1)
                        if n < 5:
                            for m in range(4):
                                i = pe.matmul(ps[:, b0 + 2, m * P:(m + 1) * P], XT[w][:, m, :], TX[w][:, m, :],
                                              start=True, stop=True)
                            i.then_inc(S(f"xlx{w}"), 1)
                        for m in range(4):
                            i = pe.matmul(ps[:, b0 + 3, m * P:(m + 1) * P], TX[w][:, m, :], XT[w][:, m, :],
                                          start=True, stop=True)
                        i.then_inc(S(f"xlx{w}"), 1)
                for c in range(NT):
                    for w in range(2):
                        n4, b0 = (2 * pair + w) % 4, 4 * w
                        if c == 0:
                            pe.wait_ge(S(f"x_level{w}"), pair * 12 + 12)
                        for hh in range(2):
                            q = slice(64 * hh, 64 * hh + 64)
                            o = ps[:, b0 + hh, 0:HD]
                            i = pe.matmul(o, kar[w][:, hh, c, 0, :], vtok[w][:, c, q], start=True, stop=(c == 0))
                            if c:
                                i = pe.matmul(o, ar[n4][q, c, 0, :], s0T[w][q, :], start=False, stop=True)
                        i.then_inc(S(f"solve_out{w}"), 1)
                    for w in range(2):
                        b0 = 4 * w
                        pe.wait_ge(S(f"solve_in{w}"), pair * 5 + 3 * c + 1)
                        for hh in range(2):
                            i = pe.matmul(ps[:, b0 + 2 + hh, 0:HD], XT[w][:, 2 * c + hh, :], rhs[w][:, hh, c, :],
                                          start=True, stop=True)
                        i.then_inc(S(f"solve_out{w}"), 1)
                    for w in range(2):
                        b0 = 4 * w
                        pe.wait_ge(S(f"solve_in{w}"), pair * 5 + 3 * c + 2)
                        if c == 0:
                            for hh in range(2):
                                q = slice(64 * hh, 64 * hh + 64)
                                pe.matmul(ps[q, b0, 0:HD], ktok[w][:, q], vtok[w][:, 0, q], start=True, stop=False,
                                          skip_group_check=True)
                                i = pe.matmul(ps[q, b0, 0:HD], btk[w][:, q], us[w][:, hh, 0, :], start=False,
                                              stop=True, skip_group_check=True)
                            i.then_inc(S(f"solve_out{w}"), 1)
                    if c == 0:
                        for w in range(2):
                            pe.wait_ge(S(f"solve_in{w}"), pair * 5 + 3)
                for w in range(2):
                    n4, b0 = (2 * pair + w) % 4, 4 * w
                    for c in range(NT):
                        for part in range(2 + c):
                            for hh in range(2):
                                q = slice(64 * hh, 64 * hh + 64)
                                x, y = ((vtok[w][:, c, q], kar[w][:, hh, c, 1, :]),
                                        (us[w][:, hh, c, :], bar[w][:, hh, c, 1, :]),
                                        (s0T[w][q, :], ar[n4][q, c, 1, :]))[part]
                                i = pe.matmul(ps[q, b0, c * P:(c + 1) * P], x, y, start=part == 0,
                                              stop=part == 1 + c, skip_group_check=True)
                    i.then_inc(S(f"solve_out{w}"), 1)
            for w in range(2):
                pe.wait_ge(S(f"solved{w}"), KD // 2 + 1)
            for j in range(KD):
                i = pe.matmul(ps[:, 4 + j // 2, (j % 2) * T:(j % 2 + 1) * T], head_mean[:], mixT[:, KD + j, :],
                              start=True, stop=True)
            i.then_inc(S("head_products"), 1)
            pe.wait_ge(S("wo_ssd_loaded0"), 16)
            project_out(mixT[:, 0:KD // 2], wo_ssd[0], first=True, part=range(0, 2))
            pe.wait_ge(S("heads_squared"), 2)
            per_head_sums(tmp8, KD, 4).then_inc(S("head_products"), 1)
            project_out(mixT[:, 0:KD // 2], wo_ssd[0], part=range(2, 4))
            pe.wait_ge(S("lengths_inverse"), 2)
            per_head_spread(range(KD), 4).then_inc(S("head_products"), 1)
            pe.wait_ge(S("wo_ssd_loaded1"), 16)
            project_out(mixT[:, KD // 2:KD], wo_ssd[1]).then_inc(S("projected_out"), 1)
            for half in range(2):
                q = slice(half * KD // 2, (half + 1) * KD // 2)
                pe.wait_ge(S("mixed"), half + 1)
                pe.wait_ge(S(f"wo_loaded{half}"), 16)
                i = project_out(mixT[:, KD:, :][:, q], wo_rwkv[:, q], last=half == 1)
            i.then_inc(S("projected_out"), 1)

            def gather(part, bank):
                for k in range(4):
                    for t in range(NT):
                        i = pe.matmul(ps[:, bank, k * P:(k + 1) * P],
                                      hf[:, t, :].rearrange("p (f k) -> p k f", k=KD)[:, 4 * part + k, :],
                                      sel[:, t, :], start=(t == 0), stop=(t == NT - 1))
                return i

            def moe(l):
                transposes_before_moe(2 * l + 1)
                for part in range(2):
                    for kk2 in range(2):
                        for q in range(4):
                            i = pe.matmul(ps[32 * q:32 * q + 32, 4, part * T:(part + 1) * T],
                                          router_w[:, l, 2 * q + kk2, GROUPS * part:GROUPS * part + 32],
                                          hfT[:, 2 * q + kk2, :], start=(kk2 == 0), stop=(kk2 == 1),
                                          skip_group_check=True)
                i.then_inc(S("logits"), 1)
                pe.wait_ge(S("logits_copied"), l + 1)
                for part in range(2):
                    for t in range(NT):
                        i = pe.matmul(ps[:, 5, (2 * part + t) * 32:(2 * part + t + 1) * 32],
                                      lgT[:, part, t * P:(t + 1) * P], fold[:], start=True, stop=True)
                i.then_inc(S("logits"), 1)

                def open_accumulators(banks):
                    for b in banks:
                        pe.matmul(ps[:, b, :], zero[:, 0:P], zero, start=True, stop=False, skip_group_check=True)
                open_accumulators((0, 1))
                pe.wait_ge(S("picked"), l + 1)
                pe.matmul(ps[:, 5, 0:EXPERTS], upper_strict[:], both[:, 0, :], start=True, stop=True)
                pe.matmul(ps[:, 5, EXPERTS:2 * EXPERTS], upper_strict[:], both[:, 1, :], start=True, stop=False)
                pe.matmul(ps[:, 5, EXPERTS:2 * EXPERTS], ones[:], both[:, 0, :], start=False, stop=True)
                for t in range(NT):
                    i = pe.matmul(ps[:, 5, 2 * EXPERTS:3 * EXPERTS], ones[:], both[:, t, :], start=(t == 0),
                                  stop=(t == 1))
                i.then_inc(S("ranked"), 1)
                open_accumulators((2, 3))
                pe.wait_ge(S(f"sel_ready_l{l}"), 1)
                for part in range(2):
                    gather(part, 6 + part).then_inc(S(f"gathered_l{l}"), 1)

                def scatter():
                    for t in range(NT):
                        for half in range(2):
                            i = pe.matmul(ps[:, 2 * t + half, :], gT[:, t, :], ys[:, half * BANK:(half + 1) * BANK],
                                          start=False, stop=False, skip_group_check=True)
                    return i

                def item(n, weights, q4, group, last, waiting=False):
                    pe.wait_ge(S(f"xg_ready_l{l}"), group * 2 + 2)
                    for w, copied in ((0, "y0_copied"), (1, "y1_copied")):
                        pe.wait_ge(S(f"{copied}_l{l}"), n + 1)
                        if w and waiting:
                            scatter()
                        place, loaded, count = weights[w]
                        pe.wait_ge(loaded, count)
                        for kk2 in range(2):
                            for q in range(4):
                                i = pe.matmul(ps[32 * q:32 * q + 32, 4 + w, :],
                                              xg[:, 2 * q + kk2, q4 * SLOTS:(q4 + 1) * SLOTS],
                                              w_up[place][:, 2 * q + kk2, :], start=(kk2 == 0), stop=(kk2 == 1),
                                              skip_group_check=True)
                        i.then_inc(S(f"{('gate_out', 'gu_used')[w]}_l{l}"), 1)
                    if last:
                        pe.wait_ge(S(f"sel_ready_l{l}"), group + 2)
                        gather(0, 6).then_inc(S(f"gathered_l{l}"), 1)
                    if not waiting:
                        scatter()
                    if last:
                        gather(1, 7).then_inc(S(f"gathered_l{l}"), 1)
                        pe.wait_ge(S(f"xg_ready_l{l}"), group * 2 + 3)
                    pe.wait_ge(S(f"selg_ready_l{l}"), n + 1)
                    for t in range(NT):
                        i = pe.transpose(ps[:, 6, t * P:(t + 1) * P], selg[:, t, :], ident[:])
                    i.then_inc(S(f"selg_turned_l{l}"), 1)
                    if last:
                        pe.wait_ge(S(f"xg_ready_l{l}"), group * 2 + 4)
                    pe.wait_ge(S(f"gate_copied_l{l}"), n + 1)
                    for w in range(2):
                        if w:
                            pe.wait_ge(S(f"up_copied_l{l}"), n + 1)
                        for k in range(KH):
                            c = (w * KH + k) * SLOTS
                            i = pe.matmul(ps[:, 7, c:c + SLOTS],
                                          gus[:, w, :].rearrange("p (f k) -> p k f", k=KH)[:, k, :], fold[:],
                                          start=True, stop=True)
                    i.then_inc(S(f"folded_l{l}"), 1)
                    pe.wait_ge(S(f"hid_ready_l{l}"), n + 1)
                    place, loaded, count = weights[2]
                    pe.wait_ge(loaded, count)
                    for half in range(2):
                        for q in range(4):
                            i = pe.matmul(ps[32 * q:32 * q + 32, 4 + half, :], hidT[:, q, :],
                                          w_down[place][:, q, half * BANK:(half + 1) * BANK], start=True, stop=True,
                                          skip_group_check=True)
                        i.then_inc(S(f"{('dn_half', 'dn_used')[half]}_l{l}"), 1)

                def eight_items(i, final):
                    for q8 in range(BLOCKS):
                        weights = []
                        for b in range(3 * q8, 3 * q8 + 3):
                            place = order[l][b % BLOCKS]
                            weights.append((place, S(f"block_loaded{place}"),
                                            i * (3 * 16) + 16 * (TURNS * l + b // BLOCKS + 1)))
                        item(i * BLOCKS + q8, weights, q8 % 4, i * 2 + q8 // 4,
                             q8 % 4 == 3 and not (final and q8 == BLOCKS - 1), waiting=final)
                with pe.Fori(0, EXPERTS // BLOCKS - 1) as i:
                    eight_items(i, False)
                eight_items(EXPERTS // BLOCKS - 1, True)
                pe.wait_ge(S("lists_ready"), l + 1)
                extra = pe.value_load(lists[0:1, l, EXTRA_MAX - 1:EXTRA_MAX], min_val=0, max_val=EXTRA_MAX - 1)
                with pe.If(extra > 0):
                    pe.wait_ge(S(f"sel_ready_l{l}"), EXPERTS // 4 + 1)
                    pe.wait_ge(S(f"y0_copied_l{l}"), EXPERTS + 1)
                    for part in range(2):
                        gather(part, 6 + part).then_inc(S(f"gathered_l{l}"), 1)
                    with pe.Fori(0, extra) as o:
                        weights = [(order[l][5 + which], S(f"extra_loaded_l{l}"), o * 48 + 48) for which in range(3)]
                        item(o + EXPERTS, weights, 0, o + EXPERTS // 4, True)
                pe.wait_ge(S(f"y0_copied_l{l}"), EXPERTS + 1)
                pe.wait_ge(S(f"y1_copied_l{l}"), EXPERTS + 1)
                pe.wait_ge(S("items_done"), 2 * l + 2)
                for b in range(4):
                    t, half = b // 2, b % 2
                    i = pe.matmul(ps[:, b, :], gT[:, t, :], ys[:, half * BANK:(half + 1) * BANK], start=False,
                                  stop=True, skip_group_check=True)
                i.then_inc(S("moe_summed"), 1)
            moe(0)

            transposes(2)
            for c in range(ODD_CHUNKS):
                s = c % RING
                if c == ODD_CHUNKS - 1:
                    pe.wait_ge(S("qkv_taken"), 10)
                    per_head_sums(sqs, 10, 6).then_inc(S("head_products"), 1)
                pe.wait_ge(S(f"ring_loaded{s}"), 16 * (c // RING + 1 + (7 if s == 0 else 6)))
                for half in range(2):
                    if c >= RING:
                        pe.wait_ge(S("qkv_taken"), 2 * (c - RING) + half + 1)
                    project(s, half, S("qkv_ready"), ring1, hnT1)
            pe.wait_ge(S("qkv_taken"), 12)
            for j in range(2):
                for t in range(NT):
                    i = pe.transpose(ps[:, 7, (2 * t + j) * P:(2 * t + j + 1) * P], qkv[:, 10 + j, t * P:(t + 1) * P],
                                     ident[:])
            i.then_inc(S("v_out"), 1)
            pe.wait_ge(S("lengths_inverse"), 3)
            per_head_spread((8, 9), 5).then_inc(S("head_products"), 1)
            per_head_spread(range(KD), 1).then_inc(S("head_products"), 1)
            pe.wait_ge(S("qk_normed"), 1)
            for g in range(KV_HEADS):
                i = pe.matmul(ps[:, 6 + g // 2, (g % 2) * T:(g % 2 + 1) * T], (dup_even, dup_odd)[g % 2][:],
                              qkv[:, 8 + g // 2, :], start=True, stop=True)
            i.then_inc(S("k_out"), 1)
            pe.wait_ge(S("att_inputs"), 1)

            def scores(n):
                g, t = n // NT, n % NT
                n_keys = (t + 1) * P
                for hh in range(4):
                    q = slice(64 * (hh % 2), 64 * (hh % 2) + 64)
                    c = (hh // 2) * 2 * P
                    i = pe.matmul(ps[:, 2 * (n % 2) + hh % 2, c:c + n_keys], qkv[q, 2 * g + hh // 2, t * P:(t + 1) * P],
                                  kdup[q, g, 0:n_keys], start=True, stop=True)
                i.then_inc(S("qk_out"), 1)
            scores(0)
            scores(1)
            for n in range(KV_HEADS * NT):
                g, t = n // NT, n % NT
                if n < KV_HEADS * NT - 2:
                    pe.wait_ge(S("shifted"), n + 1)
                    scores(n + 2)
                pe.wait_ge(S("probs"), n + 1)
                for hh in range(4):
                    for kb in range(t + 1):
                        i = pe.transpose(ps[:, 4 + kb, hh * P:(hh + 1) * P], pr[n % 2][:, hh, kb * P:(kb + 1) * P],
                                         ident[:])
                i.then_inc(S("probs_turned"), 1)
                pe.wait_ge(S("pT_ready"), n + 1)
                if n >= 2:
                    pe.wait_ge(S("att_taken"), n - 1)
                v = 64 * (g % 2)
                for hh, kb in ((2 * a + b, kb) for a in range(2) for kb in range(t + 1) for b in range(2)):
                    half = hh % 2
                    i = pe.matmul(ps[64 * half:64 * half + 64, 6 + n % 2, (hh // 2) * P:(hh // 2 + 1) * P],
                                  vtk[:, kb, g // 2, v:v + 64], pT[:, hh, kb, :], start=(kb == 0), stop=(kb == t),
                                  skip_group_check=True)
                i.then_inc(S("att_out"), 1)
            pe.wait_ge(S("att_taken"), KV_HEADS * NT)
            for half in range(2):
                q = slice(half * KD // 2, (half + 1) * KD // 2)
                pe.wait_ge(S(f"wo_loaded{half}"), 32)
                i = project_out(attT[:, q], wo_att[:, q], first=half == 0, last=half == 1)
            i.then_inc(S("projected_out"), 1)
            moe(1)

        @block.scalar
        def _(act):
            def preload(func):
                act.activation(preloaded[:], eps[:, 0:1], func)
                act.drain()

            def norm_squares(n):
                dst = (hn, hf, hn1, hf)[n]
                if n == 0:
                    act.wait_ge(S("x_loaded"), 16)
                    act.wait_ge(S("ident_ready"), 1)
                else:
                    preload(ACT.Sqrt)
                for t in range(NT):
                    if n % 2:
                        act.wait_ge(S("h_mixed"), n - 1 + t + 1)
                    elif n:
                        act.wait_ge(S("moe_added"), n - 2 + t + 1)
                    act.activation(dst[:, t, :], h[:, t, :], ACT.Square, accum_out=ss[:, t:t + 1])
                act.drain()
                act.activation(ss[:], ss[:], ACT.Sqrt, bias=eps[:, 0:1], scale=1.0 / D).then_inc(S("rms_ready"), 1)
            act.sem_inc(S("silu_done"), 4)
            norm_squares(0)
            for t in range(2 * Z_CHUNKS):
                act.wait_ge(S("projected"), t + 1)
                act.activation(zs[:, t, :], ps[:, t, 0:T], ACT.Silu).then_inc(S("z_done"), 1)
            act.wait_ge(S("consts_ready"), 1)
            act.wait_ge(S("dt_abs"), 1)
            act.activation(dtp[:, 6], dtp[:, 6], ACT.Exp, scale=-1.0)
            act.activation(dtp[:, 7, 0, :], a_log[:], ACT.Exp)
            act.drain()
            act.activation(dtp[:, 6], dtp[:, 6], ACT.Ln, bias=ones[:, 0:1]).then_inc(S("dt_log"), 1)
            with act.Fori(0, CONV_DIM // P // 4) as i:
                for s in range(4):
                    act.wait_ge(S("conv_done"), i * 4 + 8 + s + 1)
                    act.activation(xbc[:, bass.ds(i * 4 + s, 1), :].rearrange("p a t -> p (a t)"), cbuf[:, s, :],
                                   ACT.Silu).then_inc(S("silu_done"), 1)
            act.wait_ge(S("acum_taken"), 1)
            act.activation(dtp[:, 4], dtp[:, 4], ACT.Exp).then_inc(S("dst_exp"), 1)
            act.wait_ge(S("conv_done"), 8 + 16 + 2)
            act.activation(u[0:64, 24, :], u[0:64, 24, :], ACT.Tanh)
            act.activation(u[:, 25, :], u[:, 25, :], ACT.Sigmoid)
            act.drain().then_inc(S("lora_ready"), 1)
            act.wait_ge(S("par_ready"), 1)
            for n in range(0, 3 * KD, 2):
                kind, j = n // KD, n % KD
                act.wait_ge(S("lora_out"), n // 2 + 1)
                for half in range(2):
                    src = ps[:, n // 2 % 2, half * T:(half + 1) * T]
                    if kind == 2:
                        i = act.activation(gate[:, j + half, :], src, ACT.Copy)
                    else:
                        dst, col = ((dec, W0), (agate, A0))[kind]
                        i = act.activation(dst[:, j + half, :], src, ACT.Sigmoid,
                                           bias=par[:, 1, col + j + half:col + j + half + 1])
                i.then_inc(S("lora_taken"), 1)
            for g in range(SSD_GROUPS):
                act.wait_ge(S("ssd_diff"), g + 1)
                act.activation(mm.rearrange("p a b c -> p (a b c)"), mm.rearrange("p a b c -> p (a b c)"), ACT.Exp)
                act.activation(cs.rearrange("p a b -> p (a b)"), ps[:, 5, :], ACT.Exp).then_inc(S("ssd_exp"), 1)
                if g == SSD_GROUPS - 1:
                    act.wait_ge(S("head_products"), 1)
                    act.activation(lengths[:], ps[:, 2, 0:T], ACT.Sqrt).then_inc(S("lengths_root"), 1)
                act.wait_ge(S("ssd_var_eps"), g + 1)
                act.activation(sr, sr, ACT.Sqrt).then_inc(S("ssd_root"), 1)
            def decays(pair):
                for w in range(2):
                    n4 = (2 * pair + w) % 4
                    act.wait_ge(S(f"cum_ready{w}"), pair + 1)
                    for c in range(NT):
                        act.activation(e1[w][:, c, :], cum[w][:, c, :], ACT.Exp, scale=-DECAY_FACTOR,
                                       bias=edge[n4][:, c:c + 1])
                        act.activation(e2[w][:, c, :], cum[w][:, c, 1:], ACT.Exp, scale=DECAY_FACTOR,
                                       bias=edge[n4][:, 2 + c:3 + c])
                    act.activation(edge[n4][:, 5:6], edge[n4][:, 4:5], ACT.Exp).then_inc(S(f"decay_exp{w}"), 1)
            preload(ACT.Exp)
            decays(0)
            for pair in range(KD // 2):
                for w in range(2):
                    act.wait_ge(S(f"tok_turned{w}"), 2 * pair + 2)
                    act.activation(vtok[w].rearrange("p a b -> p (a b)"), ps[:, 4 * w + 2, 0:2 * P], ACT.Copy)
                    act.activation(ktok[w], ps[:, 4 * w + 2, 2 * P:3 * P], ACT.Copy)
                    act.activation(btk[w], ps[:, 4 * w + 2, 3 * P:4 * P], ACT.Copy).then_inc(S(f"tok_ready{w}"), 1)
                for n in range(6):
                    for w in range(2):
                        act.wait_ge(S(f"lx{w}"), pair * 6 + n + 1)
                        act.activation(TX[w].rearrange("p m (b r t) -> p m b r t", r=2, t=2 << n)[:, :, :, 0, :],
                                       ps[:, 4 * w + 1, :].rearrange("p (m b r t) -> p m b r t", m=4, r=2,
                                                                     t=2 << n)[:, :, :, 0],
                                       ACT.Copy).then_inc(S(f"lx_taken{w}"), 1)
                    if n == 2 and pair < KD // 2 - 1:
                        decays(pair + 1)

            preload(ACT.Sqrt)
            act.wait_ge(S("gn_centred"), 1)
            act.activation(tmp8.rearrange("p a t -> p (a t)"), mixT[:, KD:, :].rearrange("p a t -> p (a t)"),
                           ACT.Square).then_inc(S("heads_squared"), 1)
            act.wait_ge(S("head_products"), 4)
            act.activation(lengths[:], ps[:, 4, 0:T], ACT.Sqrt, bias=eps[:, 1:2],
                           scale=1.0 / HD).then_inc(S("lengths_root"), 1)

            def moe(l):
                norm_squares(2 * l + 1)
                preload(ACT.Exp)
                act.wait_ge(S("coarse_shifted"), l + 1)
                for t in range(NT):
                    act.activation(c8[:, t, 0:GROUPS], c8[:, t, 0:GROUPS], ACT.Exp, accum_out=sc[:, 0, t:t + 1])
                act.activation(sc[:, 1, :], sc[:, 1, :], ACT.Exp).then_inc(S("gates_exp"), 1)

                act.sem_inc(S(f"y0_copied_l{l}"), 1)

                def item(n):
                    act.wait_ge(S(f"gate_out_l{l}"), n + 1)
                    act.activation(gus[:, 0, :], ps[:, 4, :], ACT.Copy).then_inc(S(f"gate_copied_l{l}"), 1)
                    act.wait_ge(S(f"selg_turned_l{l}"), n + 1)
                    act.activation(gT.rearrange("p a b -> p (a b)"), ps[:, 6, 0:T], ACT.Copy)
                    act.wait_ge(S(f"folded_l{l}"), n + 1)
                    act.activation(sil.rearrange("p a b -> p (a b)"), ps[:, 7, 0:P],
                                   ACT.Silu).then_inc(S(f"silu_l{l}"), 1)
                    act.wait_ge(S(f"dn_half_l{l}"), n + 1)
                    act.activation(ys[:, 0:BANK], ps[:, 4, :], ACT.Copy).then_inc(S(f"y0_copied_l{l}"), 1)
                with act.Fori(0, EXPERTS // 4) as i:
                    for q4 in range(4):
                        item(i * 4 + q4)
                act.wait_ge(S("lists_ready"), l + 1)
                extra = act.value_load(lists[0:1, l, EXTRA_MAX - 1:EXTRA_MAX], min_val=0, max_val=EXTRA_MAX - 1)
                with act.If(extra > 0):
                    with act.Fori(0, extra) as o:
                        item(o + EXPERTS)
                act.drain().then_inc(S("items_done"), 1)
            moe(0)

            norm_squares(2)
            for j in range(12):
                act.wait_ge(S("qkv_ready"), j + 1)
                act.activation(qkv[:, j, :], ps[:, j % 8, 0:T], ACT.Copy)
                if j < 10:
                    act.activation(sqs[:, j, :], ps[:, j % 8, 0:T], ACT.Square)
                act.drain().then_inc(S("qkv_taken"), 1)
                if j == 10:
                    preload(ACT.Sqrt)
                    act.wait_ge(S("head_products"), 6)
                    act.activation(lengths[:], ps[:, 6, 0:T], ACT.Sqrt, bias=eps[:, 0:1],
                                   scale=1.0 / HD).then_inc(S("lengths_root"), 1)

            def exponentials(n):
                n_keys = (n % NT + 1) * P
                p_, s_ = pr[n % 2], st[n % 2]
                act.wait_ge(S("shifted"), n + 1)
                for hh in range(4):
                    act.activation(p_[:, hh, 0:n_keys], p_[:, hh, 0:n_keys], ACT.Exp, bias=s_[:, 1, hh:hh + 1],
                                   accum_out=s_[:, 2, hh:hh + 1])
                act.activation(s_[:, 3, :], s_[:, 3, :], ACT.Exp).then_inc(S("exped"), 1)
            preload(ACT.Exp)
            exponentials(0)
            for n in range(KV_HEADS * NT):
                if n < KV_HEADS * NT - 1:
                    exponentials(n + 1)
                act.wait_ge(S("probs_turned"), n + 1)
                for kb in range(n % NT + 1):
                    i = act.activation(pT[:, :, kb, :], ps[:, 4 + kb, :].rearrange("p (a b) -> p a b", b=P), ACT.Copy)
                i.then_inc(S("pT_ready"), 1)
            moe(1)

        @block.vector
        def _(dve):
            tt, tsc, stt, cp = dve.tensor_tensor, dve.tensor_scalar, dve.scalar_tensor_tensor, dve.tensor_copy

            def over_rms(n, dst):
                dve.wait_ge(S("rms_ready"), n + 1)
                dve.reciprocal(rstd[:], ss[:])
                dve.drain()
                for t in range(NT):
                    i = tsc(dst[:, t, :], h[:, t, :], rstd[:, t:t + 1], None, ALU.mult)
                i.then_inc(S("hn_ready"), 1)

            def times_gain(n, dstT, bank):
                for b in range(4):
                    dve.wait_ge(S("hn_turned"), 4 * n + b + 1)
                    i = tt(dstT[:, 2 * b:2 * b + 2, :], ps[:, bank + b, :].rearrange("p (k t) -> p k t", t=T),
                           bc(gains[:, n, 2 * b:2 * b + 2].unsqueeze(2), 2, T), ALU.mult)
                i.then_inc(S("hnT_ready"), 1)

            dve.wait_ge(S("gains_loaded"), 64)
            over_rms(0, hn)
            times_gain(0, hnT, 0)
            dve.tensor_reduce(fold[:], ident[:].rearrange("p (q j) -> p j q", q=4), AX.X, ALU.add)
            dve.wait_ge(S("consts_ready"), 1)
            dve.wait_ge(S("par_turned"), 1)
            cp(par[:, 0, 0:114], ps[:, 7, 0:114])
            cp(par[:, 1, 0:56], ps[:, 7, P:P + 56])
            dve.drain()
            tsc(par[:, 1, 64:64 + RWKV_TILES], par[:, 0, MU:MU + RWKV_TILES], -1.0, 1.0, ALU.mult, ALU.add)
            dve.drain().then_inc(S("par_ready"), 1)
            dve.wait_ge(S("dt_ready"), 1)
            tt(dtp[:, 0], ps[:, 6, 0:NT * SSD_HEADS].rearrange("p (c h) -> p c h", c=NT),
               bc(dt_bias[:].unsqueeze(1), NT, SSD_HEADS), ALU.add)
            dve.drain()
            tsc(dtp[:, 6], dtp[:, 0], -1.0, None, ALU.mult)
            dve.drain()
            tt(dtp[:, 6], dtp[:, 0], dtp[:, 6], ALU.max).then_inc(S("dt_abs"), 1)
            dve.sem_inc(S("conv_done"), 8)

            with dve.Fori(0, CONV_CHUNKS // RING) as i:
                for b in range(TILES_PER_RING):
                    dve.wait_ge(S("projected"), i * TILES_PER_RING + 2 * Z_CHUNKS + b + 1)
                    dve.wait_ge(S("silu_done"), i * TILES_PER_RING + b + 1)
                    tile = i * TILES_PER_RING + b
                    buf = cbuf[:, b % 4, :]
                    tsc(buf, ps[:, b, 0:T], par[:, 0, bass.ds(tile + CW + 48, 1)], par[:, 0, bass.ds(tile + CB, 1)],
                        ALU.mult, ALU.add)
                    for s in range(1, CONV_TAPS):
                        dve.drain()
                        ins = stt(buf[:, s:], ps[:, b, 0:T - s], par[:, 0, bass.ds(tile + CW + 16 * (3 - s), 1)],
                                  buf[:, s:], ALU.mult, ALU.add)
                    ins.then_inc(S("conv_done"), 1)

            dve.wait_ge(S("dt_log"), 1)
            tsc(dtp[:, 0], dtp[:, 0], 0.0, None, ALU.max)
            dve.drain()
            tt(dtp[:, 0], dtp[:, 0], dtp[:, 6], ALU.add)
            dve.drain()
            stt(dtp[:, 1], dtp[:, 0], -1.0, bc(dtp[:, 7, 0:1, :], NT, SSD_HEADS), ALU.mult,
                ALU.mult).then_inc(S("adt_ready"), 1)

            def token_shift(n, count=1):
                for n in range(n, n + count):
                    tile = (n - 2) % RWKV_TILES
                    dve.wait_ge(S("projected"), 2 * (Z_CHUNKS + CONV_CHUNKS) + n + 1)
                    tsc(u[:, tile, :], ps[:, n % 2, 0:T], par[:, 1, 64 + tile:65 + tile], None, ALU.mult)
                    dve.drain()
                    stt(u[:, tile, 1:], ps[:, n % 2, 0:T - 1], par[:, 0, MU + tile:MU + tile + 1], u[:, tile, 1:],
                        ALU.mult, ALU.add).then_inc(S("conv_done"), 1)
            token_shift(0, 2)
            dve.wait_ge(S("acum_ready"), 1)
            cp(dtp[:, 2], ps[:, 7, 0:NT * SSD_HEADS].rearrange("p (c h) -> p c h", c=NT))
            dve.drain()
            tt(dtp[:, 4], ps[:, 7, NT * SSD_HEADS:2 * NT * SSD_HEADS].rearrange("p (c h) -> p c h", c=NT), dtp[:, 2],
               ALU.subtract).then_inc(S("acum_taken"), 1)

            def per_head(row, c, g):
                return dtp[:, row, c, g * HPG:(g + 1) * HPG]

            def ssd_triangles(g):
                for c in range(NT):
                    i = tt(tria[:, c], bc(upper[:].unsqueeze(1), HPG, P), bc(per_head(1, c, g).unsqueeze(2), HPG, P),
                           ALU.mult)
                i.then_inc(S("ssd_tria"), 1)

            def ssd_scale(g):
                dve.wait_ge(S("ssd_turned"), g + 1)
                for c in range(NT):
                    tt(xdt[:, c], ps[:, 2, c * 2 * P:(c + 1) * 2 * P].rearrange("p (h d) -> p h d", d=HD),
                       bc(per_head(0, c, g).unsqueeze(2), HPG, HD), ALU.mult)
                cp(btok, ps[:, 3, 0:P])
                tt(cbm, ps[:, 3, P:3 * P].rearrange("p (c t) -> p c t", c=NT), bc(upper[:].unsqueeze(1), NT, P),
                   ALU.mult)
                dve.drain()
                tt(xst, xdt[:, 0], bc(per_head(4, 0, g).unsqueeze(2), HPG, HD), ALU.mult).then_inc(S("ssd_scaled"), 1)

            def ssd_differences(g):
                dve.wait_ge(S("ssd_cumulated"), g + 1)
                for c in range(NT):
                    tt(mm[:, c], ps[:, 4 + c, :].rearrange("p (h t) -> p h t", t=P),
                       bc(per_head(2, c, g).unsqueeze(2), HPG, P), ALU.subtract)
                dve.drain()
                tsc(mm, mm, 0.0, None, ALU.min).then_inc(S("ssd_diff"), 1)

            def times_spread(x, tiles, bank):
                for j in range(0, tiles, 2):
                    i = tt(x[:, j:j + 2, :], x[:, j:j + 2, :],
                           ps[:, bank + j // 2, :].rearrange("p (a t) -> p a t", a=2), ALU.mult)
                return i

            def prepare(j, step):
                w, n4 = j % 2, j % 4
                e = edge[n4]
                if step == 0:
                    tsc(kp[w], agate[:, j, :], -1.0, par[:, 1, KA + j:KA + j + 1], ALU.add, ALU.mult)
                    for c in range(NT):
                        dve.tensor_tensor_scan(cum[w][:, c, 1:], ones[:], dec[:, j, c * P:(c + 1) * P], 0.0, ALU.mult,
                                               ALU.add)
                elif step == 1:
                    stt(kp[w], kp[w], 1.0, kv_[:, j, :], ALU.add, ALU.mult)
                    for c in range(NT):
                        tsc(e[:, c:c + 1], cum[w][:, c, HD:HD + 1], DECAY_FACTOR, None, ALU.mult)
                        tsc(e[:, 2 + c:3 + c], cum[w][:, c, HD:HD + 1], -DECAY_FACTOR, None, ALU.mult)
                    tt(e[:, 4:5], cum[w][:, 0, HD:HD + 1], cum[w][:, 0, P:P + 1], ALU.subtract)
                    dve.drain()
                    stt(e[:, 4:5], cum[w][:, 1, HD:HD + 1], -1.0, e[:, 4:5], ALU.mult, ALU.add)
                    dve.drain()
                    tsc(e[:, 4:5], e[:, 4:5], DECAY_FACTOR, None, ALU.mult).then_inc(S(f"cum_ready{w}"), 1)
                elif step == 2:
                    stt(tmp[w], rv[:, j, :], par[:, 1, RK + j:RK + j + 1], kp[w], ALU.mult, ALU.mult)
                elif step == 3:
                    dve.wait_ge(S(f"decay_exp{w}"), j // 2 + 1)
                    stt(ar[n4][:, :, 0, :], kk[:, j, :].rearrange("p (c t) -> p c t", c=NT), -1.0, e1[w][:, :, 0:P],
                        ALU.mult, ALU.mult)
                    tt(ar[n4][:, :, 1, :], rv[:, j, :].rearrange("p (c t) -> p c t", c=NT), e1[w][:, :, 1:], ALU.mult)
                elif step == 4:
                    tt(kt[n4].rearrange("p c t -> p (c t)"), kp[w], e2[w].rearrange("p c t -> p (c t)"), ALU.mult)
                    tt(bt[n4].rearrange("p c t -> p (c t)"), agate[:, j, :], e2[w].rearrange("p c t -> p (c t)"),
                       ALU.mult)
                else:
                    tt(bt[n4].rearrange("p c t -> p (c t)"), bt[n4].rearrange("p c t -> p (c t)"), kk[:, j, :],
                       ALU.mult).then_inc(S(f"decayed{w}"), 1)

            dve.wait_ge(S("silu_done"), 4 + CONV_DIM // P)
            ssd_triangles(0)
            dve.wait_ge(S("dst_exp"), 1)
            ssd_scale(0)
            ssd_differences(0)
            for g in range(SSD_GROUPS):
                last = g == SSD_GROUPS - 1
                if not last:
                    ssd_triangles(g + 1)
                token_shift(2 + 6 * g, 2)
                dve.wait_ge(S("ssd_state"), g + 1)
                cp(state.rearrange("p a b -> p (a b)"), ps[:, 3, 0:HPG * HD])
                dve.wait_ge(S("ssd_exp"), g + 1)
                for c in range(NT):
                    tt(mm[:, c], mm[:, c], bc(cbm[:, c:c + 1, :], HPG, P), ALU.mult)
                tt(cs, cs, bc(xbc[:, 12 + g:13 + g, P:], HPG, P), ALU.mult)
                dve.drain().then_inc(S("ssd_weighted"), 1)
                token_shift(4 + 6 * g)
                dve.wait_ge(S("ssd_out"), g + 1)
                for t in range(2):
                    stt(sy[:, t, :], xbc[:, 2 * g + t, :], d_skip[:, 2 * g + t:2 * g + t + 1],
                        ps[:, 6, t * T:(t + 1) * T], ALU.mult, ALU.add)
                dve.drain()
                tt(sy, sy, zs[:, 2 * g:2 * g + 2, :], ALU.mult)
                dve.drain()
                tt(ssq, sy, sy, ALU.mult).then_inc(S("ssd_squared"), 1)
                token_shift(5 + 6 * g)
                if last:
                    dve.wait_ge(S("lengths_root"), 1)
                    tsc(lengths[:], lengths[:], 1e-12, None, ALU.max)
                    dve.drain()
                    dve.reciprocal(lengths[:], lengths[:]).then_inc(S("lengths_inverse"), 1)
                dve.wait_ge(S("ssd_mean"), g + 1)
                tsc(sr, ps[:, 7, 0:T], 1e-5, None, ALU.add).then_inc(S("ssd_var_eps"), 1)
                token_shift(6 + 6 * g)
                dve.wait_ge(S("ssd_root"), g + 1)
                dve.reciprocal(sr, sr)
                dve.drain()
                for t in range(2):
                    stt(mixT[:, 2 * g + t, :], sy[:, t, :], par[:, 0, NW_ + 2 * g + t:NW_ + 2 * g + t + 1], sr,
                        ALU.mult, ALU.mult)
                if not last:
                    ssd_scale(g + 1)
                else:
                    for w in range(2):
                        dve.memset(cum[w][:, :, 0:1], 0.0)
                    for step in range(3):
                        for w in range(2):
                            prepare(w, step)
                        dve.drain()
                    dve.wait_ge(S("head_products"), 2)
                    for b in range(KD // 2):
                        tt(kk[:, 2 * b:2 * b + 2, :], kraw[:, 2 * b:2 * b + 2, :],
                           ps[:, 2 + b, :].rearrange("p (a t) -> p a t", a=2), ALU.mult)
                    dve.drain().then_inc(S("kk_ready"), 1)
                token_shift(7 + 6 * g)
                if not last:
                    ssd_differences(g + 1)
                if g == SSD_GROUPS - 2:
                    for j in range(KD):
                        tsc(kraw[:, j, :], kv_[:, j, :], par[:, 1, KK + j:KK + j + 1], None, ALU.mult)
                    dve.drain()
                    tt(ksq, kraw, kraw, ALU.mult).then_inc(S("heads_squared"), 1)
            dve.drain()
            for step in range(3, 6):
                for w in range(2):
                    prepare(w, step)
                dve.drain()

            def residual(used, n, done):
                dve.wait_ge(used, n)
                for t in range(NT):
                    tt(h[:, t, :].rearrange("p (a b) -> p a b", a=2), h[:, t, :].rearrange("p (a b) -> p a b", a=2),
                       ps[:, 2 * t:2 * t + 2, :], ALU.add).then_inc(done, 1)

            for w in range(2):
                dve.sem_inc(S(f"solved{w}"), 1)
            for pair in range(KD // 2):
                for w in range(2):
                    j, b0 = 2 * pair + w, 4 * w
                    dve.wait_ge(S(f"tok_turned{w}"), 2 * pair + 1)
                    tt(bonus[:, j, :], ps[:, b0 + 3, 0:T], vv[:, j, :], ALU.mult).then_inc(S(f"bonus_done{w}"), 1)
                for w in range(2):
                    b0 = 4 * w
                    dve.wait_ge(S(f"scores{w}"), 2 * pair + 1)
                    dve.wait_ge(S(f"x_reset{w}"), pair + 1)
                    for hh in range(2):
                        dve.copy_predicated(bar[w][:, hh], bc(mask_ar[:].bitcast(I32).unsqueeze(1), NT, 2, P),
                                            ps[:, b0 + hh, :].rearrange("p (c a t) -> p c a t", c=NT, a=2))
                    dve.drain()
                    for hh in range(2):
                        i = dve.copy_predicated(XT[w].rearrange("p (c h) t -> p h c t", h=2)[:, hh],
                                                bc(mask_pair[:].bitcast(I32).unsqueeze(1), NT, P),
                                                bar[w][:, hh, :, 0, :])
                    i.then_inc(S(f"xt_pairs{w}"), 1)
                    dve.wait_ge(S(f"scores{w}"), 2 * pair + 2)
                    for hh in range(2):
                        dve.copy_predicated(kar[w][:, hh], bc(mask_ar[:].bitcast(I32).unsqueeze(1), NT, 2, P),
                                            ps[:, b0 + 2 + hh, :].rearrange("p (c a t) -> p c a t", c=NT, a=2))
                for w in range(2):
                    dve.wait_ge(S(f"x_turned{w}"), pair + 1)
                    cp(X[w].rearrange("p a b -> p (a b)"), ps[:, 4 * w, :]).then_inc(S(f"x_level{w}"), 1)
                for n in range(6):
                    for w in range(2):
                        for side, (dst, mask) in enumerate(((X[w], mask_level), (XT[w], mask_level_t))):
                            if n == 5 and side == 0:
                                continue
                            dve.wait_ge(S(f"xlx{w}"), pair * 11 + min(2 * n + 1 + side, 11))
                            blocks = P // (4 << n)
                            dve.copy_predicated(
                                dst.rearrange("p m (b r t) -> p m b r t", r=2, t=2 << n)[:, :, :, side, :],
                                bc(half_blocks(mask[:, n, :], n, side).bitcast(I32).unsqueeze(1), 4, blocks, 2 << n),
                                ps[:, 4 * w + 2 + side, :].rearrange("p (m b r t) -> p m b r t", m=4, r=2,
                                                                     t=2 << n)[:, :, :, side]
                                ).then_inc(S(f"x_level{w}"), 1)
                    if pair < KD // 2 - 1:
                        for w in range(2):
                            prepare(2 * pair + 2 + w, n)
                        dve.drain()
                for c in range(NT):
                    for w in range(2):
                        dve.wait_ge(S(f"solve_out{w}"), pair * 6 + 3 * c + 1)
                        cp(rhs[w][:, :, c, :], ps[:, 4 * w:4 * w + 2, 0:HD]).then_inc(S(f"solve_in{w}"), 1)
                    for w in range(2):
                        dve.wait_ge(S(f"solve_out{w}"), pair * 6 + 3 * c + 2)
                        cp(us[w][:, :, c, :], ps[:, 4 * w + 2:4 * w + 4, 0:HD]).then_inc(S(f"solve_in{w}"), 1)
                    if c == 0:
                        for w in range(2):
                            dve.wait_ge(S(f"solve_out{w}"), pair * 6 + 3)
                            tsc(s0T[w], ps[:, 4 * w, 0:HD], edge[(2 * pair + w) % 4][:, 5:6], None,
                                ALU.mult).then_inc(S(f"solve_in{w}"), 1)
                for w in range(2):
                    dve.wait_ge(S(f"solve_out{w}"), pair * 6 + 6)
                    cp(mixT[:, KD + 2 * pair + w, :], ps[:, 4 * w, 0:T]).then_inc(S(f"solved{w}"), 1)
            dve.drain()

            my = mixT[:, KD:, :]
            dve.wait_ge(S("head_products"), 3)
            for b in range(4):
                v = my[:, 2 * b:2 * b + 2, :]
                tt(v, v, ps[:, 4 + b, :].rearrange("p (a t) -> p a t", a=2), ALU.subtract)
            dve.drain().then_inc(S("gn_centred"), 1)
            dve.wait_ge(S("lengths_root"), 2)
            dve.reciprocal(lengths[:], lengths[:]).then_inc(S("lengths_inverse"), 1)
            dve.wait_ge(S("head_products"), 5)
            times_spread(my, KD, 4)
            dve.drain()
            for half in range(2):
                q = slice(half * KD // 2, (half + 1) * KD // 2)
                for j in range(half * KD // 2, (half + 1) * KD // 2):
                    tsc(my[:, j, :], my[:, j, :], par[:, 1, LNW + j:LNW + j + 1], par[:, 1, LNB + j:LNB + j + 1],
                        ALU.mult, ALU.add)
                dve.drain()
                tt(my[:, q], my[:, q], bonus[:, q], ALU.add)
                dve.drain()
                tt(my[:, q], my[:, q], gate[:, q], ALU.mult).then_inc(S("mixed"), 1)

            residual(S("projected_out"), 2, S("h_mixed"))

            def moe(l):
                dve.drain()
                dve.memset(c8, -1.0e30)
                dve.memset(ys, 0.0)
                dve.memset(gT, 0.0)
                dve.memset(zero, 0.0)
                times_gain(2 * l + 1, hfT, 4)
                over_rms(2 * l + 1, hf)
                dve.wait_ge(S("logits"), 2 * l + 1)
                cp(lgT.rearrange("p a b -> p (a b)"), ps[:, 4, :]).then_inc(S("logits_copied"), 1)
                dve.wait_ge(S("logits"), 2 * l + 2)
                for part, (lo, hi) in enumerate(((0, GROUPS), (GROUPS, GROUPS + EXPERTS))):
                    for t in range(NT):
                        c = 32 * (NT * part + t)
                        stt(lg[:, t, lo:hi], ps[:, 5, c:c + hi - lo], rstd[:, t:t + 1], router_b[:, l, lo:hi],
                            ALU.mult, ALU.add)
                dve.drain()
                cp(c8[:, :, 0:GROUPS], lg[:, :, 0:GROUPS])
                dve.drain()
                for t in range(NT):
                    dve.max(mx[:, t, :], c8[:, t, :])
                dve.drain()
                for t in range(NT):
                    dve.max_index(idx[:, 0, t, :], mx[:, t, :], c8[:, t, :])
                dve.drain()
                cp(sc[:, 2, :], idx[:, 0, :, 0])
                tt(c8[:, :, 0:GROUPS], c8[:, :, 0:GROUPS], bc(mx[:, :, 0:1], NT, GROUPS), ALU.subtract)
                dve.drain()
                for t in range(NT):
                    stt(fine[:, t], bc(iota128[:, 0:GROUPS].unsqueeze(1), PER_GROUP, GROUPS), sc[:, 2, t:t + 1],
                        lg[:, t, GROUPS:].rearrange("p (g e) -> p e g", g=GROUPS), ALU.is_equal, ALU.mult)
                dve.drain()
                dve.tensor_reduce(fsel, fine, AX.X, ALU.add)
                dve.drain()
                for t in range(NT):
                    dve.max(fmx[:, t, :], fsel[:, t, :])
                dve.drain()
                for t in range(NT):
                    dve.max_index(idx[:, 1, t, :], fmx[:, t, :], fsel[:, t, :])
                tt(sc[:, 1, :], fmx[:, :, 1], fmx[:, :, 0], ALU.subtract)
                dve.drain().then_inc(S("coarse_shifted"), 1)
                cp(sc[:, 4, :], idx[:, 1, :, 0])
                cp(sc[:, 5, :], idx[:, 1, :, 1])
                dve.drain()
                for r in (4, 5):
                    stt(sc[:, r, :], sc[:, 2, :], float(PER_GROUP), sc[:, r, :], ALU.mult, ALU.add)
                dve.drain()
                for r in range(2):
                    for t in range(NT):
                        tsc(pick[:, 2 * r + t, :], iota128[:, 0:EXPERTS], sc[:, 4 + r, t:t + 1], None, ALU.is_equal)
                dve.drain()
                tt(both, pick[:, 0:2, :], pick[:, 2:4, :], ALU.add).then_inc(S("picked"), 1)
                dve.wait_ge(S("ranked"), l + 1)
                cp(rank, ps[:, 5, 0:2 * EXPERTS].rearrange("p (t e) -> p t e", t=NT))
                cp(cnt[:, 0, :], ps[:, 5, 2 * EXPERTS:3 * EXPERTS])
                dve.drain()
                tt(above[:, 0:EXPERTS], bc(cnt[:, 0, :].unsqueeze(2), EXPERTS, EXTRA_BLOCKS),
                   bc(steps[:].unsqueeze(1), EXPERTS, EXTRA_BLOCKS), ALU.is_gt)
                dve.drain()
                dve.tensor_reduce(cnt[:, 1, :], above[:, 0:EXPERTS], AX.X, ALU.add)
                dve.drain()
                dve.tensor_tensor_scan(cnt[:, 2, :], ones[:, 0:EXPERTS], cnt[:, 1, :], 0.0, ALU.mult, ALU.add)
                dve.drain()
                tt(cnt[:, 3, :], cnt[:, 2, :], cnt[:, 1, :], ALU.subtract)
                tt(prod.rearrange("p (r t) e -> p r t e", r=2), pick.rearrange("p (r t) e -> p r t e", r=2),
                   bc(rank.unsqueeze(1), 2, NT, EXPERTS), ALU.mult)
                dve.drain()
                dve.tensor_reduce(slot[:, 0, :], prod, AX.X, ALU.add)
                dve.drain()
                tt(prod, pick, bc(cnt[:, 3:4, :], 4, EXPERTS), ALU.mult)
                tt(above[:, 0:4], bc(slot[:, 0, :].unsqueeze(2), 4, EXTRA_BLOCKS),
                   bc(steps[:].unsqueeze(1), 4, EXTRA_BLOCKS), ALU.is_ge)
                dve.drain()
                dve.tensor_reduce(slot[:, 1, :], prod, AX.X, ALU.add)
                dve.tensor_reduce(slot[:, 2, :], above[:, 0:4], AX.X, ALU.add)
                dve.drain()
                cp(slot[:, 3, :].rearrange("p (r t) -> p r t", r=2), sc[:, 4:6, :])
                tsc(slot[:, 4, :], slot[:, 2, :], 1.0, None, ALU.min)
                stt(slot[:, 5, :], slot[:, 1, :], float(EXPERTS - 1), slot[:, 2, :], ALU.add, ALU.add)
                stt(slot[:, 6, :], slot[:, 2, :], -float(SLOTS), slot[:, 0, :], ALU.mult, ALU.add)
                dve.drain()
                tt(slot[:, 5, :], slot[:, 5, :], slot[:, 3, :], ALU.subtract)
                dve.drain()
                tt(slot[:, 5, :], slot[:, 5, :], slot[:, 4, :], ALU.mult)
                dve.drain()
                tt(slot[:, 5, :], slot[:, 5, :], slot[:, 3, :], ALU.add)
                dve.drain()
                stt(slot[:, 7, :], slot[:, 5, :], float(SLOTS), slot[:, 6, :], ALU.mult, ALU.add)
                dve.drain()

                def select():
                    for t in range(NT):
                        tsc(sel[:, t, :], iota128[:], slot[:, 7, t:t + 1], None, ALU.is_equal)
                    dve.drain()
                    for t in range(NT):
                        i = stt(sel[:, t, :], iota128[:], slot[:, 7, 2 + t:3 + t], sel[:, t, :], ALU.is_equal, ALU.add)
                    i.then_inc(S(f"sel_ready_l{l}"), 1)

                def weigh(shift):
                    for t in range(NT):
                        tsc(selw[:, t, :], iota128[:], slot[:, 7, t:t + 1], sc[:, 7, t:t + 1], ALU.is_equal, ALU.mult)
                        tsc(selt[:, t, :], iota128[:], slot[:, 7, 2 + t:3 + t], sc[:, 8, t:t + 1], ALU.is_equal,
                            ALU.mult)
                    dve.drain()
                    tt(selw, selw, selt, ALU.add)
                    tsc(slot[:, 7, :], slot[:, 7, :], -float(shift), None, ALU.add)
                    dve.drain()

                def take_gathered(n, part):
                    dve.wait_ge(S(f"gathered_l{l}"), n * 2 + part + 1)
                    q = slice(4 * part, 4 * part + 4)
                    tt(xg[:, q, :], ps[:, 6 + part, :].rearrange("p (k s) -> p k s", k=4),
                       bc(gains[:, 2 * l + 1, q].unsqueeze(2), 4, P), ALU.mult).then_inc(S(f"xg_ready_l{l}"), 1)
                dve.sem_inc(S(f"y1_copied_l{l}"), 1)
                select()
                dve.wait_ge(S("gates_exp"), l + 1)
                tsc(sc[:, 6, :], sc[:, 1, :], 1.0, None, ALU.add)
                dve.drain()
                tt(sc[:, 6, :], sc[:, 6, :], sc[:, 0, :], ALU.mult)
                dve.drain()
                dve.reciprocal(sc[:, 7, :], sc[:, 6, :])
                dve.drain()
                tt(sc[:, 8, :], sc[:, 7, :], sc[:, 1, :], ALU.mult)
                for part in range(2):
                    take_gathered(0, part)
                tt(lst[0:1], bc(cnt[0:1, 2:3, :], EXTRA_MAX, EXPERTS),
                   bc(iota128[0:1, 0:EXTRA_MAX].unsqueeze(2), EXTRA_MAX, EXPERTS), ALU.is_le)
                dve.drain()
                dve.tensor_reduce(lsti[0:1, 0, :], lst[0:1], AX.X, ALU.add)
                dve.drain()
                cp(lsti[0:1, 0, EXTRA_MAX - 1:EXTRA_MAX], cnt[0:1, 2, EXPERTS - 1:EXPERTS])
                dve.drain()
                cp(lists[0:1, l, :], lsti[0:1, 0, :])
                dve.drain().then_inc(S("lists_ready"), 1)

                def item(n, q4, group, first, second, last, shift):
                    dve.wait_ge(S(f"gu_used_l{l}"), n + 1)
                    cp(gus[:, 1, :], ps[:, 5, :]).then_inc(S(f"up_copied_l{l}"), 1)
                    if first:
                        weigh(shift)
                    cp(selg.rearrange("p t (r s) -> p t r s", r=4),
                       bc(selw[:, :, q4 * SLOTS:(q4 + 1) * SLOTS].unsqueeze(2), NT, 4, SLOTS)
                       ).then_inc(S(f"selg_ready_l{l}"), 1)
                    if second:
                        select()
                    if last:
                        for part in range(2):
                            take_gathered(group + 1, part)
                    dve.wait_ge(S(f"silu_l{l}"), n + 1)
                    tt(hidT.rearrange("p a b -> p (a b)"), sil.rearrange("p a b -> p (a b)"), ps[:, 7, P:2 * P],
                       ALU.mult).then_inc(S(f"hid_ready_l{l}"), 1)
                    dve.wait_ge(S(f"dn_used_l{l}"), n + 1)
                    cp(ys[:, BANK:], ps[:, 5, :]).then_inc(S(f"y1_copied_l{l}"), 1)
                with dve.Fori(0, EXPERTS // 4 - 1) as i:
                    for q4 in range(4):
                        item(i * 4 + q4, q4, i, q4 == 0, q4 == 1, q4 == 3, P)
                for q4 in range(4):
                    item(EXPERTS - 4 + q4, q4, EXPERTS // 4 - 1, q4 == 0, False, False, P)
                extra = dve.value_load(lists[0:1, l, EXTRA_MAX - 1:EXTRA_MAX], min_val=0, max_val=EXTRA_MAX - 1)
                with dve.If(extra > 0):
                    select()
                    for part in range(2):
                        take_gathered(EXPERTS // 4, part)
                    with dve.Fori(0, extra) as o:
                        item(o + EXPERTS, 0, o + EXPERTS // 4, True, True, True, SLOTS)
                dve.drain().then_inc(S("items_done"), 1)
                residual(S("moe_summed"), l + 1, S("moe_added"))
            moe(0)

            over_rms(2, hn1)
            times_gain(2, hnT1, 0)
            dve.wait_ge(S("qkv_taken"), 10)
            for n, (lo, hi, scale) in enumerate(((0, 8, HD ** -0.5), (8, 10, 1.0))):
                tsc(qkv[:, lo:hi, :], qkv[:, lo:hi, :], qk_gain[:, n:n + 1], scale, ALU.mult, ALU.mult)
            dve.wait_ge(S("lengths_root"), 3)
            dve.reciprocal(lengths[:], lengths[:]).then_inc(S("lengths_inverse"), 1)
            dve.wait_ge(S("v_out"), 1)
            cp(vtk.rearrange("p t a b -> p (t a b)"), ps[:, 7, :])
            dve.drain()
            dve.wait_ge(S("head_products"), 7)
            times_spread(qkv[:, 8:10, :], 2, 5).then_inc(S("qk_normed"), 1)
            dve.wait_ge(S("head_products"), 8)
            times_spread(qkv[:, 0:KD, :], KD, 1)
            dve.wait_ge(S("k_out"), 1)
            for b in range(2):
                cp(kdup[:, 2 * b:2 * b + 2, :].rearrange("p a t -> p (a t)"), ps[:, 6 + b, :])
            dve.drain().then_inc(S("att_inputs"), 1)

            def shifted_scores(n):
                g, n_keys = n // NT, (n % NT + 1) * P
                p_, s_ = pr[n % 2], st[n % 2]
                dve.wait_ge(S("qk_out"), n + 1)
                for hh in range(4):
                    c = (hh // 2) * 2 * P
                    stt(p_[:, hh, 0:n_keys], band[:, 2 * P - n_keys:], 2.0 ** (-8.0 * (4 * g + hh + 1) / ATT_HEADS),
                        ps[:, 2 * (n % 2) + hh % 2, c:c + n_keys], ALU.mult, ALU.add)
                dve.drain()
                dve.tensor_reduce(s_[:, 0, :], p_[:, :, 0:n_keys], AX.X, ALU.max)
                dve.drain()
                tt(s_[:, 0, :], s_[:, 0, :], sinks[:, 4 * g:4 * g + 4], ALU.max)
                dve.drain()
                tsc(s_[:, 1, :], s_[:, 0, :], -1.0, None, ALU.mult)
                tt(s_[:, 3, :], sinks[:, 4 * g:4 * g + 4], s_[:, 0, :], ALU.subtract)
                dve.drain().then_inc(S("shifted"), 1)
            def take_attended(n):
                g, t = n // NT, n % NT
                dve.wait_ge(S("att_out"), n + 1)
                cp(attT[:, 2 * g:2 * g + 2, t * P:(t + 1) * P],
                   ps[:, 6 + n % 2, 0:2 * P].rearrange("p (a b) -> p a b", a=2)).then_inc(S("att_taken"), 1)
            shifted_scores(0)
            for n in range(KV_HEADS * NT):
                n_keys = (n % NT + 1) * P
                p_, s_ = pr[n % 2], st[n % 2]
                if n < KV_HEADS * NT - 1:
                    if n >= 1:
                        dve.wait_ge(S("probs_turned"), n)
                    shifted_scores(n + 1)
                dve.wait_ge(S("exped"), n + 1)
                tt(s_[:, 2, :], s_[:, 2, :], s_[:, 3, :], ALU.add)
                dve.drain()
                dve.reciprocal(s_[:, 2, :], s_[:, 2, :])
                dve.drain()
                tt(p_[:, :, 0:n_keys], p_[:, :, 0:n_keys], bc(s_[:, 2, :].unsqueeze(2), 4, n_keys),
                   ALU.mult).then_inc(S("probs"), 1)
                if n:
                    take_attended(n - 1)
            take_attended(KV_HEADS * NT - 1)
            residual(S("projected_out"), 3, S("h_mixed"))
            moe(1)


PARAM_LOADS = 38


def kernel(**inputs):
    import numpy as np
    import concourse.bacc as bacc
    from concourse.bass_utils import run_bass_kernel_spmd

    nc = bacc.Bacc("TRN2", target_bir_lowering=False, num_devices=1)
    arrays, args = {}, {}
    for name, value in inputs.items():
        array = np.ascontiguousarray(value)
        arrays[f"in_{name}"] = array
        args[name] = nc.dram_tensor(f"in_{name}", array.shape, mybir.dt.from_np(array.dtype), kind="ExternalInput").ap()
    out = nc.dram_tensor("out_h", inputs["x"].shape, F32, kind="ExternalOutput").ap()
    trunk(nc, args, out)
    result = run_bass_kernel_spmd(nc, [arrays], core_ids=[0])
    return result.results[0]["out_h"]
```
